# Optimizing a Trainium2 kernel written in Bass

```python
import jax, jax.numpy as jnp
from jax import lax
import numpy as np

D_MODEL = 1024
BATCH = 1
SEQ = 1024
DEPTH = 1

CHUNK = 64
Q_BLOCK = 128
MIX_WIDTH = D_MODEL
MLA_HEADS = 4
QK_NOPE_DIM = 128
QK_ROPE_DIM = 64
V_HEAD_DIM = 128
Q_LORA_RANK = 256
KV_LORA_RANK = 128
MLA_WIDTH = MLA_HEADS * V_HEAD_DIM
POOL_WIDTH = MIX_WIDTH - MLA_WIDTH
POOL_WINDOWS = (2, 4, 8, 16)
POOL_GROUPS = len(POOL_WINDOWS)
POOL_GROUP_DIM = POOL_WIDTH // POOL_GROUPS
IN_COLS = Q_LORA_RANK + KV_LORA_RANK + QK_ROPE_DIM + POOL_WIDTH
D_FF = ((8 * D_MODEL + 3 * 256 - 1) // (3 * 256)) * 256
ROPE_THETA = 10000.0
EPS = 1e-6
SM_SCALE = (QK_NOPE_DIM + QK_ROPE_DIM) ** -0.5
N_MOD = 6

kernel_name = "hybrid_mla_pool_adaln_block"

def rmsnorm(x, g):
    xf = x.astype(jnp.float32)
    y = xf * lax.rsqrt(jnp.mean(xf * xf, axis=-1, keepdims=True) + EPS)
    return (y * g.astype(jnp.float32)).astype(x.dtype)

def rope_tables(positions, dtype):
    half = QK_ROPE_DIM // 2
    freqs = jnp.power(ROPE_THETA, -jnp.arange(half, dtype=jnp.float32) / half)
    ang = positions.astype(jnp.float32)[..., None] * freqs
    return jnp.cos(ang).astype(dtype), jnp.sin(ang).astype(dtype)

def apply_rope(x, cos, sin):
    x1, x2 = jnp.split(x, 2, axis=-1)
    return jnp.concatenate([x1 * cos - x2 * sin, x1 * sin + x2 * cos], axis=-1)

def mla_mixer(cq_raw, ckv_raw, kr_raw, positions, g_q, g_kv, w_uq, w_uk, w_uv):
    B, S, _ = ckv_raw.shape
    c_q = rmsnorm(cq_raw, g_q)
    c_kv = rmsnorm(ckv_raw, g_kv)
    q = jnp.einsum('bsr,rhd->bshd', c_q, w_uq)
    q_nope, q_rope = q[..., :QK_NOPE_DIM], q[..., QK_NOPE_DIM:]
    cos, sin = rope_tables(positions, q.dtype)
    q_rope = apply_rope(q_rope, cos[:, :, None, :], sin[:, :, None, :])
    k_rope = apply_rope(kr_raw, cos, sin)
    q_lat = jnp.einsum('bshd,chd->bshc', q_nope, w_uk)
    nblk = S // Q_BLOCK
    q_lat_b = q_lat.reshape(B, nblk, Q_BLOCK, MLA_HEADS, KV_LORA_RANK).transpose(1, 0, 2, 3, 4)
    q_rope_b = q_rope.reshape(B, nblk, Q_BLOCK, MLA_HEADS, QK_ROPE_DIM).transpose(1, 0, 2, 3, 4)
    key_chunk = jnp.arange(S) // CHUNK

    def block(args):
        ql, qr, blk = args
        s = (jnp.einsum('bqhc,bkc->bhqk', ql, c_kv)
             + jnp.einsum('bqhr,bkr->bhqk', qr, k_rope)).astype(jnp.float32) * SM_SCALE
        q_chunk = (blk * Q_BLOCK + jnp.arange(Q_BLOCK)) // CHUNK
        mask = key_chunk[None, :] <= q_chunk[:, None]
        s = jnp.where(mask[None, None], s, -jnp.inf)
        p = jax.nn.softmax(s, axis=-1).astype(c_kv.dtype)
        o_lat = jnp.einsum('bhqk,bkc->bqhc', p, c_kv)
        o = jnp.einsum('bqhc,chv->bqhv', o_lat, w_uv)
        return o.reshape(B, Q_BLOCK, MLA_WIDTH)

    out = lax.map(block, (q_lat_b, q_rope_b, jnp.arange(nblk)))
    return out.transpose(1, 0, 2, 3).reshape(B, S, MLA_WIDTH)

def pool_mixer(u, w_pool, pool_scale):
    B, S, _ = u.shape
    ug = u.reshape(B, S, POOL_GROUPS, POOL_GROUP_DIM)
    cs = jnp.cumsum(ug.astype(jnp.float32), axis=1)
    t = jnp.arange(1, S + 1, dtype=jnp.float32)
    pooled = []
    for g, w in enumerate(POOL_WINDOWS):
        csg = cs[:, :, g]
        lagged = jnp.pad(csg, ((0, 0), (w, 0), (0, 0)))[:, :S]
        count = jnp.minimum(t, float(w))[None, :, None]
        pooled.append((csg - lagged) / count)
    pooled = jnp.stack(pooled, axis=2).astype(u.dtype) - ug
    y = jnp.einsum('bsgc,gcd->bsgd', pooled, w_pool).reshape(B, S, POOL_WIDTH)
    return y * pool_scale

def setup_inputs(seed: int = 0) -> dict:
    key = jax.random.key(seed)
    ks = jax.random.split(key, 24)
    f32 = jnp.float32
    nrm = lambda k, shape, s: jax.random.normal(k, shape, f32) * s
    gain = lambda k, shape: 1.0 + 0.05 * jax.random.normal(k, shape, f32)
    x = jax.random.normal(ks[0], (BATCH, SEQ, D_MODEL), f32)
    c = jax.random.normal(ks[1], (BATCH, D_MODEL), f32)
    offset = jax.random.randint(ks[2], (BATCH, 1), 0, 8192, dtype=jnp.int32)
    positions = offset + jnp.arange(SEQ, dtype=jnp.int32)[None, :]
    return {
        "x": x,
        "c": c,
        "positions": positions,
        "w_ada": nrm(ks[3], (DEPTH, D_MODEL, N_MOD * D_MODEL), 0.5 * D_MODEL ** -0.5),
        "b_ada": nrm(ks[4], (DEPTH, N_MOD * D_MODEL), 0.02),
        "g_mix": gain(ks[5], (DEPTH, D_MODEL)),
        "w_in": nrm(ks[6], (DEPTH, D_MODEL, IN_COLS), D_MODEL ** -0.5),
        "g_q": gain(ks[7], (DEPTH, Q_LORA_RANK)),
        "g_kv": gain(ks[8], (DEPTH, KV_LORA_RANK)),
        "w_uq": nrm(ks[9], (DEPTH, Q_LORA_RANK, MLA_HEADS, QK_NOPE_DIM + QK_ROPE_DIM), Q_LORA_RANK ** -0.5),
        "w_uk": nrm(ks[10], (DEPTH, KV_LORA_RANK, MLA_HEADS, QK_NOPE_DIM), KV_LORA_RANK ** -0.5),
        "w_uv": nrm(ks[11], (DEPTH, KV_LORA_RANK, MLA_HEADS, V_HEAD_DIM), KV_LORA_RANK ** -0.5),
        "w_pool": nrm(ks[12], (DEPTH, POOL_GROUPS, POOL_GROUP_DIM, POOL_GROUP_DIM), POOL_GROUP_DIM ** -0.5),
        "pool_scale": gain(ks[13], (DEPTH, POOL_WIDTH)),
        "w_o": nrm(ks[14], (DEPTH, MIX_WIDTH, D_MODEL), MIX_WIDTH ** -0.5),
        "g_ffn": gain(ks[15], (DEPTH, D_MODEL)),
        "w_gate": nrm(ks[16], (DEPTH, D_MODEL, D_FF), D_MODEL ** -0.5),
        "w_up": nrm(ks[17], (DEPTH, D_MODEL, D_FF), D_MODEL ** -0.5),
        "w_down": nrm(ks[18], (DEPTH, D_FF, D_MODEL), D_FF ** -0.5),
        "g_final": gain(ks[19], (D_MODEL,)),
    }

def reference(x, c, positions, w_ada, b_ada, g_mix, w_in, g_q, g_kv, w_uq, w_uk,
              w_uv, w_pool, pool_scale, w_o, g_ffn, w_gate, w_up, w_down, g_final):
    c_act = jax.nn.silu(c)
    for l in range(DEPTH):
        mod = (c_act @ w_ada[l] + b_ada[l])[:, None, :]
        sh1, sc1, gt1, sh2, sc2, gt2 = jnp.split(mod, N_MOD, axis=-1)

        h = rmsnorm(x, g_mix[l]) * (1.0 + sc1) + sh1
        proj = h @ w_in[l]
        o1 = Q_LORA_RANK
        o2 = o1 + KV_LORA_RANK
        o3 = o2 + QK_ROPE_DIM
        y_mla = mla_mixer(proj[..., :o1], proj[..., o1:o2], proj[..., o2:o3], positions,
                          g_q[l], g_kv[l], w_uq[l], w_uk[l], w_uv[l])
        y_pool = pool_mixer(proj[..., o3:], w_pool[l], pool_scale[l])
        mix = jnp.concatenate([y_mla, y_pool], axis=-1) @ w_o[l]
        x = x + gt1 * mix

        h = rmsnorm(x, g_ffn[l]) * (1.0 + sc2) + sh2
        ff = (jax.nn.silu(h @ w_gate[l]) * (h @ w_up[l])) @ w_down[l]
        x = x + gt2 * ff
    return rmsnorm(x, g_final)


_drawn_inputs = setup_inputs


def setup_inputs(seed=0):
    import zlib

    import numpy as np

    out = dict(_drawn_inputs(seed))
    spreads = {}
    factors = {'g_mix': 5.294,
     'g_q': 8.0,
     'g_kv': 8.0,
     'w_uk': 2.846,
     'pool_scale': 5.703,
     'g_ffn': 3.862}
    for name, (base, spread) in spreads.items():
        noise = np.random.default_rng([zlib.crc32(name.encode()), seed]).standard_normal(out[name].shape)
        drawn = base * np.exp(spread * noise) if base else spread * noise
        out[name] = __import__('jax').numpy.asarray(drawn.astype(out[name].dtype))
    for name, factor in factors.items():
        out[name] = (out[name] * factor).astype(out[name].dtype)
    return out
```

```python
from contextlib import ExitStack

import numpy as np

import concourse.bass as bass
from concourse import mybir

ALU = mybir.AluOpType
ACT = mybir.ActivationFunctionType
AX = mybir.AxisListType
F32 = mybir.dt.float32
F32R = mybir.dt.float32r
BF16 = mybir.dt.bfloat16
I32 = mybir.dt.int32

P = 128
SEQ = 1024
D = 1024
KT = D // P
NT = SEQ // P
HALF = 512
HEADS = 4
NOPE = 128
ROPE = 64
RH = ROPE // 2
QR = 256
LAT = 128
VD = 128
TM = QR + LAT + ROPE
TMW = TM + ROPE
CHUNK = 64
GROUPS = 4
PADW = 16
DFF = 2816
FT = DFF // P
NC = FT // 2
EPS = 1e-6
SCALE = float((NOPE + ROPE) ** -0.5)
MASKED = -float(2.0 ** 100)
HI, LO = 0, 1
PASSES = ((HI, LO), (HI, HI), (LO, HI))
RSQRT_MAGIC = float(0x5F3759DF)
ROUND_MAGIC = float(3 * 2 ** 22)
N_ROWS = 48 + 8 + 8 + 4
ROW_MIX, ROW_FFN, ROW_POOL = 48, 56, 64
KB = 1024


def two_pi_parts():
    rest, parts = 2 * np.pi, []
    for _ in range(4):
        e = int(np.floor(np.log2(rest))) - 6
        part = float(np.floor(rest / 2.0 ** e) * 2.0 ** e)
        parts.append(part)
        rest -= part
    return parts + [float(np.float32(rest))]


def hybrid_block(nc, x, c, positions, w_ada, b_ada, g_mix, w_in, g_q, g_kv, w_uq, w_uk, w_uv,
                 w_pool, pool_scale, w_o, g_ffn, w_gate, w_up, w_down, g_final, freqs, out):
    ctx = ExitStack()
    enter = ctx.enter_context
    base = 16512
    nc.alloc_sbuf_tensor("arena", [P, (229344 - base) // 4], F32)

    def at(name, kb, shape, dt=F32):
        return nc.alloc_sbuf_tensor_at(name, shape, dt, offset=base + int(kb * KB))

    def sem(name):
        return enter(nc.semaphore(name))

    X = at("X", 0, [P, NT, D])
    PT = at("PT", 0, [P, 2, NT, HEADS, P], F32R)
    U = at("U", 0, [P, GROUPS, PADW + SEQ])
    UR = at("UR", 0, [P, GROUPS, PADW + SEQ], F32R)
    WIN = at("WIN", 16.25, [P, 2, PADW + SEQ])
    ropeK = at("ropeK", 16.25, [P, 4, NT, RH])
    ropeQ = at("ropeQ", 16.25, [P, 4, HEADS, RH])
    QRD = at("QRD", 18.25, [P, 2, HEADS, 2, ROPE])
    WP = at("WP", 24.5, [P, 2, GROUPS, P], F32R)
    WPraw = at("WPraw", 26.5, [P, GROUPS, P])
    HT = at("HT", 32, [P, 2, KT, SEQ], F32R)
    HTf = at("HTf", 64, [P, KT, SEQ])
    ADA0 = at("ADA0", 32, [P, 4, 4, HALF])
    QRAW = at("QRAW", 32, [P, NT, HEADS, ROPE])
    QN = at("QN", 40, [P, 2, 2, HALF], F32R)
    POOLHI = at("POOLHI", 64, [P, GROUPS, SEQ], F32R)
    QS = at("QS", 64, [P, HEADS, SEQ], F32R)
    WTM = at("WTM", 96, [P, 2, KT, TM], F32R)
    WTMraw = at("WTMraw", 110, [P, KT, TM])
    LT = at("LT", 96, [P, 3, 2, SEQ], F32R)
    PR = at("PR", 96, [P, HEADS, SEQ])
    WUV = at("WUV", 120, [P, 2, HEADS, VD], F32R)
    WUVraw = at("WUVraw", 122, [P, HEADS, VD])
    WU = at("WU", 124, [P, 2, 2, KT, P], F32R)
    WUraw = at("WUraw", 124, [P, 2, 2, KT, P])
    ADA6 = at("ADA6", 124, [P, 2, 4, HALF])
    QLhi = at("QLhi", 124, [P, HEADS, SEQ], F32R)
    QLlo = at("QLlo", 156, [P, HEADS, SEQ], F32R)
    ADA4 = at("ADA4", 140, [P, 2, 4, HALF])
    WUQ = at("WUQ", 140, [P, 2, 2, HEADS, NOPE + ROPE], F32R)
    WUQraw = at("WUQraw", 146, [P, 2, HEADS, NOPE + ROPE])
    WUK = at("WUK", 152, [P, 2, HEADS, LAT], F32R)
    WUKraw = at("WUKraw", 152, [P, HEADS, NOPE])
    TMO = at("TMO", 156, [P, NT, TMW])
    JUNK = at("JUNK", 156, [P, SEQ])
    ACC = at("ACC", 172, [P, 2, HALF])
    OL = at("OL", 172, [P, 2, HALF], F32R)
    CKV = at("CKV", 176, [P, 2, NT, LAT], F32R)
    KRT = at("KRT", 184, [P, 2, SEQ], F32R)
    COS = at("COS", 192, [P, NT, RH])
    SIN = at("SIN", 193, [P, NT, RH])
    GQ = at("GQ", 194, [P, QR])
    GKV = at("GKV", 195, [P, LAT])
    ROWS = at("ROWS", 195.5, [P, P])
    ANG = at("ANG", 160, [P, NT, RH])
    TURN = at("TURN", 161, [P, NT, RH])
    SHALF = at("SHALF", 162, [P, NT, RH])
    SQUART = at("SQUART", 163, [P, NT, RH])
    FREQ = at("FREQ", 164, [P, RH])
    WOlo = [at("WOlo0", 140, [P, KT, HALF], F32R), at("WOlo1", 112, [P, KT, HALF], F32R)]
    WOraw = [at("WOraw0", 140, [P, KT, HALF]), at("WOraw1", 112, [P, KT, HALF])]
    WOhi = [at("WOhi0", 156, [P, KT, HALF], F32R), at("WOhi1", 96, [P, KT, HALF], F32R)]
    MIX = at("MIX", 176, [P, 2, HALF])
    JUNK2 = at("JUNK2", 180, [P, SEQ])
    XN = at("XN", 184, [P, 2, D])
    ACTS = at("ACTS", 96, [P, 4, 2, SEQ], F32R)
    WGU = at("WGU", 128, [P, 2, 2, 2, KT, P], F32R)
    WGUraw = at("WGUraw", 128, [P, 2, 2, 2, KT, P])
    WD = at("WD", 160, [P, 2, 2, D], F32R)
    WDraw = at("WDraw", 168, [P, 2, D])
    HID = at("HID", 176, [P, 2, HALF])
    IDENT = at("IDENT", 196, [P, P])
    ONES = at("ONES", 196.5, [P, P])
    MASKQ = at("MASKQ", 197, [P, P], BF16)
    MASKK = at("MASKK", 197.25, [P, P], BF16)
    o = 197.5

    def small(name, n, dt=F32):
        nonlocal o
        t = at(name, o, [P, n], dt)
        o += (4 * n + 31) // 32 * 32 / KB
        return t

    COLS = small("COLS", N_ROWS)
    MOD = small("MOD", 32)
    G1 = small("G1", KT)
    G2 = small("G2", KT)
    CT = small("CT", KT)
    CS = small("CS", KT)
    POSI = small("POSI", NT, I32)
    POSF = small("POSF", NT)
    INV = small("INV", 16)
    SS = small("SS", 16)
    VAR = small("VAR", 16)
    RS = small("RS", 16)
    RT = small("RT", 16)
    RI = small("RI", 16, I32)
    NEGM = small("NEGM", 32)
    SUM = small("SUM", 32)
    RSUM = small("RSUM", 32)
    SS2 = small("SS2", NT)
    RS2 = small("RS2", NT)
    SS3 = small("SS3", NT)
    RS3 = small("RS3", NT)
    assert o <= 199.8
    GT1 = at("GT1", 199.8125, [P, D])
    GT2 = at("GT2", 203.8125, [P, D])

    PS = enter(nc.psum_tensor("PS", [P, 8, HALF], F32))

    names = """c_in rows_in pos_in freq_in gq_in gkv_in gt_in wp_in wuv_in wuq_in wuk_in gfin_in out_done
        pool_const  act_silu ang_ready sin_ready dve_step pool_step
        ss1 rs1 xn1 t1 ev1 acc_done colsum modcols gt_ready rowsT
        hmod h_hi h_ready wtm_hi wtm_ready tm_done tm_out tm_norm kr_ready ckv_hi ckv_ready
        wu_hi wu_ready u_done u_out pooled lt_T lt_hi lt_lo pool_hi pool_lo wp_hi wp_ready pm_done pm_y pm_hi pm_lo
        wuq_hi wuq_ready wukT wuk_hi wuk_ready wuv_hi wuv_ready
        qr_done qr_raw qr_rot qr_T qr_hi qr_lo qn_done qn_hi qn_lo ql_done ql_hi ql_lo
        s_done negmax exp_done rsum p_norm p_T pt_hi pt_lo pv_done ol_hi ol_lo op_done y_hi y_lo
        wo_hi wo_hi_odd wo_ready mix_done mix_gated x_new ss2 rs2 xn2 t2 ev2 h2_hi h2_ready
        wgu_hi wgu_ready wd_fold wd_hi wd_ready gu_half silu hid act_hi act_ready
        d_bank d_free ss3 rs3 fin""".split()
    S = {n: sem(n) for n in names}
    x_in = [sem(f"x_in{t}") for t in range(NT)]
    ada_in = [sem(f"ada_in{i}") for i in range(8)]
    wtm_in = [sem(f"wtm_in{i}") for i in range(4)]
    wu_in = [sem(f"wu_in{i}") for i in range(2)]
    wo_in = [sem(f"wo_in{i}") for i in range(4)]
    wgu_in = [sem(f"wgu_in{i}") for i in range(2)]
    wd_in = sem("wd_in")

    x_d = x.rearrange("b (t p) d -> (b t) p d", p=P)
    out_d = out.rearrange("b (t p) d -> (b t) p d", p=P)
    ada_d = w_ada.rearrange("l (p t) n -> p (l t) n", t=KT)
    win_d = w_in.rearrange("l (k p) n -> p (l k) n", p=P)
    gate_d = w_gate.rearrange("l (k p) n -> p (l k) n", p=P)
    up_d = w_up.rearrange("l (k p) n -> p (l k) n", p=P)
    down_d = w_down.rearrange("l (f p) n -> p (l f) n", p=P)
    wo_d = w_o.rearrange("l (k p) n -> p (l k) n", p=P)
    wuq_d = w_uq.rearrange("l (k p) h d -> p (l k) h d", p=P)

    N_PIECES = 24

    def ada_buf(q):
        if q < 4:
            return ADA0[:, q]
        if q in (4, 5):
            return ADA4[:, q - 4]
        if q in (6, 7):
            return ADA6[:, q - 6]
        return ADA4[:, q % 2]

    def ada_sem(q):
        if q < 8:
            return ada_in[q], 16
        return ada_in[4 + q % 2], 16 * ((q - 8) // 2 + 2)

    def flat(ap):
        return ap.rearrange("p a b -> p (a b)")

    def tok(t):
        return slice(t * P, (t + 1) * P)

    def half(i):
        return slice(i * HALF, (i + 1) * HALF)

    BLOCKS = list(range(NT - 1, -1, -1))
    GORDER = list(range(GROUPS - 1, -1, -1))


    block = enter(nc.Block())

    @block.sync
    def _(sp):
        def load_ada(q):
            s, _ = ada_sem(q)
            col = (q // 2) * HALF
            sp.dma_start(ada_buf(q), ada_d[:, 4 * (q % 2):4 * (q % 2) + 4, col:col + HALF]).then_inc(s, 16)

        sp.dma_start(CT[:], c.rearrange("b (p t) -> p (b t)", t=KT)).then_inc(S["c_in"], 16)
        sp.dma_start(POSI[:], positions.rearrange("b (t p) -> p (b t)", p=P), allow_slow_non_contiguous=True).then_inc(S["pos_in"], 16)
        sp.dma_start(FREQ[:], freqs.partition_broadcast(P)).then_inc(S["freq_in"], 16)
        load_ada(0)
        for t in range(4):
            sp.dma_start(X[:, t, :], x_d[t]).then_inc(x_in[t], 16)
        load_ada(1)
        for t in range(4, NT):
            sp.dma_start(X[:, t, :], x_d[t]).then_inc(x_in[t], 16)
        for src, r, n in ((b_ada, 0, 48), (g_mix, ROW_MIX, 8), (g_ffn, ROW_FFN, 8), (pool_scale, ROW_POOL, 4)):
            sp.dma_start(ROWS[r:r + n, :], src.rearrange("l (r n) -> (l r) n", n=P)).then_inc(S["rows_in"], 16)
        for q in range(2, 8):
            load_ada(q)
        for i in range(4):
            sp.dma_start(WTMraw[:, 2 * i:2 * i + 2, :], win_d[:, 2 * i:2 * i + 2, 0:TM]).then_inc(wtm_in[i], 16)
        sp.dma_start(GQ[:], g_q.rearrange("l n -> (l n)").partition_broadcast(P)).then_inc(S["gq_in"], 16)
        sp.dma_start(GKV[:], g_kv.rearrange("l n -> (l n)").partition_broadcast(P)).then_inc(S["gkv_in"], 16)
        sp.dma_start(GT1[:], b_ada[0, 2 * D:3 * D].partition_broadcast(P)).then_inc(S["gt_in"], 16)
        sp.dma_start(GT2[:], b_ada[0, 5 * D:6 * D].partition_broadcast(P)).then_inc(S["gt_in"], 16)

        def load_wu(i):
            g = GORDER[i]
            sp.dma_start(WUraw[:, i % 2, LO], win_d[:, :, TM + g * P:TM + (g + 1) * P]).then_inc(wu_in[i % 2], 16)

        def ring_ada(q):
            sp.wait_ge(S["acc_done"], (q - 1) if q >= 10 else q - 3)
            load_ada(q)

        for q in range(8, 10):
            ring_ada(q)
        sp.wait_ge(S["acc_done"], 8)
        load_wu(0)
        load_wu(1)
        sp.wait_ge(S["t1"], NT)
        sp.dma_start(WPraw[:], w_pool.rearrange("l g c d -> c (l g) d")).then_inc(S["wp_in"], 16)
        for q in range(10, N_PIECES):
            ring_ada(q)
        sp.wait_ge(S["tm_done"], NT)
        sp.dma_start(WUVraw[:], w_uv.rearrange("l c h v -> c (l h) v")).then_inc(S["wuv_in"], 16)
        sp.wait_ge(S["u_done"], 2)
        load_wu(2)
        sp.wait_ge(S["acc_done"], N_PIECES)
        sp.dma_start(WUQraw[:], wuq_d).then_inc(S["wuq_in"], 16)
        sp.dma_start(WUKraw[:], w_uk.rearrange("l c h d -> c (l h) d")).then_inc(S["wuk_in"], 16)
        sp.wait_ge(S["u_done"], 4)
        load_wu(3)
        sp.wait_ge(S["ql_done"], 8)
        for i in range(4):
            sp.dma_start(WOraw[0][:, 2 * i:2 * i + 2, :], wo_d[:, 2 * i:2 * i + 2, half(0)]).then_inc(wo_in[i], 16)
        sp.wait_ge(S["pv_done"], NT)
        for t in range(NT):
            sp.dma_start(X[:, t, :], x_d[t]).then_inc(x_in[t], 16)
            if t == 2:
                sp.wait_ge(S["op_done"], NT)
                sp.wait_ge(S["wo_ready"], KT)
                for i in range(4):
                    sp.dma_start(WOraw[1][:, 2 * i:2 * i + 2, :],
                                 wo_d[:, 2 * i:2 * i + 2, half(1)]).then_inc(wo_in[i], 16)

        def load_wgu(f, s):
            sp.dma_start(WGUraw[:, s, LO, 0], gate_d[:, :, bass.ds(f * P, P)]).then_inc(wgu_in[s], 16)
            sp.dma_start(WGUraw[:, s, LO, 1], up_d[:, :, bass.ds(f * P, P)]).then_inc(wgu_in[s], 16)

        def load_wd(i):
            sp.dma_start(WDraw[:], down_d[:, bass.ds(2 * i, 2), :]).then_inc(wd_in, 16)

        sp.wait_ge(S["mix_done"], NT)
        load_wgu(0, 0)
        load_wgu(1, 1)
        load_wd(0)
        sp.wait_ge(S["x_new"], 2 * NT)
        sp.dma_start(GT1[:], g_final.partition_broadcast(P)).then_inc(S["gfin_in"], 16)

        def chunk_loads(i, more=True):
            if more:
                for s in range(2):
                    sp.wait_ge(S["gu_half"], 4 * i + 2 * s + 2)
                    load_wgu(2 * i + 2 + s, s)
            if not isinstance(i, int) or i > 0:
                sp.wait_ge(S["d_bank"], 16 * i)
                load_wd(i)

        chunk_loads(0)
        with sp.Fori(0, (NC - 3) // 2) as j:
            for par in (1, 0):
                chunk_loads(2 * j + (1 if par else 2))
        chunk_loads(NC - 2)
        chunk_loads(NC - 1, more=False)
        for t in range(NT):
            sp.wait_ge(S["fin"], t + 1)
            sp.dma_start(out_d[t], X[:, t, :]).then_inc(S["out_done"], 16)
        sp.wait_ge(S["out_done"], 16 * NT)

    @block.gpsimd
    def _(pool):
        n = 0

        def then(ins):
            nonlocal n
            n += 1
            ins.then_inc(S["pool_step"], 1)
            pool.wait_ge(S["pool_step"], n)

        then(pool.memset(IDENT[:], 0.0))
        then(pool.affine_select(out=IDENT[:], in_=IDENT[:], compare_op=ALU.not_equal, fill=1.0, base=0,
                                pattern=[[-1, P]], channel_multiplier=1))
        then(pool.memset(MASKQ[:], 0.0))
        then(pool.memset(MASKK[:], 0.0))
        then(pool.memset(MASKQ[0:1, 0:CHUNK], 1.0))
        then(pool.memset(MASKK[0:1, CHUNK:P], MASKED))
        for t in range(PADW):
            pool.memset(INV[:, t:t + 1], 1.0 / (t + 1))
        pool.memset(ONES[:], 1.0).then_inc(S["pool_const"], 1)

        for t in range(NT):
            pool.wait_ge(S["rs1"], t // 4 + 1)
            pool.tensor_scalar(X[:, t, :], X[:, t, :], RS[:, t:t + 1], None, ALU.mult).then_inc(S["xn1"], 1)

        for i in range(4):
            pool.wait_ge(wtm_in[i], 16)
            pool.tensor_scalar(flat(WTM[:, HI, 2 * i:2 * i + 2, :]), flat(WTMraw[:, 2 * i:2 * i + 2, :]),
                               1.0, None, ALU.mult).then_inc(S["wtm_hi"], 1)
        for m in range(2 * KT):
            hf, k = divmod(m, KT)
            pool.wait_ge(S["hmod"], m + 1)
            pool.tensor_scalar(HT[:, HI, k, half(hf)], HTf[:, k, half(hf)], 1.0, None, ALU.mult).then_inc(S["h_hi"], 1)

        def wu_hi(g):
            pool.wait_ge(wu_in[g % 2], 16 * (g // 2 + 1))
            pool.tensor_scalar(flat(WU[:, g % 2, HI]), flat(WUraw[:, g % 2, LO]), 1.0, None, ALU.mult).then_inc(S["wu_hi"], 1)

        wu_hi(0)
        wu_hi(1)
        pool.wait_ge(S["t1"], NT)
        pool.memset(U[:, :, 0:PADW], 0.0)
        pool.wait_ge(S["tm_norm"], NT)
        pool.tensor_scalar(CKV[:, HI], TMO[:, :, QR:QR + LAT], 1.0, None, ALU.mult).then_inc(S["ckv_hi"], 1)
        k1, k2 = TMO[:, :, QR + LAT:QR + LAT + RH], TMO[:, :, QR + LAT + RH:TM]
        pool.tensor_tensor(ropeK[:, 0], k1, COS[:], ALU.mult)
        pool.tensor_tensor(ropeK[:, 1], k2, SIN[:], ALU.mult)
        pool.tensor_tensor(ropeK[:, 2], k1, SIN[:], ALU.mult)
        then(pool.tensor_tensor(ropeK[:, 3], k2, COS[:], ALU.mult))
        for d in range(2):
            o_ = QR + LAT + d * ROPE
            pool.tensor_tensor(TMO[:, :, o_:o_ + RH], ropeK[:, 0], ropeK[:, 1], ALU.subtract)
            last = pool.tensor_tensor(TMO[:, :, o_ + RH:o_ + ROPE], ropeK[:, 2], ropeK[:, 3], ALU.add)
        then(last)
        pool.memset(WIN[:, :, 0:PADW], 0.0).then_inc(S["kr_ready"], 1)

        pool.wait_ge(S["wp_in"], 16)
        pool.tensor_scalar(flat(WP[:, HI]), flat(WPraw[:]), 1.0, None, ALU.mult).then_inc(S["wp_hi"], 1)
        pool.wait_ge(S["wuv_in"], 16)
        pool.tensor_scalar(flat(WUV[:, HI]), flat(WUVraw[:]), 1.0, None, ALU.mult).then_inc(S["wuv_hi"], 1)
        for i, g in enumerate(GORDER):
            pool.wait_ge(S["u_out"], 2 * (i + 1))
            if i < 2:
                wu_hi(i + 2)
            u = U[:, g]
            src, dst = u, WIN[:, 0]
            for s in range(g + 1):
                then(pool.tensor_tensor(dst[:, PADW:], src[:, PADW:], src[:, PADW - 2 ** s:PADW + SEQ - 2 ** s], ALU.add))
                src, dst = dst, WIN[:, (s + 1) % 2]
            w = 2 ** (g + 1)
            pool.tensor_scalar(src[:, PADW + w:], src[:, PADW + w:], 1.0 / w, None, ALU.mult)
            then(pool.tensor_tensor(src[:, PADW:PADW + w], src[:, PADW:PADW + w], INV[:, 0:w], ALU.mult))
            pool.tensor_tensor(u[:, PADW:], src[:, PADW:], u[:, PADW:], ALU.subtract).then_inc(S["pooled"], 1)
            pool.wait_ge(S["pooled"], i + 1)
            if i == 1:
                pool.wait_ge(S["wuq_in"], 16)
                pool.tensor_scalar(WUQ[:, HI].rearrange("p k h d -> p (k h d)"), WUQraw[:].rearrange("p k h d -> p (k h d)"),
                                   1.0, None, ALU.mult).then_inc(S["wuq_hi"], 1)

        def rotate(i, t):
            pool.wait_ge(S["qr_raw"], i + 1)
            if i >= 2:
                pool.wait_ge(S["qr_T"], i - 1)
            q1, q2 = QRAW[:, t, :, 0:RH], QRAW[:, t, :, RH:ROPE]
            cs = COS[:, t:t + 1, :].broadcast_to([P, HEADS, RH])
            sn = SIN[:, t:t + 1, :].broadcast_to([P, HEADS, RH])
            pool.tensor_tensor(ropeQ[:, 0], q1, cs, ALU.mult)
            pool.tensor_tensor(ropeQ[:, 1], q2, sn, ALU.mult)
            pool.tensor_tensor(ropeQ[:, 2], q1, sn, ALU.mult)
            then(pool.tensor_tensor(ropeQ[:, 3], q2, cs, ALU.mult))
            for d in range(2):
                pool.tensor_tensor(QRD[:, i % 2, :, d, 0:RH], ropeQ[:, 0], ropeQ[:, 1], ALU.subtract)
                last = pool.tensor_tensor(QRD[:, i % 2, :, d, RH:ROPE], ropeQ[:, 2], ropeQ[:, 3], ALU.add)
            last.then_inc(S["qr_rot"], 1)
            pool.wait_ge(S["qr_rot"], i + 1)

        pm = 0

        def pm_hi():
            nonlocal pm
            g, hf = GORDER[pm // 2], pm % 2
            pm += 1
            pool.wait_ge(S["pm_y"], pm)
            pool.tensor_scalar(HT[:, HI, 4 + g, half(hf)], HTf[:, 4 + g, half(hf)], 1.0, None, ALU.mult).then_inc(S["pm_hi"], 1)

        for i, t in enumerate(BLOCKS):
            pm_hi()
            rotate(i, t)

        def p_norm(n_, b, h):
            pool.wait_ge(S["rsum"], 4 * n_ + h + 1)
            m = 4 * n_ + h
            pool.tensor_scalar(PR[:, h, 0:(b + 1) * P], PR[:, h, 0:(b + 1) * P], RSUM[:, m:m + 1], None,
                               ALU.mult).then_inc(S["p_norm"], 1)

        for n_, b in enumerate(BLOCKS):
            for h in range(HEADS):
                p_norm(n_, b, h)

        pool.wait_ge(S["s_done"], 4 * NT)
        for i in range(4):
            pool.wait_ge(wo_in[i], 16)
            pool.tensor_scalar(WOhi[0][:, 2 * i, :], WOraw[0][:, 2 * i, :], 1.0, None, ALU.mult).then_inc(S["wo_hi"], 1)

        def x_add(m, c_, t):
            pool.wait_ge(S["mix_gated"], m + 1)
            if c_ == 0:
                pool.wait_ge(x_in[t], 32)
            pool.tensor_tensor(X[:, t, half(c_)], X[:, t, half(c_)], MIX[:, m % 2], ALU.add).then_inc(S["x_new"], 1)

        for t in range(NT):
            x_add(t, 0, t)
            if t == 1:
                pool.wait_ge(S["op_done"], NT)
            if t >= 1 and t % 2 == 1:
                i = t // 2
                pool.wait_ge(wo_in[i], 32)
                pool.tensor_scalar(WOhi[1][:, 2 * i, :], WOraw[1][:, 2 * i, :], 1.0, None, ALU.mult).then_inc(S["wo_hi"], 1)

        def h2_hi(t):
            pool.wait_ge(S["ev2"], t + 1)
            pool.tensor_scalar(HT[:, HI, :, tok(t)], HTf[:, :, tok(t)], 1.0, None, ALU.mult).then_inc(S["h2_hi"], 1)

        def xn2(t):
            pool.wait_ge(S["rs2"], t + 1)
            if t >= 2:
                pool.wait_ge(S["t2"], t - 1)
            pool.tensor_scalar(XN[:, t % 2], X[:, t, :], RS2[:, t:t + 1], None, ALU.mult).then_inc(S["xn2"], 1)

        def wd_fold(i):
            pool.wait_ge(wd_in, 16 * i + 16)
            for r in range(2):
                ins = pool.tensor_tensor(WDraw[:, r], WDraw[:, r], GT2[:], ALU.mult)
            ins.then_inc(S["wd_fold"], 1)

        for t in range(NT):
            x_add(NT + t, 1, t)
            if t >= 1:
                xn2(t - 1)
            if t >= 2:
                h2_hi(t - 2)
        xn2(NT - 1)
        h2_hi(NT - 2)
        h2_hi(NT - 1)
        wd_fold(0)
        wd_fold(1)
        with pool.Fori(2, NC) as i:
            wd_fold(i)

    @block.scalar
    def _(act):
        act.wait_ge(S["c_in"], 16)
        act.activation(CS[:], CT[:], ACT.Silu).then_inc(S["act_silu"], 1)
        act.wait_ge(S["ang_ready"], 1)
        act.activation(SHALF[:], ANG[:], ACT.Sin, scale=0.5)
        act.activation(SQUART[:], ANG[:], ACT.Sin, scale=0.25).then_inc(S["sin_ready"], 1)
        for t in range(NT):
            act.wait_ge(x_in[t], 16)
            act.activation(JUNK[:], X[:, t, :], ACT.Square, accum_out=SS[:, t:t + 1]).then_inc(S["ss1"], 1)
            act.wait_ge(S["ss1"], t + 1)
        for m in range(2 * NT):
            t, kk = divmod(m, 2)
            act.wait_ge(S["t1"], t + 1)
            act.activation(HTf[:, 4 * kk:4 * kk + 4, tok(t)],
                           PS[:, m % 4, :].rearrange("p (k n) -> p k n", k=4), ACT.Copy).then_inc(S["ev1"], 1)
        act.wait_ge(S["modcols"], 1)
        act.wait_ge(S["ev1"], 2 * NT)
        for m in range(2 * KT):
            hf, k = divmod(m, KT)
            act.activation(HTf[:, k, half(hf)], HTf[:, k, half(hf)], ACT.Identity,
                           scale=G1[:, k:k + 1], bias=MOD[:, k:k + 1]).then_inc(S["hmod"], 1)
        for t in range(NT):
            act.wait_ge(S["tm_done"], t + 1)
            b = 4 + t % 2
            act.activation(TMO[:, t, 0:TM], PS[:, b, 0:TM], ACT.Copy)
            act.activation(JUNK2[:, 0:QR], PS[:, b, 0:QR], ACT.Square, accum_out=SS[:, t:t + 1])
            act.activation(JUNK2[:, QR:QR + LAT], PS[:, b, QR:QR + LAT], ACT.Square,
                           accum_out=SS[:, 8 + t:9 + t]).then_inc(S["tm_out"], 1)
            act.wait_ge(S["tm_out"], t + 1)

        def u_out(i):
            g = GORDER[i]
            for hf in range(2):
                act.wait_ge(S["u_done"], 2 * i + hf + 1)
                act.activation(U[:, g, PADW + hf * HALF:PADW + (hf + 1) * HALF], PS[:, hf, :], ACT.Copy).then_inc(S["u_out"], 1)

        def lt_hi(t):
            act.wait_ge(S["lt_T"], t + 1)
            b = 2 + t % 2
            act.activation(LT[:, :, HI, tok(t)], PS[:, b, 0:3 * P].rearrange("p (k n) -> p k n", k=3), ACT.Copy)
            act.activation(KRT[:, HI, tok(t)], PS[:, b, 3 * P:], ACT.Copy).then_inc(S["lt_hi"], 1)

        def pooled_hi(i):
            g = GORDER[i]
            act.wait_ge(S["pooled"], i + 1)
            act.wait_ge(S["u_done"], 2 * GROUPS)
            act.activation(POOLHI[:, g], U[:, g, PADW:], ACT.Copy).then_inc(S["pool_hi"], 1)

        u_out(0)
        u_out(1)
        for t in range(4):
            lt_hi(t)
        u_out(2)
        for t in range(4, NT):
            lt_hi(t)
        act.wait_ge(S["wukT"], 1)
        act.activation(WUK[:, HI].rearrange("p h c -> p (h c)"), PS[:, 4, :], ACT.Copy).then_inc(S["wuk_hi"], 1)
        u_out(3)
        for i, t in enumerate(BLOCKS):
            act.wait_ge(S["qr_done"], i + 1)
            act.activation(QRAW[:, t].rearrange("p h d -> p (h d)"), PS[:, 2 + i % 2, 0:HEADS * ROPE], ACT.Copy).then_inc(S["qr_raw"], 1)
        for i in range(GROUPS):
            pooled_hi(i)

        def pm_y(m):
            g, hf = GORDER[m // 2], m % 2
            act.wait_ge(S["pm_done"], m + 1)
            act.activation(HTf[:, 4 + g, half(hf)], PS[:, m % 2, :], ACT.Copy,
                           scale=COLS[:, ROW_POOL + g:ROW_POOL + g + 1]).then_inc(S["pm_y"], 1)

        def ql_hi(i):
            hf, h = 1 - i // 4, i % 4
            act.wait_ge(S["ql_done"], i + 1)
            act.activation(QLhi[:, h, half(hf)], PS[:, 6 + i % 2, :], ACT.Copy).then_inc(S["ql_hi"], 1)

        for m in range(8):
            pm_y(m)
        for i, t in enumerate(BLOCKS):
            act.wait_ge(S["qn_done"], i + 1)
            if i >= 2:
                act.wait_ge(S["ql_done"], i - 1)
            act.activation(QN[:, i % 2, HI], PS[:, 4 + i % 2, :], ACT.Copy).then_inc(S["qn_hi"], 1)
            if i >= 1:
                ql_hi(i - 1)
            act.wait_ge(S["qr_T"], i + 1)
            act.activation(QS[:, :, tok(t)], PS[:, 2 + i % 2, :].rearrange("p (h n) -> p h n", h=HEADS), ACT.Copy).then_inc(S["qr_hi"], 1)
        ql_hi(7)

        def softmax_exp(n_, b, h):
            m = 4 * n_ + h
            act.wait_ge(S["negmax"], m + 1)
            if n_ >= 1:
                act.wait_ge(S["p_T"], m - 3)
            sl = 2 * (h % 2)
            act.activation(PR[:, h, 0:(b + 1) * P], flat(PS[:, sl:sl + 2, :])[:, 0:(b + 1) * P], ACT.Exp,
                           scale=SCALE, bias=NEGM[:, m:m + 1], accum_out=SUM[:, m:m + 1]).then_inc(S["exp_done"], 1)

        def turned_hi(n_, h):
            b = BLOCKS[n_]
            act.wait_ge(S["p_T"], 4 * n_ + h + 1)
            if h == 0 and n_ >= 1:
                act.wait_ge(S["pv_done"], n_)
            for j0 in range(0, b + 1, 4):
                nj = min(4, b + 1 - j0)
                last = act.activation(PT[:, HI, j0:j0 + nj, h, :],
                                      PS[:, 4 + j0 // 4, 0:nj * P].rearrange("p (j n) -> p j n", j=nj), ACT.Copy)
            last.then_inc(S["pt_hi"], 1)

        def latent_hi(n_):
            act.wait_ge(S["pv_done"], n_ + 1)
            if n_ >= 1:
                act.wait_ge(S["op_done"], n_)
            act.activation(OL[:, HI], PS[:, 6, :], ACT.Copy).then_inc(S["ol_hi"], 1)

        def out_hi(n_):
            act.wait_ge(S["op_done"], n_ + 1)
            act.activation(HT[:, HI, 0:HEADS, tok(BLOCKS[n_])], PS[:, 7, :].rearrange("p (h n) -> p h n", h=HEADS),
                           ACT.Copy).then_inc(S["y_hi"], 1)

        for n_, b in enumerate(BLOCKS):
            if n_ >= 2:
                out_hi(n_ - 2)
            for h in range(HEADS):
                if n_ >= 1:
                    turned_hi(n_ - 1, h)
                softmax_exp(n_, b, h)
            if n_ >= 1:
                latent_hi(n_ - 1)
        out_hi(NT - 2)
        for h in range(HEADS):
            turned_hi(NT - 1, h)
        latent_hi(NT - 1)

        for i in range(4):
            act.wait_ge(wo_in[i], 16)
            act.activation(WOhi[0][:, 2 * i + 1, :], WOraw[0][:, 2 * i + 1, :], ACT.Copy).then_inc(S["wo_hi_odd"], 1)
        out_hi(NT - 1)
        act.wait_ge(S["op_done"], NT)
        for i in range(4):
            act.wait_ge(wo_in[i], 32)
            act.activation(WOhi[1][:, 2 * i + 1, :], WOraw[1][:, 2 * i + 1, :], ACT.Copy).then_inc(S["wo_hi_odd"], 1)

        def squares2(t):
            act.wait_ge(S["x_new"], NT + t + 1)
            act.activation(JUNK2[:], X[:, t, :], ACT.Square, accum_out=SS2[:, t:t + 1]).then_inc(S["ss2"], 1)
            act.wait_ge(S["ss2"], t + 1)

        def modulate2(t):
            act.wait_ge(S["t2"], t + 1)
            act.wait_ge(S["modcols"], 2)
            for k in range(KT):
                bank = 4 + 2 * (t % 2) + k // 4
                last = act.activation(HTf[:, k, tok(t)], PS[:, bank, (k % 4) * P:(k % 4 + 1) * P], ACT.Identity,
                                      scale=G2[:, k:k + 1], bias=MOD[:, 16 + k:17 + k])
            last.then_inc(S["ev2"], 1)

        def wgu_hi(i, s):
            act.wait_ge(wgu_in[s], 32 * i + 32)
            act.activation(WGU[:, s, HI].rearrange("p a k n -> p (a k n)"),
                           WGUraw[:, s, LO].rearrange("p a k n -> p (a k n)"), ACT.Copy).then_inc(S["wgu_hi"], 1)

        def wd_hi(i):
            act.wait_ge(S["wd_fold"], i + 1)
            act.activation(flat(WD[:, HI]), flat(WDraw[:]), ACT.Copy).then_inc(S["wd_hi"], 1)

        for t in range(NT):
            squares2(t)
            if t >= 2:
                modulate2(t - 2)
            if t == 4:
                wgu_hi(0, 0)
        modulate2(NT - 2)
        modulate2(NT - 1)
        wgu_hi(0, 1)

        def chunk_act(i, par, more=True):
            first = isinstance(i, int) and i == 0
            if not first:
                wgu_hi(i, 1)
            for s in range(2):
                for hf in range(2):
                    m = 4 * i + 2 * s + hf
                    act.wait_ge(S["gu_half"], m + 1)
                    if not isinstance(m, int) or m >= 2:
                        act.wait_ge(S["act_ready"], m - 1)
                    act.activation(HID[:, hf], PS[:, 2 * hf, :], ACT.Silu).then_inc(S["silu"], 1)
                    act.wait_ge(S["hid"], m + 1)
                    act.activation(ACTS[:, 2 * par + s, HI, half(hf)], HID[:, hf], ACT.Copy).then_inc(S["act_hi"], 1)
                    if s == 1 and hf == 0 and not first:
                        wd_hi(i - 1)
                if s == 0 and more:
                    wgu_hi(i + 1, 0)

        chunk_act(0, 0)
        with act.Fori(0, (NC - 3) // 2) as j:
            for par in (1, 0):
                chunk_act(2 * j + (1 if par else 2), par)
        chunk_act(NC - 2, (NC - 2) % 2)
        chunk_act(NC - 1, (NC - 1) % 2, more=False)
        wd_hi(NC - 1)
        for t in range(NT):
            act.wait_ge(S["d_free"], 4 + 16 * (NC - 1) + 2 * t + 2)
            act.activation(JUNK2[:], X[:, t, :], ACT.Square, accum_out=SS3[:, t:t + 1]).then_inc(S["ss3"], 1)
            act.wait_ge(S["ss3"], t + 1)

    @block.vector
    def _(dve):
        n = 0

        def then(ins):
            nonlocal n
            n += 1
            ins.then_inc(S["dve_step"], 1)
            dve.wait_ge(S["dve_step"], n)

        def inverse_root(res, ss, cols, width, done):
            v, r, rt, ri = VAR[:, 0:cols], RS[:, 0:cols], RT[:, 0:cols], RI[:, 0:cols]
            if res is not None:
                r = res
            then(dve.tensor_scalar(v, ss, 1.0 / width, EPS, ALU.mult, ALU.add))
            then(dve.tensor_scalar(ri, v.bitcast(I32), 1, None, ALU.logical_shift_right))
            then(dve.tensor_scalar(r.bitcast(I32), ri, -1.0, RSQRT_MAGIC, ALU.mult, ALU.add))
            for step in range(4):
                then(dve.tensor_tensor(rt, r, r, ALU.mult))
                then(dve.scalar_tensor_tensor(rt, rt, -0.5, v, ALU.mult, ALU.mult))
                ins = dve.scalar_tensor_tensor(r, rt, 1.5, r, ALU.add, ALU.mult)
                if step < 3:
                    then(ins)
            ins.then_inc(done, 1)

        dve.wait_ge(S["pos_in"], 16)
        dve.wait_ge(S["freq_in"], 16)
        then(dve.tensor_copy(POSF[:], POSI[:]))
        for t in range(NT):
            ins = dve.tensor_scalar(ANG[:, t, :], FREQ[:], POSF[:, t:t + 1], None, ALU.mult)
        then(ins)
        for turns in (4096.0, 1.0):
            then(dve.tensor_scalar(TURN[:], ANG[:], float(1 / (2 * np.pi * turns)), ROUND_MAGIC, ALU.mult, ALU.add))
            then(dve.tensor_scalar(TURN[:], TURN[:], -ROUND_MAGIC, None, ALU.add))
            for part in two_pi_parts():
                then(dve.scalar_tensor_tensor(ANG[:], TURN[:], -part * turns, ANG[:], ALU.mult, ALU.add))
        dve.tensor_copy(TURN[:], ANG[:]).then_inc(S["ang_ready"], 1)

        def accumulate(q):
            ch, kh = divmod(q, 2)
            s, v = ada_sem(q)
            dve.wait_ge(s, v)
            if kh == 0 and ch >= 2:
                dve.wait_ge(S["colsum"], ch - 1)
            buf, acc = ada_buf(q), ACC[:, ch % 2]
            for t in range(4):
                cs = CS[:, 4 * kh + t:4 * kh + t + 1]
                if kh == 0 and t == 0:
                    ins = dve.tensor_scalar(acc, buf[:, t, :], cs, None, ALU.mult)
                else:
                    ins = dve.scalar_tensor_tensor(acc, buf[:, t, :], cs, acc, ALU.mult, ALU.add)
                if t < 3:
                    then(ins)
            ins.then_inc(S["acc_done"], 1)
            dve.wait_ge(S["acc_done"], q + 1)

        dve.wait_ge(S["act_silu"], 1)
        accumulate(0)
        dve.wait_ge(S["ss1"], 4)
        inverse_root(RS[:, 0:4], SS[:, 0:4], 4, D, S["rs1"])
        accumulate(1)
        dve.wait_ge(S["sin_ready"], 1)
        then(dve.tensor_tensor(COS[:], SHALF[:], SHALF[:], ALU.mult))
        then(dve.tensor_scalar(COS[:], COS[:], -2.0, 1.0, ALU.mult, ALU.add))
        then(dve.tensor_tensor(SIN[:], SQUART[:], SQUART[:], ALU.mult))
        then(dve.tensor_scalar(SIN[:], SIN[:], -4.0, 2.0, ALU.mult, ALU.add))
        then(dve.tensor_tensor(SIN[:], SIN[:], SHALF[:], ALU.mult))
        dve.wait_ge(S["ss1"], 8)
        inverse_root(RS[:, 4:8], SS[:, 4:8], 4, D, S["rs1"])
        accumulate(2)
        accumulate(3)
        dve.wait_ge(S["rowsT"], 1)
        then(dve.tensor_copy(COLS[:], PS[:, 6, 0:N_ROWS]))
        for q in range(4, 8):
            accumulate(q)
        dve.wait_ge(S["colsum"], 4)
        then(dve.tensor_tensor(MOD[:, 0:16], PS[:, 7, 0:16], COLS[:, 0:16], ALU.add))
        dve.scalar_tensor_tensor(G1[:], MOD[:, 8:16], 1.0, COLS[:, ROW_MIX:ROW_MIX + 8], ALU.add, ALU.mult).then_inc(S["modcols"], 1)

        def lo(out_, full, hi, ready):
            dve.tensor_tensor(out_, full, hi.bitcast(F32), ALU.subtract).then_inc(ready, 1)

        for i in range(4):
            dve.wait_ge(S["wtm_hi"], i + 1)
            lo(flat(WTM[:, LO, 2 * i:2 * i + 2, :]), flat(WTMraw[:, 2 * i:2 * i + 2, :]),
               flat(WTM[:, HI, 2 * i:2 * i + 2, :]), S["wtm_ready"])
        for m in range(2 * KT):
            hf, k = divmod(m, KT)
            dve.wait_ge(S["h_hi"], m + 1)
            lo(HT[:, LO, k, half(hf)], HTf[:, k, half(hf)], HT[:, HI, k, half(hf)], S["h_ready"])

        def wu_lo(g):
            dve.wait_ge(S["wu_hi"], g + 1)
            lo(flat(WU[:, g % 2, LO]), flat(WUraw[:, g % 2, LO]), flat(WU[:, g % 2, HI]), S["wu_ready"])

        def gate(ch):
            dve.wait_ge(S["gt_in"], 32)
            dve.wait_ge(S["colsum"], ch + 1)
            gt = GT1 if ch < 6 else GT2
            dve.tensor_tensor(gt[:, half(ch % 2)], PS[:, 6, :], gt[:, half(ch % 2)], ALU.add).then_inc(S["gt_ready"], 1)

        for q in range(8, 16):
            accumulate(q)
            if q == 9:
                wu_lo(0)
            if q == 10:
                wu_lo(1)
            if q == 12:
                gate(4)
            if q == 14:
                gate(5)
        dve.wait_ge(S["tm_out"], NT)
        inverse_root(None, SS[:, 0:8], 8, QR, S["rs1"])
        dve.wait_ge(S["rs1"], 3)
        dve.wait_ge(S["gq_in"], 16)
        dve.wait_ge(S["gkv_in"], 16)
        for t in range(NT):
            ins = dve.scalar_tensor_tensor(TMO[:, t, 0:QR], TMO[:, t, 0:QR], RS[:, t:t + 1], GQ[:], ALU.mult, ALU.mult)
        then(ins)
        inverse_root(None, SS[:, 8:16], 8, LAT, S["rs1"])
        dve.wait_ge(S["rs1"], 4)
        for t in range(NT):
            dve.scalar_tensor_tensor(TMO[:, t, QR:QR + LAT], TMO[:, t, QR:QR + LAT], RS[:, t:t + 1], GKV[:],
                                     ALU.mult, ALU.mult).then_inc(S["tm_norm"], 1)
        for q in range(16, 18):
            accumulate(q)
        dve.wait_ge(S["ckv_hi"], 1)
        lo(CKV[:, LO], TMO[:, :, QR:QR + LAT], CKV[:, HI], S["ckv_ready"])
        def lt_lo(t):
            dve.wait_ge(S["lt_hi"], t + 1)
            b = 2 + t % 2
            dve.tensor_tensor(LT[:, :, LO, tok(t)], PS[:, b, 0:3 * P].rearrange("p (k n) -> p k n", k=3),
                              LT[:, :, HI, tok(t)].bitcast(F32), ALU.subtract)
            lo(KRT[:, LO, tok(t)], PS[:, b, 3 * P:], KRT[:, HI, tok(t)], S["lt_lo"])

        for q in range(18, 22):
            accumulate(q)
        wu_lo(2)
        for t in range(4):
            lt_lo(t)
        for q in range(22, 24):
            accumulate(q)
        dve.wait_ge(S["colsum"], 10)
        then(dve.tensor_tensor(MOD[:, 16:32], PS[:, 7, 16:32], COLS[:, 24:40], ALU.add))
        dve.scalar_tensor_tensor(G2[:], MOD[:, 24:32], 1.0, COLS[:, ROW_FFN:ROW_FFN + 8],
                                 ALU.add, ALU.mult).then_inc(S["modcols"], 1)
        dve.wait_ge(S["wp_hi"], 1)
        lo(flat(WP[:, LO]), flat(WPraw[:]), flat(WP[:, HI]), S["wp_ready"])
        dve.wait_ge(S["wuv_hi"], 1)
        lo(flat(WUV[:, LO]), flat(WUVraw[:]), flat(WUV[:, HI]), S["wuv_ready"])
        wu_lo(3)
        gate(10)
        for t in range(4, NT):
            lt_lo(t)
        gate(11)
        dve.wait_ge(S["wuq_hi"], 1)
        lo(WUQ[:, LO].rearrange("p k h d -> p (k h d)"), WUQraw[:].rearrange("p k h d -> p (k h d)"),
           WUQ[:, HI].rearrange("p k h d -> p (k h d)"), S["wuq_ready"])
        dve.wait_ge(S["wuk_hi"], 1)
        lo(WUK[:, LO].rearrange("p h c -> p (h c)"), PS[:, 4, :], WUK[:, HI].rearrange("p h c -> p (h c)"), S["wuk_ready"])
        for i, g in enumerate(GORDER):
            dve.wait_ge(S["pool_hi"], i + 1)
            lo(UR[:, g, PADW:], U[:, g, PADW:], POOLHI[:, g], S["pool_lo"])

        def pm_lo(m):
            g, hf = GORDER[m // 2], m % 2
            dve.wait_ge(S["pm_hi"], m + 1)
            lo(HT[:, LO, 4 + g, half(hf)], HTf[:, 4 + g, half(hf)], HT[:, HI, 4 + g, half(hf)], S["pm_lo"])

        def ql_lo(i):
            hf, h = 1 - i // 4, i % 4
            dve.wait_ge(S["ql_hi"], i + 1)
            lo(QLlo[:, h, half(hf)], PS[:, 6 + i % 2, :], QLhi[:, h, half(hf)], S["ql_lo"])

        for i, t in enumerate(BLOCKS):
            dve.wait_ge(S["qn_hi"], i + 1)
            lo(QN[:, i % 2, LO], PS[:, 4 + i % 2, :], QN[:, i % 2, HI], S["qn_lo"])
            if i >= 1:
                ql_lo(i - 1)
            pm_lo(i)
            dve.wait_ge(S["qr_hi"], i + 1)
            lo(QS[ROPE:P, :, tok(t)], PS[ROPE:P, 2 + i % 2, :].rearrange("p (h n) -> p h n", h=HEADS),
               QS[ROPE:P, :, tok(t)], S["qr_lo"])
        ql_lo(7)

        def row_max(n_, h):
            m = 4 * n_ + h
            dve.wait_ge(S["s_done"], m + 1)
            sl = 2 * (h % 2)
            then(dve.tensor_reduce(RSUM[:, m:m + 1], flat(PS[:, sl:sl + 2, :])[:, 0:(BLOCKS[n_] + 1) * P], AX.X, ALU.max))
            dve.tensor_scalar(NEGM[:, m:m + 1], RSUM[:, m:m + 1], -SCALE, None, ALU.mult).then_inc(S["negmax"], 1)

        def inv_sum(n_, h):
            m = 4 * n_ + h
            dve.wait_ge(S["exp_done"], m + 1)
            dve.reciprocal(RSUM[:, m:m + 1], SUM[:, m:m + 1]).then_inc(S["rsum"], 1)

        def turned_lo(n_, h):
            b = BLOCKS[n_]
            dve.wait_ge(S["pt_hi"], 4 * n_ + h + 1)
            for j0 in range(0, b + 1, 4):
                nj = min(4, b + 1 - j0)
                ins = dve.tensor_tensor(PT[:, LO, j0:j0 + nj, h, :],
                                        PS[:, 4 + j0 // 4, 0:nj * P].rearrange("p (j n) -> p j n", j=nj),
                                        PT[:, HI, j0:j0 + nj, h, :].bitcast(F32), ALU.subtract)
            ins.then_inc(S["pt_lo"], 1)

        def latent_lo(n_):
            dve.wait_ge(S["ol_hi"], n_ + 1)
            lo(OL[:, LO], PS[:, 6, :], OL[:, HI], S["ol_lo"])

        def out_lo(n_):
            dve.wait_ge(S["y_hi"], n_ + 1)
            t = tok(BLOCKS[n_])
            lo(HT[:, LO, 0:HEADS, t], PS[:, 7, :].rearrange("p (h n) -> p h n", h=HEADS), HT[:, HI, 0:HEADS, t], S["y_lo"])

        for n_ in range(NT):
            row_max(n_, 0)
            if n_ >= 2:
                out_lo(n_ - 2)
            for h in range(HEADS):
                if n_ >= 1 and h < 3:
                    turned_lo(n_ - 1, h)
                if h == 2 and n_ >= 1:
                    turned_lo(n_ - 1, 3)
                if h < 3:
                    row_max(n_, h + 1)
                inv_sum(n_, h)
            if n_ >= 1:
                latent_lo(n_ - 1)
        out_lo(NT - 2)
        for h in range(HEADS):
            turned_lo(NT - 1, h)
        latent_lo(NT - 1)

        def wo_lo(c_, k):
            i, odd = divmod(k, 2)
            if odd:
                dve.wait_ge(S["wo_hi_odd"], 4 * c_ + i + 1)
            else:
                dve.wait_ge(S["wo_hi"], 4 * c_ + i + 1)
            lo(WOlo[c_][:, k, :], WOraw[c_][:, k, :], WOhi[c_][:, k, :], S["wo_ready"])

        for k in range(KT):
            wo_lo(0, k)
        out_lo(NT - 1)

        def gated(m, c_):
            dve.wait_ge(S["mix_done"], m + 1)
            if m >= 2:
                dve.wait_ge(S["x_new"], m - 1)
            dve.tensor_tensor(MIX[:, m % 2], PS[:, m % 4, :], GT1[:, half(c_)], ALU.mult).then_inc(S["mix_gated"], 1)

        for t in range(NT):
            gated(t, 0)
            if t in (2, 4, 6):
                for k in (t - 2, t - 1):
                    wo_lo(1, k)
        wo_lo(1, 6)
        wo_lo(1, 7)

        def wgu_lo(i, s):
            dve.wait_ge(S["wgu_hi"], 2 * i + s + 1)
            dve.tensor_tensor(WGU[:, s, LO].rearrange("p a k n -> p (a k n)"),
                              WGUraw[:, s, LO].rearrange("p a k n -> p (a k n)"),
                              WGU[:, s, HI].bitcast(F32).rearrange("p a k n -> p (a k n)"), ALU.subtract).then_inc(S["wgu_ready"], 1)

        def h2_lo(t):
            dve.wait_ge(S["h2_hi"], t + 1)
            lo(HT[:, LO, :, tok(t)], HTf[:, :, tok(t)], HT[:, HI, :, tok(t)], S["h2_ready"])

        for t in range(NT):
            gated(NT + t, 1)
            if t >= 1:
                dve.wait_ge(S["ss2"], t)
                inverse_root(RS2[:, t - 1:t], SS2[:, t - 1:t], 1, D, S["rs2"])
            if t >= 2:
                h2_lo(t - 2)
            if t == 5:
                wgu_lo(0, 0)
        dve.wait_ge(S["ss2"], NT)
        inverse_root(RS2[:, NT - 1:NT], SS2[:, NT - 1:NT], 1, D, S["rs2"])
        h2_lo(NT - 2)
        h2_lo(NT - 1)
        dve.sem_inc(S["d_free"], 4)
        wgu_lo(0, 1)

        def hid(m, r):
            dve.wait_ge(S["silu"], m + 1)
            dve.tensor_tensor(HID[:, r], HID[:, r], PS[:, 2 * r + 1, :], ALU.mult).then_inc(S["hid"], 1)

        def act_lo(m, r, slot, hf):
            dve.wait_ge(S["act_hi"], m + 1)
            lo(ACTS[:, slot, LO, half(hf)], HID[:, r], ACTS[:, slot, HI, half(hf)], S["act_ready"])

        def wd_lo(i):
            dve.wait_ge(S["wd_hi"], i + 1)
            lo(flat(WD[:, LO]), flat(WDraw[:]), flat(WD[:, HI]), S["wd_ready"])

        def add_down(i):
            for m in range(2 * NT):
                t, c_ = divmod(m, 2)
                dve.wait_ge(S["d_bank"], 16 * i + m + 1)
                dve.tensor_tensor(X[:, t, half(c_)], PS[:, 4 + m % 4, :], X[:, t, half(c_)], ALU.add).then_inc(S["d_free"], 1)

        def chunk_dve(i, par, more=True):
            first = isinstance(i, int) and i == 0
            if not first:
                wgu_lo(i, 1)
            for s in range(2):
                for hf in range(2):
                    m = 4 * i + 2 * s + hf
                    hid(m, hf)
                    act_lo(m, hf, 2 * par + s, hf)
                    if s == 1 and hf == 0 and not first:
                        wd_lo(i - 1)
                if s == 0 and more:
                    wgu_lo(i + 1, 0)
            if not first:
                add_down(i - 1)

        chunk_dve(0, 0)
        with dve.Fori(0, (NC - 3) // 2) as j:
            for par in (1, 0):
                chunk_dve(2 * j + (1 if par else 2), par)
        chunk_dve(NC - 2, (NC - 2) % 2)
        chunk_dve(NC - 1, (NC - 1) % 2, more=False)
        wd_lo(NC - 1)

        def finish(t):
            dve.wait_ge(S["ss3"], t + 1)
            inverse_root(RS3[:, t:t + 1], SS3[:, t:t + 1], 1, D, S["rs3"])
            dve.wait_ge(S["rs3"], t + 1)
            dve.wait_ge(S["gfin_in"], 16)
            dve.scalar_tensor_tensor(X[:, t, :], X[:, t, :], RS3[:, t:t + 1], GT1[:], ALU.mult, ALU.mult).then_inc(S["fin"], 1)

        for m in range(2 * NT):
            t, c_ = divmod(m, 2)
            dve.wait_ge(S["d_bank"], 16 * (NC - 1) + m + 1)
            dve.tensor_tensor(X[:, t, half(c_)], PS[:, 4 + m % 4, :], X[:, t, half(c_)], ALU.add).then_inc(S["d_free"], 1)
            if c_ == 1 and t >= 1:
                finish(t - 1)
        finish(NT - 1)

    @block.tensor
    def _(pe):
        def product(ps, terms):
            terms = list(terms)
            for n_, (l, r) in enumerate(terms):
                ins = pe.matmul(ps, l, r, start=(n_ == 0), stop=(n_ == len(terms) - 1))
            return ins

        pe.wait_ge(S["pool_const"], 1)
        for t in range(NT):
            pe.wait_ge(S["xn1"], t + 1)
            if t >= 2:
                pe.wait_ge(S["ev1"], 2 * t - 2)
            for k in range(KT):
                ins = pe.transpose(PS[:, 2 * (t % 2) + k // 4, (k % 4) * P:(k % 4 + 1) * P], X[:, t, k * P:(k + 1) * P], IDENT[:])
            ins.then_inc(S["t1"], 1)
            if t == 3:
                pe.wait_ge(S["rows_in"], 64)
                pe.transpose(PS[:, 6, 0:N_ROWS], ROWS[0:N_ROWS, :], IDENT[0:N_ROWS, 0:N_ROWS]).then_inc(S["rowsT"], 1)

        def col_sum(ch):
            pe.wait_ge(S["acc_done"], 2 * ch + 2)
            if ch in (4, 5, 10, 11):
                if ch in (5, 11):
                    pe.wait_ge(S["gt_ready"], 1 if ch == 5 else 3)
                if ch == 10:
                    pe.wait_ge(S["gt_ready"], 2)
                if ch == 4:
                    pe.wait_ge(S["modcols"], 1)
                pe.matmul(PS[:, 6, :], ONES[:], ACC[:, ch % 2], start=True, stop=True).then_inc(S["colsum"], 1)
                return
            col = 4 * ch if ch < 4 else 16 + 4 * (ch - 6)
            for j in range(4):
                ins = pe.matmul(PS[:, 7, col + j:col + j + 1], ACC[:, ch % 2, j * P:(j + 1) * P], ONES[:, 0:1], start=True, stop=True)
            ins.then_inc(S["colsum"], 1)

        for ch in range(4):
            col_sum(ch)

        for t in range(NT):
            pe.wait_ge(S["wtm_ready"], 4)
            pe.wait_ge(S["h_ready"], KT * (t // 4 + 1))
            if t >= 2:
                pe.wait_ge(S["tm_out"], t - 1)
            product(PS[:, 4 + t % 2, 0:TM], [(HT[:, a, k, tok(t)], WTM[:, b, k, :]) for k in range(KT) for a, b in PASSES]
                    ).then_inc(S["tm_done"], 1)
            if t in (3, 5, 7):
                col_sum(4 + (t - 3) // 2)

        def pool_group(i):
            pe.wait_ge(S["wu_ready"], i + 1)
            for hf in range(2):
                if i >= 1:
                    pe.wait_ge(S["u_out"], 2 * i - 1 + hf)
                product(PS[:, hf, :], [(WU[:, i % 2, a, k, :], HT[:, b, k, half(hf)]) for k in range(KT) for a, b in PASSES]
                        ).then_inc(S["u_done"], 1)

        def turn_latents(t):
            pe.wait_ge(S["tm_norm"], NT)
            pe.wait_ge(S["kr_ready"], 1)
            if t >= 2:
                pe.wait_ge(S["lt_lo"], t - 1)
            for i, c0 in enumerate((0, P, QR, QR + LAT)):
                ins = pe.transpose(PS[:, 2 + t % 2, i * P:(i + 1) * P], TMO[:, t, c0:c0 + P], IDENT[:])
            ins.then_inc(S["lt_T"], 1)

        pool_group(0)
        col_sum(7)
        col_sum(8)
        pool_group(1)
        col_sum(9)
        for t in range(4):
            turn_latents(t)
        pool_group(2)
        col_sum(10)
        for t in range(4, NT):
            turn_latents(t)
        col_sum(11)
        pe.wait_ge(S["wuk_in"], 16)
        for h in range(HEADS):
            ins = pe.transpose(PS[:, 4, h * P:(h + 1) * P], WUKraw[:, h, :], IDENT[:])
        ins.then_inc(S["wukT"], 1)
        pool_group(3)

        pe.wait_ge(S["wuq_ready"], 1)
        pe.wait_ge(S["lt_lo"], NT)
        for i, t in enumerate(BLOCKS):
            if i >= 2:
                pe.wait_ge(S["qr_raw"], i - 1)
            product(PS[:, 2 + i % 2, 0:HEADS * ROPE].rearrange("p (h d) -> p h d", h=HEADS),
                    [(LT[:, k, a, tok(t)], WUQ[:, b, k, :, NOPE:]) for k in range(2) for a, b in PASSES]).then_inc(S["qr_done"], 1)

        pe.wait_ge(S["wp_ready"], 1)
        pe.wait_ge(S["u_out"], 2 * GROUPS)
        pool_parts = {HI: POOLHI, LO: UR}
        for m in range(2 * GROUPS):
            g, hf = GORDER[m // 2], m % 2
            pe.wait_ge(S["pool_lo"], m // 2 + 1)
            if m >= 2:
                pe.wait_ge(S["pm_y"], m - 1)
            product(PS[:, m % 2, :], [(WP[:, a, g, :], POOLHI[:, g, half(hf)] if b == HI else UR[:, g, PADW + hf * HALF:PADW + (hf + 1) * HALF])
                                      for a, b in PASSES]).then_inc(S["pm_done"], 1)

        def q_nope(i):
            hf, h = 1 - i // 4, i % 4
            if i == 0:
                pe.wait_ge(S["wuk_ready"], 1)
            if i >= 2:
                pe.wait_ge(S["qn_lo"], i - 1)
            product(PS[:, 4 + i % 2, :], [(WUQ[:, a, k, h, 0:NOPE], LT[:, k, b, half(hf)]) for k in range(2) for a, b in PASSES]
                    ).then_inc(S["qn_done"], 1)

        def q_latent(i):
            h = i % 4
            if i == 0:
                pe.wait_ge(S["gt_ready"], 4)
                pe.wait_ge(S["modcols"], 2)
            pe.wait_ge(S["qn_lo"], i + 1)
            if i >= 2:
                pe.wait_ge(S["ql_lo"], i - 1)
            product(PS[:, 6 + i % 2, :], [(WUK[:, a, h, :], QN[:, i % 2, b, :]) for a, b in PASSES]).then_inc(S["ql_done"], 1)

        def turn_rope(i):
            pe.wait_ge(S["qr_rot"], i + 1)
            pe.wait_ge(S["qr_raw"], NT)
            if i >= 2:
                pe.wait_ge(S["qr_lo"], i - 1)
            for h in range(HEADS):
                ins = pe.transpose(PS[:, 2 + i % 2, h * P:(h + 1) * P], QRD[:, i % 2, h].rearrange("p a d -> p (a d)"), IDENT[:])
            ins.then_inc(S["qr_T"], 1)

        for i in range(NT):
            q_nope(i)
            if i >= 1:
                q_latent(i - 1)
            turn_rope(i)
        q_latent(NT - 1)

        QL = (QLhi, QLlo)

        def scores(n_, h):
            b = BLOCKS[n_]
            m = 4 * n_ + h
            if m == 0:
                pe.wait_ge(S["ql_lo"], 8)
                pe.wait_ge(S["qr_lo"], NT)
                pe.wait_ge(S["pm_y"], 8)
            if m >= 2:
                pe.wait_ge(S["exp_done"], m - 1)
            for c0 in range(0, b + 1, 4):
                nk = min(4, b + 1 - c0)
                ks = slice(c0 * P, (c0 + nk) * P)
                bank = PS[:, 2 * (h % 2) + c0 // 4, 0:nk * P]
                q = tok(b)
                terms = [(QL[a_][:, h, q], LT[:, 2, b_, ks]) for a_, b_ in PASSES]
                terms += [(QS[:, h, q], KRT[:, a_, ks]) for a_ in (HI, LO)]
                diag = c0 + nk == b + 1
                for z, (l, r) in enumerate(terms):
                    ins = pe.matmul(bank, l, r, start=(z == 0), stop=(z == 4 and not diag))
                if diag:
                    ins = pe.matmul(bank[:, (nk - 1) * P:nk * P], MASKQ[:], MASKK[:], start=False, stop=True)
            ins.then_inc(S["s_done"], 1)

        def turn_p(n_, h):
            b = BLOCKS[n_]
            m = 4 * n_ + h
            pe.wait_ge(S["p_norm"], m + 1)
            if m >= 1:
                pe.wait_ge(S["pt_lo"], m)
            for j in range(b + 1):
                ins = pe.transpose(PS[:, 4 + j // 4, (j % 4) * P:(j % 4 + 1) * P], PR[:, h, j * P:(j + 1) * P], IDENT[:])
            ins.then_inc(S["p_T"], 1)

        def values(n_):
            b = BLOCKS[n_]
            pe.wait_ge(S["ckv_ready"], 1)
            pe.wait_ge(S["pt_lo"], 4 * n_ + 4)
            if n_ >= 1:
                pe.wait_ge(S["ol_lo"], n_)
            product(PS[:, 6, :], [(CKV[:, a_, j, :], PT[:, b_, j].rearrange("p h n -> p (h n)"))
                                  for j in range(b + 1) for a_, b_ in PASSES]).then_inc(S["pv_done"], 1)

        def up_values(n_):
            pe.wait_ge(S["wuv_ready"], 1)
            pe.wait_ge(S["ol_lo"], n_ + 1)
            if n_ >= 1:
                pe.wait_ge(S["y_lo"], n_)
            for h in range(HEADS):
                ins = product(PS[:, 7, h * P:(h + 1) * P], [(WUV[:, a_, h, :], OL[:, b_, h * P:(h + 1) * P]) for a_, b_ in PASSES])
            ins.then_inc(S["op_done"], 1)

        for n_ in range(NT):
            scores(n_, 0)
            if n_ >= 2:
                up_values(n_ - 2)
            if n_ >= 1:
                turn_p(n_ - 1, 0)
            scores(n_, 1)
            if n_ >= 1:
                turn_p(n_ - 1, 1)
            scores(n_, 2)
            if n_ >= 1:
                turn_p(n_ - 1, 2)
                turn_p(n_ - 1, 3)
            scores(n_, 3)
            if n_ >= 1:
                values(n_ - 1)
        up_values(NT - 2)
        for h in range(HEADS):
            turn_p(NT - 1, h)
        values(NT - 1)
        up_values(NT - 1)

        def mix(m):
            c_, t = divmod(m, NT)
            if m == 0:
                pe.wait_ge(S["y_lo"], NT)
                pe.wait_ge(S["pm_lo"], 8)
            pe.wait_ge(S["wo_ready"], KT * (c_ + 1))
            if m >= 4:
                pe.wait_ge(S["mix_gated"], m - 3)
            W = {HI: WOhi[c_], LO: WOlo[c_]}
            product(PS[:, m % 4, :], [(HT[:, a_, k, tok(t)], W[b_][:, k, :]) for k in range(KT) for a_, b_ in PASSES]
                    ).then_inc(S["mix_done"], 1)

        def turn_x(t):
            pe.wait_ge(S["xn2"], t + 1)
            if t >= 2:
                pe.wait_ge(S["ev2"], t - 1)
            for k in range(KT):
                ins = pe.transpose(PS[:, 4 + 2 * (t % 2) + k // 4, (k % 4) * P:(k % 4 + 1) * P], XN[:, t % 2, k * P:(k + 1) * P], IDENT[:])
            ins.then_inc(S["t2"], 1)

        for m in range(2 * NT):
            mix(m)
            if m >= NT + 2:
                turn_x(m - NT - 2)

        def gate_up(i, s, hf, first=False):
            if hf == 0:
                pe.wait_ge(S["wgu_ready"], 2 * i + s + 1)
            m = 4 * i + 2 * s + hf
            if not first:
                pe.wait_ge(S["hid"], m - 1)
            for a in range(2):
                ins = product(PS[:, 2 * hf + a, :], [(WGU[:, s, w_, a, k, :], HT[:, h_, k, half(hf)])
                                                     for k in range(KT) for w_, h_ in PASSES])
            ins.then_inc(S["gu_half"], 1)

        def down(i, par):
            pe.wait_ge(S["wd_ready"], i + 1)
            pe.wait_ge(S["act_ready"], 4 * i + 4)
            for m in range(2 * NT):
                t, c_ = divmod(m, 2)
                pe.wait_ge(S["d_free"], 16 * i + m + 1)
                product(PS[:, 4 + m % 4, :], [(ACTS[:, 2 * par + s, a_, tok(t)], WD[:, b_, s, half(c_)])
                                              for s in range(2) for a_, b_ in PASSES]).then_inc(S["d_bank"], 1)

        pe.wait_ge(S["mix_gated"], 2 * NT)
        pe.wait_ge(S["h2_ready"], 4)
        gate_up(0, 0, 0, first=True)
        turn_x(NT - 2)
        turn_x(NT - 1)
        pe.wait_ge(S["h2_ready"], NT)
        gate_up(0, 0, 1, first=True)
        for hf in range(2):
            gate_up(0, 1, hf)

        def chunk_pe(i, par):
            for s in range(2):
                for hf in range(2):
                    gate_up(i, s, hf)
            down(i - 1, 1 - par)

        with pe.Fori(0, (NC - 3) // 2) as j:
            for par in (1, 0):
                chunk_pe(2 * j + (1 if par else 2), par)
        chunk_pe(NC - 2, (NC - 2) % 2)
        chunk_pe(NC - 1, (NC - 1) % 2)
        down(NC - 1, (NC - 1) % 2)

    ctx.close()


_INS = ["x", "c", "positions", "w_ada", "b_ada", "g_mix", "w_in", "g_q", "g_kv", "w_uq", "w_uk", "w_uv",
        "w_pool", "pool_scale", "w_o", "g_ffn", "w_gate", "w_up", "w_down", "g_final"]


def kernel(**inputs):
    import concourse.bacc as bacc
    from concourse.bass_utils import run_bass_kernel_spmd as run

    nc = bacc.Bacc("TRN2", target_bir_lowering=False, num_devices=1)
    arrays, args = {}, []
    for name in _INS:
        a = np.ascontiguousarray(inputs[name])
        arrays[f"in_{name}"] = a
        args.append(nc.dram_tensor(f"in_{name}", a.shape, mybir.dt.from_np(a.dtype), kind="ExternalInput").ap())
    f = np.power(10000.0, -np.arange(RH) / RH).astype(np.float32)
    arrays["freqs"] = f
    args.append(nc.dram_tensor("freqs", f.shape, F32, kind="ExternalInput").ap())
    args.append(nc.dram_tensor("out", (1, SEQ, D), F32, kind="ExternalOutput").ap())
    hybrid_block(nc, *args)
    r = run(nc, [arrays], core_ids=[0])
    return r.results[0]["out"]
```

```python
from contextlib import ExitStack

import numpy as np

import concourse.bass as bass
from concourse import mybir

ALU = mybir.AluOpType
ACT = mybir.ActivationFunctionType
AX = mybir.AxisListType
F32 = mybir.dt.float32
F32R = mybir.dt.float32r
BF16 = mybir.dt.bfloat16
I32 = mybir.dt.int32

P = 128
SEQ = 1024
D = 1024
KT = D // P
NT = SEQ // P
HALF = 512
HEADS = 4
NOPE = 128
ROPE = 64
RH = ROPE // 2
QR = 256
LAT = 128
VD = 128
TM = QR + LAT + ROPE
TMW = TM + ROPE
CHUNK = 64
GROUPS = 4
PADW = 16
DFF = 2816
FT = DFF // P
NC = FT // 2
EPS = 1e-6
SCALE = float((NOPE + ROPE) ** -0.5)
MASKED = -float(2.0 ** 100)
HI, LO = 0, 1
PASSES = ((HI, LO), (HI, HI), (LO, HI))
RSQRT_MAGIC = float(0x5F3759DF)
ROUND_MAGIC = float(3 * 2 ** 22)
N_ROWS = 48 + 8 + 8 + 4
ROW_MIX, ROW_FFN, ROW_POOL = 48, 56, 64
KB = 1024


def two_pi_parts():
    rest, parts = 2 * np.pi, []
    for _ in range(4):
        e = int(np.floor(np.log2(rest))) - 6
        part = float(np.floor(rest / 2.0 ** e) * 2.0 ** e)
        parts.append(part)
        rest -= part
    return parts + [float(np.float32(rest))]


def hybrid_block(nc, x, c, positions, w_ada, b_ada, g_mix, w_in, g_q, g_kv, w_uq, w_uk, w_uv,
                 w_pool, pool_scale, w_o, g_ffn, w_gate, w_up, w_down, g_final, freqs, out):
    ctx = ExitStack()
    enter = ctx.enter_context
    base = 16512
    nc.alloc_sbuf_tensor("arena", [P, (229344 - base) // 4], F32)

    def at(name, kb, shape, dt=F32):
        return nc.alloc_sbuf_tensor_at(name, shape, dt, offset=base + int(kb * KB))

    def sem(name):
        return enter(nc.semaphore(name))

    X = at("X", 0, [P, NT, D])
    PT = at("PT", 0, [P, 2, NT, HEADS, P], F32R)
    U = at("U", 0, [P, GROUPS, PADW + SEQ])
    UR = at("UR", 0, [P, GROUPS, PADW + SEQ], F32R)
    WIN = at("WIN", 16.25, [P, 2, PADW + SEQ])
    ropeK = at("ropeK", 16.25, [P, 2, NT, 2, RH])
    ropeQ = at("ropeQ", 16.25, [P, 2, HEADS, 2, RH])
    QRD = at("QRD", 18.25, [P, 2, HEADS, 2, ROPE])
    WP = at("WP", 24.5, [P, 2, GROUPS, P], F32R)
    WPraw = at("WPraw", 26.5, [P, GROUPS, P])
    HT = at("HT", 32, [P, 2, KT, SEQ], F32R)
    HTf = at("HTf", 64, [P, KT, SEQ])
    ADA0 = at("ADA0", 32, [P, 4, 4, HALF])
    QRAW = at("QRAW", 32, [P, NT, HEADS, ROPE])
    QN = at("QN", 40, [P, 2, 2, HALF], F32R)
    POOLHI = at("POOLHI", 64, [P, GROUPS, SEQ], F32R)
    QS = at("QS", 64, [P, HEADS, SEQ], F32R)
    WTM = at("WTM", 96, [P, 2, KT, TM], F32R)
    WTMraw = at("WTMraw", 110, [P, KT, TM])
    LT = at("LT", 96, [P, 3, 2, SEQ], F32R)
    PR = at("PR", 96, [P, HEADS, SEQ])
    WUV = at("WUV", 120, [P, 2, HEADS, VD], F32R)
    WUVraw = at("WUVraw", 122, [P, HEADS, VD])
    WU = at("WU", 124, [P, 2, 2, KT, P], F32R)
    WUraw = at("WUraw", 124, [P, 2, 2, KT, P])
    ADAS = at("ADAS", 124, [P, 4, 4, HALF])
    QLhi = at("QLhi", 124, [P, HEADS, SEQ], F32R)
    QLlo = at("QLlo", 156, [P, HEADS, SEQ], F32R)
    ADA1 = at("ADA1", 140, [P, 2, 4, HALF])
    WUQ = at("WUQ", 140, [P, 2, 2, HEADS, NOPE + ROPE], F32R)
    WUQraw = at("WUQraw", 146, [P, 2, HEADS, NOPE + ROPE])
    WUK = at("WUK", 152, [P, 2, HEADS, LAT], F32R)
    WUKraw = at("WUKraw", 152, [P, HEADS, NOPE])
    TMO = at("TMO", 156, [P, NT, TMW])
    JUNK = at("JUNK", 156, [P, SEQ])
    ACC = at("ACC", 172, [P, 2, HALF])
    OL = at("OL", 172, [P, 2, HALF], F32R)
    CKV = at("CKV", 176, [P, 2, NT, LAT], F32R)
    KRT = at("KRT", 184, [P, 2, SEQ], F32R)
    COS = at("COS", 192, [P, NT, RH])
    SIN = at("SIN", 193, [P, NT, RH])
    GQ = at("GQ", 194, [P, QR])
    GKV = at("GKV", 195, [P, LAT])
    ROWS = at("ROWS", 195.5, [P, P])
    ANG = at("ANG", 0, [P, NT, RH])
    TURN = at("TURN", 1, [P, NT, RH])
    SHALF = at("SHALF", 2, [P, NT, RH])
    SQUART = at("SQUART", 3, [P, NT, RH])
    WOlo = [at("WOlo0", 140, [P, KT, HALF], F32R), at("WOlo1", 112, [P, KT, HALF], F32R)]
    WOraw = [at("WOraw0", 140, [P, KT, HALF]), at("WOraw1", 112, [P, KT, HALF])]
    WOhi = [at("WOhi0", 156, [P, KT, HALF], F32R), at("WOhi1", 96, [P, KT, HALF], F32R)]
    MIX = at("MIX", 176, [P, 2, HALF])
    JUNK2 = at("JUNK2", 180, [P, SEQ])
    XN = at("XN", 184, [P, 2, D])
    ADA2 = at("ADA2", 180, [P, 2, 4, HALF])
    ACTS = at("ACTS", 96, [P, 4, 2, SEQ], F32R)
    WGU = at("WGU", 128, [P, 2, 2, 2, KT, P], F32R)
    WGUraw = at("WGUraw", 128, [P, 2, 2, 2, KT, P])
    WD = at("WD", 160, [P, 2, 2, D], F32R)
    WDraw = at("WDraw", 168, [P, 2, D])
    WD2 = at("WD2", 128, [P, 2, 2, D], F32R)
    WD2raw = at("WD2raw", 136, [P, 2, D])
    HID = at("HID", 176, [P, 2, HALF])
    IDENT = at("IDENT", 196, [P, P])
    ONES = at("ONES", 196.5, [P, P])
    MASKQ = at("MASKQ", 197, [P, P], BF16)
    MASKK = at("MASKK", 197.25, [P, P], BF16)
    o = 197.5

    def small(name, n, dt=F32):
        nonlocal o
        t = at(name, o, [P, n], dt)
        o += (4 * n + 31) // 32 * 32 / KB
        return t

    COLS = small("COLS", N_ROWS)
    MOD = small("MOD", 32)
    G1 = small("G1", KT)
    G2 = small("G2", KT)
    CT = small("CT", KT)
    CS = small("CS", KT)
    POSI = small("POSI", NT, I32)
    POSF = small("POSF", NT)
    FREQ = small("FREQ", RH)
    INV = small("INV", 16)
    SS = small("SS", 16)
    VAR = small("VAR", 16)
    RS = small("RS", 16)
    RT = small("RT", 16)
    RI = small("RI", 16, I32)
    NEGM = small("NEGM", 32)
    SUM = small("SUM", 32)
    RSUM = small("RSUM", 32)
    SS2 = small("SS2", NT)
    RS2 = small("RS2", NT)
    SS3 = small("SS3", NT)
    RS3 = small("RS3", NT)
    assert o <= 199.8
    GT1 = at("GT1", 199.8125, [P, D])
    GT2 = at("GT2", 203.8125, [P, D])

    PS = enter(nc.psum_tensor("PS", [P, 8, HALF], F32))

    names = """c_in rows_in pos_in freq_in gq_in gkv_in gt_in wp_in wuv_in wuq_in wuk_in gfin_in out_done
        pool_const  act_silu ang_ready sin_ready dve_step pool_step
        ss1 rs1 xn1 t1 ev1 gt_zero acc_done sh1_sum colsum modcols gt_ready rowsT
        hmod h_hi h_ready wtm_hi wtm_ready tm_done tm_out tm_norm kr_ready ckv_hi ckv_ready
        wu_hi wu_ready u_done u_out windowed pooled lt_T lt_hi lt_lo pool_hi pool_lo wp_hi wp_ready pm_done pm_y pm_hi pm_lo
        wuq_hi wuq_ready wukT wuk_hi wuk_ready wuv_hi wuv_ready
        qr_done qr_raw qr_rot qr_dup qr_T qr_hi qr_lo qn_done qn_hi qn_lo ql_done ql_hi ql_lo
        s_done negmax exp_done p_norm p_T pt_hi pt_lo pv_done ol_hi ol_lo op_done y_hi y_lo
        wo_hi wo_hi_odd wo_ready mix_done mix_gated x_new ss2 rs2 xn2 t2 ev2 h2_hi h2_ready
        wgu_hi wgu_ready wd_fold wd_hi wd_ready gu_half silu hid act_hi act_ready
        d_bank d_free ss3 rs3 fin""".split()
    S = {n: sem(n) for n in names}
    x_in = [sem(f"x_in{t}") for t in range(NT)]
    sc1_in = [sem(f"sc1_in{i}") for i in range(4)]
    sh1_in = [sem(f"sh1_in{i}") for i in range(2)]
    ada_in = [sem(f"ada_in{i}") for i in range(2)]
    wtm_in = [sem(f"wtm_in{i}") for i in range(4)]
    wu_in = [sem(f"wu_in{i}") for i in range(2)]
    wo_in = [sem(f"wo_in{i}") for i in range(4)]
    wgu_in = [sem(f"wgu_in{i}") for i in range(2)]
    wd_in = sem("wd_in")

    x_d = x.rearrange("b (t p) d -> (b t) p d", p=P)
    out_d = out.rearrange("b (t p) d -> (b t) p d", p=P)
    ada_d = w_ada.rearrange("l (p t) n -> p (l t) n", t=KT)
    win_d = w_in.rearrange("l (k p) n -> p (l k) n", p=P)
    gate_d = w_gate.rearrange("l (k p) n -> p (l k) n", p=P)
    up_d = w_up.rearrange("l (k p) n -> p (l k) n", p=P)
    down_d = w_down.rearrange("l (f p) n -> p (l f) n", p=P)
    wo_d = w_o.rearrange("l (k p) n -> p (l k) n", p=P)
    wuq_d = w_uq.rearrange("l (k p) h d -> p (l k) h d", p=P)

    DVE_CHUNKS = (2, 3, 4, 5, 6, 7, 8, 9, 10, 11)
    N_PIECES = 2 * len(DVE_CHUNKS)

    def ada_piece(j):
        if j < 4:
            return ADA0[:, j], sc1_in[j], 16
        ring = ADA1 if j < 8 else ADA2
        return ring[:, j % 2], ada_in[j % 2], 16 * ((j - 4) // 2 + 1)

    def ada_source(ch, kh):
        return ada_d[:, 4 * kh:4 * kh + 4, ch * HALF:(ch + 1) * HALF]

    def flat(ap):
        return ap.rearrange("p a b -> p (a b)")

    def tok(t):
        return slice(t * P, (t + 1) * P)

    def half(i):
        return slice(i * HALF, (i + 1) * HALF)

    BLOCKS = list(range(NT - 1, -1, -1))
    GORDER = list(range(GROUPS - 1, -1, -1))


    block = enter(nc.Block())

    @block.sync
    def _(sp):
        def load_ada(j):
            buf, s, _ = ada_piece(j)
            if j == 4:
                sp.wait_ge(S["sh1_sum"], 1)
            elif j == 8:
                sp.wait_ge(S["op_done"], NT)
            elif j == 16:
                sp.wait_ge(S["t2"], NT)
            if j >= 4:
                sp.wait_ge(S["acc_done"], j - 1)
            sp.dma_start(buf, ada_source(DVE_CHUNKS[j // 2], j % 2)).then_inc(s, 16)

        sp.dma_start(CT[:], c.rearrange("b (p t) -> p (b t)", t=KT)).then_inc(S["c_in"], 16)
        load_ada(0)
        for t in range(4):
            sp.dma_start(X[:, t, :], x_d[t]).then_inc(x_in[t], 16)
        load_ada(1)
        for t in range(4, NT):
            sp.dma_start(X[:, t, :], x_d[t]).then_inc(x_in[t], 16)
        for src, r, n in ((b_ada, 0, 48), (g_mix, ROW_MIX, 8), (g_ffn, ROW_FFN, 8), (pool_scale, ROW_POOL, 4)):
            sp.dma_start(ROWS[r:r + n, :], src.rearrange("l (r n) -> (l r) n", n=P)).then_inc(S["rows_in"], 16)
        load_ada(2)
        load_ada(3)
        for ch in range(2):
            for kh in range(2):
                sp.dma_start(ADAS[:, 2 * ch + kh], ada_source(ch, kh)).then_inc(sh1_in[ch], 16)
        for i in range(4):
            sp.dma_start(WTMraw[:, 2 * i:2 * i + 2, :], win_d[:, 2 * i:2 * i + 2, 0:TM]).then_inc(wtm_in[i], 16)
        sp.dma_start(POSI[:], positions.rearrange("b (t p) -> p (b t)", p=P), allow_slow_non_contiguous=True).then_inc(S["pos_in"], 16)
        sp.dma_start(FREQ[:], freqs.partition_broadcast(P)).then_inc(S["freq_in"], 16)
        sp.dma_start(GQ[:], g_q.rearrange("l n -> (l n)").partition_broadcast(P)).then_inc(S["gq_in"], 16)
        sp.dma_start(GKV[:], g_kv.rearrange("l n -> (l n)").partition_broadcast(P)).then_inc(S["gkv_in"], 16)
        sp.wait_ge(S["gt_zero"], 1)
        sp.dma_start(GT1[0:1, :], b_ada[:, 2 * D:3 * D]).then_inc(S["gt_in"], 16)
        sp.dma_start(GT2[0:1, :], b_ada[:, 5 * D:6 * D]).then_inc(S["gt_in"], 16)

        def load_wu(i):
            g = GORDER[i]
            sp.dma_start(WUraw[:, i % 2, LO], win_d[:, :, TM + g * P:TM + (g + 1) * P]).then_inc(wu_in[i % 2], 16)

        sp.wait_ge(S["sh1_sum"], 1)
        load_wu(0)
        load_wu(1)
        sp.wait_ge(S["t1"], NT)
        sp.dma_start(WPraw[:], w_pool.rearrange("l g c d -> c (l g) d")).then_inc(S["wp_in"], 16)
        for j in range(4, 8):
            load_ada(j)
        sp.wait_ge(S["tm_done"], NT)
        sp.dma_start(WUVraw[:], w_uv.rearrange("l c h v -> c (l h) v")).then_inc(S["wuv_in"], 16)
        sp.wait_ge(S["acc_done"], 8)
        sp.dma_start(WUQraw[:], wuq_d).then_inc(S["wuq_in"], 16)
        sp.dma_start(WUKraw[:], w_uk.rearrange("l c h d -> c (l h) d")).then_inc(S["wuk_in"], 16)
        for i in (2, 3):
            sp.wait_ge(S["u_done"], 2 * (i - 1))
            load_wu(i)
        sp.wait_ge(S["ql_done"], 8)
        for i in range(4):
            sp.dma_start(WOraw[0][:, 2 * i:2 * i + 2, :], wo_d[:, 2 * i:2 * i + 2, half(0)]).then_inc(wo_in[i], 16)
        sp.wait_ge(S["pv_done"], NT)
        for t in range(4):
            sp.dma_start(X[:, t, :], x_d[t]).then_inc(x_in[t], 16)
        load_ada(8)
        load_ada(9)
        sp.wait_ge(S["wo_ready"], KT)
        for i in range(4):
            sp.dma_start(WOraw[1][:, 2 * i:2 * i + 2, :], wo_d[:, 2 * i:2 * i + 2, half(1)]).then_inc(wo_in[i], 16)
        for t in range(4, NT):
            sp.dma_start(X[:, t, :], x_d[t]).then_inc(x_in[t], 16)
        for j in range(10, 16):
            load_ada(j)

        def load_wgu(f, s):
            sp.dma_start(WGUraw[:, s, LO, 0], gate_d[:, :, bass.ds(f * P, P)]).then_inc(wgu_in[s], 16)
            sp.dma_start(WGUraw[:, s, LO, 1], up_d[:, :, bass.ds(f * P, P)]).then_inc(wgu_in[s], 16)

        def load_wd(i, buf=WDraw):
            sp.dma_start(buf[:], down_d[:, bass.ds(2 * i, 2), :]).then_inc(wd_in, 16)

        sp.wait_ge(S["mix_done"], NT)
        load_wgu(0, 0)
        load_wgu(1, 1)
        sp.wait_ge(S["colsum"], 8)
        load_wd(0)
        sp.wait_ge(S["x_new"], 2 * NT)
        sp.dma_start(GT1[:], g_final.partition_broadcast(P)).then_inc(S["gfin_in"], 16)

        def chunk_loads(i):
            for s in range(2):
                sp.wait_ge(S["gu_half"], 4 * i + 2 * s + 2)
                load_wgu(2 * i + 2 + s, s)
            if not isinstance(i, int) or i > 0:
                sp.wait_ge(S["d_bank"], 16 * i)
                load_wd(i)

        for j in range(16, N_PIECES):
            load_ada(j)
        chunk_loads(0)
        with sp.Fori(0, (NC - 3) // 2) as j:
            for par in (1, 0):
                chunk_loads(2 * j + (1 if par else 2))
        chunk_loads(NC - 2)
        sp.wait_ge(S["gu_half"], 4 * (NC - 1) + 2)
        sp.wait_ge(S["wd_fold"], NC - 1)
        load_wd(NC - 1, WD2raw)
        for t in range(NT):
            sp.wait_ge(S["fin"], t + 1)
            sp.dma_start(out_d[t], X[:, t, :]).then_inc(S["out_done"], 16)
        sp.wait_ge(S["out_done"], 16 * NT)

    @block.gpsimd
    def _(pool):
        n = 0

        def then(ins):
            nonlocal n
            n += 1
            ins.then_inc(S["pool_step"], 1)
            pool.wait_ge(S["pool_step"], n)

        then(pool.memset(IDENT[:], 0.0))
        then(pool.affine_select(out=IDENT[:], in_=IDENT[:], compare_op=ALU.not_equal, fill=1.0, base=0,
                                pattern=[[-1, P]], channel_multiplier=1))
        then(pool.memset(MASKQ[:], 0.0))
        then(pool.memset(MASKK[:], 0.0))
        then(pool.memset(MASKQ[0:1, 0:CHUNK], 1.0))
        then(pool.memset(MASKK[0:1, CHUNK:P], MASKED))
        for t in range(PADW):
            pool.memset(INV[:, t:t + 1], 1.0 / (t + 1))
        pool.memset(ONES[:], 1.0).then_inc(S["pool_const"], 1)
        pool.memset(GT1[:], 0.0)
        pool.memset(GT2[:], 0.0).then_inc(S["gt_zero"], 1)

        for i in range(4):
            pool.wait_ge(wtm_in[i], 16)
            pool.tensor_scalar(flat(WTM[:, HI, 2 * i:2 * i + 2, :]), flat(WTMraw[:, 2 * i:2 * i + 2, :]),
                               1.0, 0.0, ALU.mult, ALU.add).then_inc(S["wtm_hi"], 1)
        for m in range(2 * KT):
            hf, k = divmod(m, KT)
            pool.wait_ge(S["hmod"], m + 1)
            pool.tensor_scalar(HT[:, HI, k, half(hf)], HTf[:, k, half(hf)], 1.0, 0.0, ALU.mult, ALU.add).then_inc(S["h_hi"], 1)

        def wu_hi(g):
            pool.wait_ge(wu_in[g % 2], 16 * (g // 2 + 1))
            pool.tensor_scalar(flat(WU[:, g % 2, HI]), flat(WUraw[:, g % 2, LO]), 1.0, 0.0, ALU.mult, ALU.add).then_inc(S["wu_hi"], 1)

        wu_hi(0)
        wu_hi(1)
        pool.wait_ge(S["tm_norm"], NT)
        pool.memset(U[:, :, 0:PADW], 0.0)
        pool.tensor_scalar(CKV[:, HI], TMO[:, :, QR:QR + LAT], 1.0, 0.0, ALU.mult, ALU.add).then_inc(S["ckv_hi"], 1)
        keys = TMO[:, :, QR + LAT:TM].rearrange("p t (a d) -> p t a d", a=2)
        for table, trig in ((0, COS), (1, SIN)):
            for a in range(2):
                ins = pool.tensor_tensor(ropeK[:, table, :, a], keys[:, :, a], trig[:], ALU.mult)
        then(ins)
        both = TMO[:, :, QR + LAT:TMW].rearrange("p t (c a d) -> p t c a d", c=2, a=2)

        def twice(ap):
            return ap.rearrange("p t (o d) -> p t o d", o=1).broadcast_to([P, NT, 2, RH])

        pool.tensor_tensor(both[:, :, :, 0], twice(ropeK[:, 0, :, 0]), twice(ropeK[:, 1, :, 1]), ALU.subtract)
        then(pool.tensor_tensor(both[:, :, :, 1], twice(ropeK[:, 1, :, 0]), twice(ropeK[:, 0, :, 1]), ALU.add))
        pool.memset(WIN[:, :, 0:PADW], 0.0).then_inc(S["kr_ready"], 1)

        pool.wait_ge(S["wp_in"], 16)
        pool.tensor_scalar(flat(WP[:, HI]), flat(WPraw[:]), 1.0, 0.0, ALU.mult, ALU.add).then_inc(S["wp_hi"], 1)
        pool.wait_ge(S["wuv_in"], 16)
        pool.tensor_scalar(flat(WUV[:, HI]), flat(WUVraw[:]), 1.0, 0.0, ALU.mult, ALU.add).then_inc(S["wuv_hi"], 1)
        for i, g in enumerate(GORDER):
            pool.wait_ge(S["u_out"], 2 * (i + 1))
            if i < 2:
                wu_hi(i + 2)
            u = U[:, g]
            src, dst = u, WIN[:, 0]
            for s in range(g + 1):
                then(pool.tensor_tensor(dst[:, PADW:], src[:, PADW:], src[:, PADW - 2 ** s:PADW + SEQ - 2 ** s], ALU.add))
                src, dst = dst, WIN[:, (s + 1) % 2]
            w = 2 ** (g + 1)
            then(pool.tensor_tensor(src[:, PADW:PADW + w], src[:, PADW:PADW + w], INV[:, 0:w], ALU.mult))
            pool.tensor_scalar(src[:, PADW:PADW + w], src[:, PADW:PADW + w], float(w), 0.0, ALU.mult, ALU.add).then_inc(S["windowed"], 1)
            pool.wait_ge(S["pooled"], i + 1)
            if i == 1:
                pool.wait_ge(S["wuq_in"], 16)
                pool.tensor_scalar(WUQ[:, HI].rearrange("p k h d -> p (k h d)"), WUQraw[:].rearrange("p k h d -> p (k h d)"),
                                   1.0, 0.0, ALU.mult, ALU.add).then_inc(S["wuq_hi"], 1)

        def rotate(i, t):
            pool.wait_ge(S["qr_raw"], i + 1)
            if i >= 2:
                pool.wait_ge(S["qr_T"], i - 1)
            q = QRAW[:, t].rearrange("p h (a d) -> p h a d", a=2)
            for table, trig in ((0, COS), (1, SIN)):
                wide = trig[:, t:t + 1, :].rearrange("p (o a) d -> p o a d", o=1).broadcast_to([P, HEADS, 2, RH])
                ins = pool.tensor_tensor(ropeQ[:, table], q, wide, ALU.mult)
            then(ins)

            pool.tensor_tensor(QRD[:, i % 2, :, 0, 0:RH], ropeQ[:, 0, :, 0], ropeQ[:, 1, :, 1], ALU.subtract)
            pool.tensor_tensor(QRD[:, i % 2, :, 0, RH:ROPE], ropeQ[:, 1, :, 0], ropeQ[:, 0, :, 1],
                               ALU.add).then_inc(S["qr_rot"], 1)
            pool.wait_ge(S["qr_rot"], i + 1)

        pm = 0

        def pm_hi():
            nonlocal pm
            g, hf = GORDER[pm // 2], pm % 2
            pm += 1
            pool.wait_ge(S["pm_y"], pm)
            pool.tensor_scalar(HT[:, HI, 4 + g, half(hf)], HTf[:, 4 + g, half(hf)], 1.0, 0.0, ALU.mult, ALU.add).then_inc(S["pm_hi"], 1)

        for i, t in enumerate(BLOCKS):
            pm_hi()
            rotate(i, t)

        pool.wait_ge(S["s_done"], 4 * NT)
        for i in range(4):
            pool.wait_ge(wo_in[i], 16)
            pool.tensor_scalar(WOhi[0][:, 2 * i, :], WOraw[0][:, 2 * i, :], 1.0, 0.0, ALU.mult, ALU.add).then_inc(S["wo_hi"], 1)

        def x_add(m, c_, t):
            pool.wait_ge(S["mix_gated"], m + 1)
            if c_ == 0:
                pool.wait_ge(x_in[t], 32)
            pool.tensor_tensor(X[:, t, half(c_)], X[:, t, half(c_)], MIX[:, m % 2], ALU.add).then_inc(S["x_new"], 1)

        for t in range(NT):
            x_add(t, 0, t)
            if t == 1:
                pool.wait_ge(S["op_done"], NT)
            if t >= 1 and t % 2 == 1:
                i = t // 2
                pool.wait_ge(wo_in[i], 32)
                pool.tensor_scalar(WOhi[1][:, 2 * i, :], WOraw[1][:, 2 * i, :], 1.0, 0.0, ALU.mult, ALU.add).then_inc(S["wo_hi"], 1)

        def h2_hi(t):
            pool.wait_ge(S["ev2"], t + 1)
            pool.tensor_scalar(HT[:, HI, :, tok(t)], HTf[:, :, tok(t)], 1.0, 0.0, ALU.mult, ALU.add).then_inc(S["h2_hi"], 1)

        def wd_fold(i, buf=WDraw):
            pool.wait_ge(wd_in, 16 * i + 16)
            for r in range(2):
                ins = pool.tensor_tensor(buf[:, r], buf[:, r], GT2[:], ALU.mult)
            ins.then_inc(S["wd_fold"], 1)

        for t in range(NT):
            x_add(NT + t, 1, t)
            if t >= 2:
                h2_hi(t - 2)
        h2_hi(NT - 2)
        h2_hi(NT - 1)
        pool.wait_ge(S["gt_ready"], 4)
        wd_fold(0)
        wd_fold(1)
        with pool.Fori(2, NC - 1) as i:
            wd_fold(i)
        wd_fold(NC - 1, WD2raw)

    @block.scalar
    def _(act):
        act.wait_ge(S["c_in"], 16)
        act.activation(CS[:], CT[:], ACT.Silu).then_inc(S["act_silu"], 1)
        for t in range(NT):
            act.wait_ge(x_in[t], 16)
            act.activation(JUNK[:], X[:, t, :], ACT.Square, accum_out=SS[:, t:t + 1]).then_inc(S["ss1"], 1)
            act.wait_ge(S["ss1"], t + 1)
        for m in range(2 * NT):
            t, kk = divmod(m, 2)
            act.wait_ge(S["t1"], t + 1)
            act.activation(HTf[:, 4 * kk:4 * kk + 4, tok(t)],
                           PS[:, m % 4, :].rearrange("p (k n) -> p k n", k=4), ACT.Copy).then_inc(S["ev1"], 1)
        act.wait_ge(S["modcols"], 1)
        act.wait_ge(S["ev1"], 2 * NT)
        for m in range(2 * KT):
            hf, k = divmod(m, KT)
            act.activation(HTf[:, k, half(hf)], HTf[:, k, half(hf)], ACT.Identity,
                           scale=G1[:, k:k + 1], bias=MOD[:, k:k + 1]).then_inc(S["hmod"], 1)
        act.wait_ge(S["ang_ready"], 1)
        act.activation(SHALF[:], ANG[:], ACT.Sin, scale=0.5)
        act.activation(SQUART[:], ANG[:], ACT.Sin, scale=0.25).then_inc(S["sin_ready"], 1)
        for t in range(NT):
            act.wait_ge(S["tm_done"], t + 1)
            b = 4 + t % 2
            act.activation(TMO[:, t, 0:TM], PS[:, b, 0:TM], ACT.Copy)
            act.activation(JUNK2[:, 0:QR], PS[:, b, 0:QR], ACT.Square, accum_out=SS[:, t:t + 1])
            act.activation(JUNK2[:, QR:QR + LAT], PS[:, b, QR:QR + LAT], ACT.Square,
                           accum_out=SS[:, 8 + t:9 + t]).then_inc(S["tm_out"], 1)
            act.wait_ge(S["tm_out"], t + 1)

        def u_out(i):
            g = GORDER[i]
            for hf in range(2):
                act.wait_ge(S["u_done"], 2 * i + hf + 1)
                act.activation(U[:, g, PADW + hf * HALF:PADW + (hf + 1) * HALF], PS[:, hf, :], ACT.Copy).then_inc(S["u_out"], 1)

        def lt_hi(t):
            act.wait_ge(S["lt_T"], t + 1)
            b = 2 + t % 2
            act.activation(LT[:, :, HI, tok(t)], PS[:, b, 0:3 * P].rearrange("p (k n) -> p k n", k=3), ACT.Copy)
            act.activation(KRT[:, HI, tok(t)], PS[:, b, 3 * P:], ACT.Copy).then_inc(S["lt_hi"], 1)

        def pooled_hi(i):
            g = GORDER[i]
            act.wait_ge(S["pooled"], i + 1)
            act.wait_ge(S["u_done"], 2 * GROUPS)
            act.activation(POOLHI[:, g], U[:, g, PADW:], ACT.Copy).then_inc(S["pool_hi"], 1)

        u_out(0)
        u_out(1)
        for t in range(4):
            lt_hi(t)
        u_out(2)
        for t in range(4, NT):
            lt_hi(t)
        act.wait_ge(S["wukT"], 1)
        act.activation(WUK[:, HI].rearrange("p h c -> p (h c)"), PS[:, 4, :], ACT.Copy).then_inc(S["wuk_hi"], 1)
        u_out(3)
        for i, t in enumerate(BLOCKS):
            act.wait_ge(S["qr_done"], i + 1)
            act.activation(QRAW[:, t].rearrange("p h d -> p (h d)"), PS[:, 2 + i % 2, 0:HEADS * ROPE], ACT.Copy).then_inc(S["qr_raw"], 1)
        for i in range(GROUPS):
            pooled_hi(i)

        def pm_y(m):
            g, hf = GORDER[m // 2], m % 2
            act.wait_ge(S["pm_done"], m + 1)
            act.activation(HTf[:, 4 + g, half(hf)], PS[:, m % 2, :], ACT.Copy,
                           scale=COLS[:, ROW_POOL + g:ROW_POOL + g + 1]).then_inc(S["pm_y"], 1)

        def ql_hi(i):
            hf, h = 1 - i // 4, i % 4
            act.wait_ge(S["ql_done"], i + 1)
            act.activation(QLhi[:, h, half(hf)], PS[:, 6 + i % 2, :], ACT.Copy).then_inc(S["ql_hi"], 1)

        def qr_twice(i):
            act.wait_ge(S["qr_rot"], i + 1)
            act.activation(QRD[:, i % 2, :, 1], QRD[:, i % 2, :, 0], ACT.Copy).then_inc(S["qr_dup"], 1)

        for m in range(8):
            pm_y(m)
            if m in (3, 5):
                qr_twice((m - 3) // 2)
        for i, t in enumerate(BLOCKS):
            act.wait_ge(S["qn_done"], i + 1)
            if i >= 2:
                act.wait_ge(S["ql_done"], i - 1)
            act.activation(QN[:, i % 2, HI], PS[:, 4 + i % 2, :], ACT.Copy).then_inc(S["qn_hi"], 1)
            if i >= 1:
                ql_hi(i - 1)
            act.wait_ge(S["qr_T"], i + 1)
            act.activation(QS[:, :, tok(t)], PS[:, 2 + i % 2, :].rearrange("p (h n) -> p h n", h=HEADS), ACT.Copy).then_inc(S["qr_hi"], 1)
            if i < NT - 2:
                qr_twice(i + 2)
        ql_hi(7)

        def softmax_exp(n_, b, h):
            m = 4 * n_ + h
            act.wait_ge(S["negmax"], m + 1)
            if n_ >= 1:
                act.wait_ge(S["p_T"], m - 3)
            sl = 2 * (h % 2)
            act.activation(PR[:, h, 0:(b + 1) * P], flat(PS[:, sl:sl + 2, :])[:, 0:(b + 1) * P], ACT.Exp,
                           scale=SCALE, bias=NEGM[:, m:m + 1], accum_out=SUM[:, m:m + 1]).then_inc(S["exp_done"], 1)

        def turned_hi(n_, h):
            b = BLOCKS[n_]
            act.wait_ge(S["p_T"], 4 * n_ + h + 1)
            if h == 0 and n_ >= 1:
                act.wait_ge(S["pv_done"], n_)
            for j0 in range(0, b + 1, 4):
                nj = min(4, b + 1 - j0)
                last = act.activation(PT[:, HI, j0:j0 + nj, h, :],
                                      PS[:, 4 + j0 // 4, 0:nj * P].rearrange("p (j n) -> p j n", j=nj), ACT.Copy)
            last.then_inc(S["pt_hi"], 1)

        def latent_hi(n_):
            act.wait_ge(S["pv_done"], n_ + 1)
            if n_ >= 1:
                act.wait_ge(S["op_done"], n_)
            act.activation(OL[:, HI], PS[:, 6, :], ACT.Copy).then_inc(S["ol_hi"], 1)

        def out_hi(n_):
            act.wait_ge(S["op_done"], n_ + 1)
            act.activation(HT[:, HI, 0:HEADS, tok(BLOCKS[n_])], PS[:, 7, :].rearrange("p (h n) -> p h n", h=HEADS),
                           ACT.Copy).then_inc(S["y_hi"], 1)

        for n_, b in enumerate(BLOCKS):
            if n_ >= 2:
                out_hi(n_ - 2)
            for h in range(HEADS):
                if n_ >= 1:
                    turned_hi(n_ - 1, h)
                softmax_exp(n_, b, h)
            if n_ >= 1:
                latent_hi(n_ - 1)
        out_hi(NT - 2)
        for h in range(HEADS):
            turned_hi(NT - 1, h)
        latent_hi(NT - 1)

        for i in range(4):
            act.wait_ge(wo_in[i], 16)
            act.activation(WOhi[0][:, 2 * i + 1, :], WOraw[0][:, 2 * i + 1, :], ACT.Copy).then_inc(S["wo_hi_odd"], 1)
        out_hi(NT - 1)
        act.wait_ge(S["op_done"], NT)
        for i in range(4):
            act.wait_ge(wo_in[i], 32)
            act.activation(WOhi[1][:, 2 * i + 1, :], WOraw[1][:, 2 * i + 1, :], ACT.Copy).then_inc(S["wo_hi_odd"], 1)

        def squares2(t):
            act.wait_ge(S["x_new"], NT + t + 1)
            if t == 0:
                act.wait_ge(S["acc_done"], 16)
            act.activation(JUNK2[:], X[:, t, :], ACT.Square, accum_out=SS2[:, t:t + 1]).then_inc(S["ss2"], 1)
            act.wait_ge(S["ss2"], t + 1)

        def modulate2(t):
            act.wait_ge(S["t2"], t + 1)
            act.wait_ge(S["modcols"], 2)
            for k in range(KT):
                bank = 4 + 2 * (t % 2) + k // 4
                last = act.activation(HTf[:, k, tok(t)], PS[:, bank, (k % 4) * P:(k % 4 + 1) * P], ACT.Identity,
                                      scale=G2[:, k:k + 1], bias=MOD[:, 16 + k:17 + k])
            last.then_inc(S["ev2"], 1)

        def wgu_hi(i, s):
            act.wait_ge(wgu_in[s], 32 * i + 32)
            act.activation(WGU[:, s, HI].rearrange("p a k n -> p (a k n)"),
                           WGUraw[:, s, LO].rearrange("p a k n -> p (a k n)"), ACT.Copy).then_inc(S["wgu_hi"], 1)

        def wd_hi(i, rows=WD, raw=WDraw):
            act.wait_ge(S["wd_fold"], i + 1)
            act.activation(flat(rows[:, HI]), flat(raw[:]), ACT.Copy).then_inc(S["wd_hi"], 1)

        for t in range(NT):
            squares2(t)
            if t >= 2:
                modulate2(t - 2)
            if t == 4:
                wgu_hi(0, 0)
        modulate2(NT - 2)
        modulate2(NT - 1)
        wgu_hi(0, 1)

        def chunk_act(i, par, more=True):
            first = isinstance(i, int) and i == 0
            if not first:
                wgu_hi(i, 1)
            for s in range(2):
                for hf in range(2):
                    m = 4 * i + 2 * s + hf
                    act.wait_ge(S["gu_half"], m + 1)
                    if not isinstance(m, int) or m >= 2:
                        act.wait_ge(S["act_ready"], m - 1)
                    act.activation(HID[:, hf], PS[:, 2 * hf, :], ACT.Silu).then_inc(S["silu"], 1)
                    act.wait_ge(S["hid"], m + 1)
                    act.activation(ACTS[:, 2 * par + s, HI, half(hf)], HID[:, hf], ACT.Copy).then_inc(S["act_hi"], 1)
                    if s == 1 and hf == 0 and not first:
                        wd_hi(i - 1)
                if s == 0 and more:
                    wgu_hi(i + 1, 0)

        chunk_act(0, 0)
        with act.Fori(0, (NC - 3) // 2) as j:
            for par in (1, 0):
                chunk_act(2 * j + (1 if par else 2), par)
        chunk_act(NC - 2, (NC - 2) % 2)
        chunk_act(NC - 1, (NC - 1) % 2, more=False)
        wd_hi(NC - 1, WD2, WD2raw)
        for t in range(NT):
            act.wait_ge(S["d_free"], 4 + 16 * (NC - 1) + 2 * t + 2)
            act.activation(JUNK2[:], X[:, t, :], ACT.Square, accum_out=SS3[:, t:t + 1]).then_inc(S["ss3"], 1)
            act.wait_ge(S["ss3"], t + 1)

    @block.vector
    def _(dve):
        n = 0

        def then(ins):
            nonlocal n
            n += 1
            ins.then_inc(S["dve_step"], 1)
            dve.wait_ge(S["dve_step"], n)

        def inverse_root(res, ss, cols, width, done):
            v, r, rt, ri = VAR[:, 0:cols], RS[:, 0:cols], RT[:, 0:cols], RI[:, 0:cols]
            if res is not None:
                r = res
            then(dve.tensor_scalar(v, ss, 1.0 / width, EPS, ALU.mult, ALU.add))
            then(dve.tensor_scalar(ri, v.bitcast(I32), 1, None, ALU.logical_shift_right))
            then(dve.tensor_scalar(r.bitcast(I32), ri, -1.0, RSQRT_MAGIC, ALU.mult, ALU.add))
            for step in range(3):
                then(dve.tensor_tensor(rt, r, r, ALU.mult))
                then(dve.scalar_tensor_tensor(rt, rt, -0.5, v, ALU.mult, ALU.mult))
                ins = dve.scalar_tensor_tensor(r, rt, 1.5, r, ALU.add, ALU.mult)
                if step < 2:
                    then(ins)
            ins.then_inc(done, 1)

        def accumulate(j):
            buf, s, v = ada_piece(j)
            o_, kh = divmod(j, 2)
            ch = DVE_CHUNKS[o_]
            dve.wait_ge(s, v)
            gate_sum = ch in (4, 5, 10, 11)
            if gate_sum:
                dve.wait_ge(S["gt_in"], 32)
                acc = (GT1 if ch < 6 else GT2)[:, half(ch % 2)]
            else:
                acc = ACC[:, ch % 2]
                if kh == 0 and o_ >= 2:
                    dve.wait_ge(S["colsum"], o_ - 1)
            for t in range(4):
                cs = CS[:, 4 * kh + t:4 * kh + t + 1]
                if not gate_sum and kh == 0 and t == 0:
                    ins = dve.tensor_scalar(acc, buf[:, t, :], cs, None, ALU.mult)
                else:
                    ins = dve.scalar_tensor_tensor(acc, buf[:, t, :], cs, acc, ALU.mult, ALU.add)
                if t < 3:
                    then(ins)
            ins.then_inc(S["acc_done"], 1)
            dve.wait_ge(S["acc_done"], j + 1)

        def xn1(t):
            dve.tensor_scalar(X[:, t, :], X[:, t, :], RS[:, t:t + 1], None, ALU.mult).then_inc(S["xn1"], 1)

        dve.wait_ge(S["act_silu"], 1)
        accumulate(0)
        for b in range(2):
            dve.wait_ge(S["ss1"], 4 * b + 4)
            inverse_root(RS[:, 4 * b:4 * b + 4], SS[:, 4 * b:4 * b + 4], 4, D, S["rs1"])
            dve.wait_ge(S["rs1"], b + 1)
            for t in range(4 * b, 4 * b + 4):
                xn1(t)
            accumulate(b + 1)
        accumulate(3)
        dve.wait_ge(S["rowsT"], 1)
        then(dve.tensor_copy(COLS[:], PS[:, 6, 0:N_ROWS]))
        dve.wait_ge(S["colsum"], 2)
        dve.wait_ge(S["sh1_sum"], 1)
        then(dve.tensor_tensor(MOD[:, 0:16], PS[:, 7, 0:16], COLS[:, 0:16], ALU.add))
        dve.scalar_tensor_tensor(G1[:], MOD[:, 8:16], 1.0, COLS[:, ROW_MIX:ROW_MIX + 8], ALU.add, ALU.mult).then_inc(S["modcols"], 1)

        def lo(out_, full, hi, ready):
            dve.tensor_tensor(out_, full, hi.bitcast(F32), ALU.subtract).then_inc(ready, 1)

        for i in range(4):
            dve.wait_ge(S["wtm_hi"], i + 1)
            lo(flat(WTM[:, LO, 2 * i:2 * i + 2, :]), flat(WTMraw[:, 2 * i:2 * i + 2, :]),
               flat(WTM[:, HI, 2 * i:2 * i + 2, :]), S["wtm_ready"])
        for m in range(2 * KT):
            hf, k = divmod(m, KT)
            dve.wait_ge(S["h_hi"], m + 1)
            lo(HT[:, LO, k, half(hf)], HTf[:, k, half(hf)], HT[:, HI, k, half(hf)], S["h_ready"])

        def wu_lo(g):
            dve.wait_ge(S["wu_hi"], g + 1)
            lo(flat(WU[:, g % 2, LO]), flat(WUraw[:, g % 2, LO]), flat(WU[:, g % 2, HI]), S["wu_ready"])

        def gate(n_):
            dve.wait_ge(S["colsum"], (3, 4, 9, 10)[n_])
            gt = GT1 if n_ < 2 else GT2
            dve.tensor_copy(gt[:, half(n_ % 2)], PS[:, 6 + n_ % 2 if n_ < 2 else 4 + n_ % 2, :]).then_inc(S["gt_ready"], 1)

        dve.wait_ge(S["t1"], NT)
        dve.wait_ge(S["pos_in"], 16)
        dve.wait_ge(S["freq_in"], 16)
        then(dve.tensor_copy(POSF[:], POSI[:]))
        for t in range(NT):
            ins = dve.tensor_scalar(ANG[:, t, :], FREQ[:], POSF[:, t:t + 1], None, ALU.mult)
        then(ins)
        for turns in (4096.0, 1.0):
            then(dve.tensor_scalar(TURN[:], ANG[:], float(1 / (2 * np.pi * turns)), ROUND_MAGIC, ALU.mult, ALU.add))
            then(dve.tensor_scalar(TURN[:], TURN[:], -ROUND_MAGIC, None, ALU.add))
            for part in two_pi_parts():
                ins = dve.scalar_tensor_tensor(ANG[:], TURN[:], -part * turns, ANG[:], ALU.mult, ALU.add)
                then(ins)
        dve.sem_inc(S["ang_ready"], 1)

        accumulate(4)
        accumulate(5)
        wu_lo(0)
        wu_lo(1)
        dve.wait_ge(S["sin_ready"], 1)
        then(dve.tensor_tensor(COS[:], SHALF[:], SHALF[:], ALU.mult))
        then(dve.tensor_scalar(COS[:], COS[:], -2.0, 1.0, ALU.mult, ALU.add))
        then(dve.tensor_tensor(SIN[:], SQUART[:], SQUART[:], ALU.mult))
        then(dve.tensor_scalar(SIN[:], SIN[:], -4.0, 2.0, ALU.mult, ALU.add))
        then(dve.tensor_tensor(SIN[:], SIN[:], SHALF[:], ALU.mult))
        accumulate(6)
        accumulate(7)
        gate(0)
        gate(1)
        dve.wait_ge(S["tm_out"], NT)
        inverse_root(None, SS[:, 0:8], 8, QR, S["rs1"])
        dve.wait_ge(S["rs1"], 3)
        dve.wait_ge(S["gq_in"], 16)
        dve.wait_ge(S["gkv_in"], 16)
        for t in range(NT):
            ins = dve.scalar_tensor_tensor(TMO[:, t, 0:QR], TMO[:, t, 0:QR], RS[:, t:t + 1], GQ[:], ALU.mult, ALU.mult)
        then(ins)
        inverse_root(None, SS[:, 8:16], 8, LAT, S["rs1"])
        dve.wait_ge(S["rs1"], 4)
        for t in range(NT):
            dve.scalar_tensor_tensor(TMO[:, t, QR:QR + LAT], TMO[:, t, QR:QR + LAT], RS[:, t:t + 1], GKV[:],
                                     ALU.mult, ALU.mult).then_inc(S["tm_norm"], 1)
        dve.wait_ge(S["ckv_hi"], 1)
        lo(CKV[:, LO], TMO[:, :, QR:QR + LAT], CKV[:, HI], S["ckv_ready"])
        def lt_lo(t):
            dve.wait_ge(S["lt_hi"], t + 1)
            b = 2 + t % 2
            dve.tensor_tensor(LT[:, :, LO, tok(t)], PS[:, b, 0:3 * P].rearrange("p (k n) -> p k n", k=3),
                              LT[:, :, HI, tok(t)].bitcast(F32), ALU.subtract)
            lo(KRT[:, LO, tok(t)], PS[:, b, 3 * P:], KRT[:, HI, tok(t)], S["lt_lo"])

        def pooled(i):
            g = GORDER[i]
            dve.wait_ge(S["windowed"], i + 1)
            sums = WIN[:, (0, 1, 0, 1)[g], PADW:]
            dve.scalar_tensor_tensor(U[:, g, PADW:], sums, 1.0 / 2 ** (g + 1), U[:, g, PADW:],
                                     ALU.mult, ALU.subtract).then_inc(S["pooled"], 1)

        dve.wait_ge(S["wp_hi"], 1)
        lo(flat(WP[:, LO]), flat(WPraw[:]), flat(WP[:, HI]), S["wp_ready"])
        dve.wait_ge(S["wuv_hi"], 1)
        lo(flat(WUV[:, LO]), flat(WUVraw[:]), flat(WUV[:, HI]), S["wuv_ready"])
        wu_lo(2)
        for t in range(4):
            lt_lo(t)
        pooled(0)
        wu_lo(3)
        pooled(1)
        for t in range(4, NT):
            lt_lo(t)
        dve.wait_ge(S["wuq_hi"], 1)
        lo(WUQ[:, LO].rearrange("p k h d -> p (k h d)"), WUQraw[:].rearrange("p k h d -> p (k h d)"),
           WUQ[:, HI].rearrange("p k h d -> p (k h d)"), S["wuq_ready"])
        pooled(2)
        pooled(3)
        dve.wait_ge(S["wuk_hi"], 1)
        lo(WUK[:, LO].rearrange("p h c -> p (h c)"), PS[:, 4, :], WUK[:, HI].rearrange("p h c -> p (h c)"), S["wuk_ready"])
        for i, g in enumerate(GORDER):
            dve.wait_ge(S["pool_hi"], i + 1)
            lo(UR[:, g, PADW:], U[:, g, PADW:], POOLHI[:, g], S["pool_lo"])

        def pm_lo(m):
            g, hf = GORDER[m // 2], m % 2
            dve.wait_ge(S["pm_hi"], m + 1)
            lo(HT[:, LO, 4 + g, half(hf)], HTf[:, 4 + g, half(hf)], HT[:, HI, 4 + g, half(hf)], S["pm_lo"])

        def ql_lo(i):
            hf, h = 1 - i // 4, i % 4
            dve.wait_ge(S["ql_hi"], i + 1)
            lo(QLlo[:, h, half(hf)], PS[:, 6 + i % 2, :], QLhi[:, h, half(hf)], S["ql_lo"])

        for i, t in enumerate(BLOCKS):
            dve.wait_ge(S["qn_hi"], i + 1)
            lo(QN[:, i % 2, LO], PS[:, 4 + i % 2, :], QN[:, i % 2, HI], S["qn_lo"])
            if i >= 1:
                ql_lo(i - 1)
            pm_lo(i)
            dve.wait_ge(S["qr_hi"], i + 1)
            lo(QS[ROPE:P, :, tok(t)], PS[ROPE:P, 2 + i % 2, :].rearrange("p (h n) -> p h n", h=HEADS),
               QS[ROPE:P, :, tok(t)], S["qr_lo"])
        ql_lo(7)

        def row_max(n_, h):
            m = 4 * n_ + h
            dve.wait_ge(S["s_done"], m + 1)
            sl = 2 * (h % 2)
            then(dve.tensor_reduce(RSUM[:, m:m + 1], flat(PS[:, sl:sl + 2, :])[:, 0:(BLOCKS[n_] + 1) * P], AX.X, ALU.max))
            dve.tensor_scalar(NEGM[:, m:m + 1], RSUM[:, m:m + 1], -SCALE, None, ALU.mult).then_inc(S["negmax"], 1)

        def inv_sum(n_, h):
            m, b = 4 * n_ + h, BLOCKS[n_]
            dve.wait_ge(S["exp_done"], m + 1)
            then(dve.reciprocal(RSUM[:, m:m + 1], SUM[:, m:m + 1]))
            dve.tensor_scalar(PR[:, h, 0:(b + 1) * P], PR[:, h, 0:(b + 1) * P], RSUM[:, m:m + 1], None,
                              ALU.mult).then_inc(S["p_norm"], 1)

        def turned_lo(n_, h):
            b = BLOCKS[n_]
            dve.wait_ge(S["pt_hi"], 4 * n_ + h + 1)
            for j0 in range(0, b + 1, 4):
                nj = min(4, b + 1 - j0)
                ins = dve.tensor_tensor(PT[:, LO, j0:j0 + nj, h, :],
                                        PS[:, 4 + j0 // 4, 0:nj * P].rearrange("p (j n) -> p j n", j=nj),
                                        PT[:, HI, j0:j0 + nj, h, :].bitcast(F32), ALU.subtract)
            ins.then_inc(S["pt_lo"], 1)

        def latent_lo(n_):
            dve.wait_ge(S["ol_hi"], n_ + 1)
            lo(OL[:, LO], PS[:, 6, :], OL[:, HI], S["ol_lo"])

        def out_lo(n_):
            dve.wait_ge(S["y_hi"], n_ + 1)
            t = tok(BLOCKS[n_])
            lo(HT[:, LO, 0:HEADS, t], PS[:, 7, :].rearrange("p (h n) -> p h n", h=HEADS), HT[:, HI, 0:HEADS, t], S["y_lo"])

        for n_ in range(NT):
            row_max(n_, 0)
            if n_ >= 2:
                out_lo(n_ - 2)
            for h in range(HEADS):
                if n_ >= 1 and h < 3:
                    turned_lo(n_ - 1, h)
                if h == 2 and n_ >= 1:
                    turned_lo(n_ - 1, 3)
                if h < 3:
                    row_max(n_, h + 1)
                inv_sum(n_, h)
            if n_ >= 1:
                latent_lo(n_ - 1)
        out_lo(NT - 2)
        for h in range(HEADS):
            turned_lo(NT - 1, h)
        latent_lo(NT - 1)

        def wo_lo(c_, k):
            i, odd = divmod(k, 2)
            if odd:
                dve.wait_ge(S["wo_hi_odd"], 4 * c_ + i + 1)
            else:
                dve.wait_ge(S["wo_hi"], 4 * c_ + i + 1)
            lo(WOlo[c_][:, k, :], WOraw[c_][:, k, :], WOhi[c_][:, k, :], S["wo_ready"])

        for k in range(KT):
            wo_lo(0, k)
        out_lo(NT - 1)

        def gated(m, c_):
            dve.wait_ge(S["mix_done"], m + 1)
            if m >= 2:
                dve.wait_ge(S["x_new"], m - 1)
            dve.tensor_tensor(MIX[:, m % 2], PS[:, m % 4, :], GT1[:, half(c_)], ALU.mult).then_inc(S["mix_gated"], 1)

        for t in range(NT):
            gated(t, 0)
            accumulate(8 + t)
            if t in (2, 4, 6):
                for k in (t - 2, t - 1):
                    wo_lo(1, k)
        wo_lo(1, 6)
        wo_lo(1, 7)

        def wgu_lo(i, s):
            dve.wait_ge(S["wgu_hi"], 2 * i + s + 1)
            dve.tensor_tensor(WGU[:, s, LO].rearrange("p a k n -> p (a k n)"),
                              WGUraw[:, s, LO].rearrange("p a k n -> p (a k n)"),
                              WGU[:, s, HI].bitcast(F32).rearrange("p a k n -> p (a k n)"), ALU.subtract).then_inc(S["wgu_ready"], 1)

        def h2_lo(t):
            dve.wait_ge(S["h2_hi"], t + 1)
            lo(HT[:, LO, :, tok(t)], HTf[:, :, tok(t)], HT[:, HI, :, tok(t)], S["h2_ready"])

        def xn2(t):
            dve.wait_ge(S["ss2"], t + 1)
            inverse_root(RS2[:, t:t + 1], SS2[:, t:t + 1], 1, D, S["rs2"])
            dve.wait_ge(S["rs2"], t + 1)
            if t >= 2:
                dve.wait_ge(S["t2"], t - 1)
            dve.tensor_scalar(XN[:, t % 2], X[:, t, :], RS2[:, t:t + 1], None, ALU.mult).then_inc(S["xn2"], 1)

        for t in range(NT):
            gated(NT + t, 1)
            if t == 0:
                dve.wait_ge(S["colsum"], 8)
                then(dve.tensor_tensor(MOD[:, 16:32], PS[:, 7, 16:32], COLS[:, 24:40], ALU.add))
                dve.scalar_tensor_tensor(G2[:], MOD[:, 24:32], 1.0, COLS[:, ROW_FFN:ROW_FFN + 8],
                                         ALU.add, ALU.mult).then_inc(S["modcols"], 1)
            if t >= 1:
                xn2(t - 1)
            if t >= 2:
                h2_lo(t - 2)
            if t == 5:
                wgu_lo(0, 0)
        xn2(NT - 1)
        h2_lo(NT - 2)
        h2_lo(NT - 1)
        wgu_lo(0, 1)

        def hid(m, r):
            dve.wait_ge(S["silu"], m + 1)
            dve.tensor_tensor(HID[:, r], HID[:, r], PS[:, 2 * r + 1, :], ALU.mult).then_inc(S["hid"], 1)

        def act_lo(m, r, slot, hf):
            dve.wait_ge(S["act_hi"], m + 1)
            lo(ACTS[:, slot, LO, half(hf)], HID[:, r], ACTS[:, slot, HI, half(hf)], S["act_ready"])

        def wd_lo(i, rows=WD, raw=WDraw):
            dve.wait_ge(S["wd_hi"], i + 1)
            lo(flat(rows[:, LO]), flat(raw[:]), flat(rows[:, HI]), S["wd_ready"])

        def add_down(i):
            for m in range(2 * NT):
                t, c_ = divmod(m, 2)
                dve.wait_ge(S["d_bank"], 16 * i + m + 1)
                dve.tensor_tensor(X[:, t, half(c_)], PS[:, 4 + m % 4, :], X[:, t, half(c_)], ALU.add).then_inc(S["d_free"], 1)

        def chunk_dve(i, par, more=True):
            first = isinstance(i, int) and i == 0
            if not first:
                wgu_lo(i, 1)
            for s in range(2):
                for hf in range(2):
                    m = 4 * i + 2 * s + hf
                    hid(m, hf)
                    act_lo(m, hf, 2 * par + s, hf)
                    if s == 1 and hf == 0 and not first:
                        wd_lo(i - 1)
                    if first and m == 0:
                        accumulate(18)
                        accumulate(19)
                if s == 0 and more:
                    wgu_lo(i + 1, 0)
            if not first:
                add_down(i - 1)

        accumulate(16)
        accumulate(17)
        chunk_dve(0, 0)
        gate(2)
        gate(3)
        dve.sem_inc(S["d_free"], 4)
        with dve.Fori(0, (NC - 3) // 2) as j:
            for par in (1, 0):
                chunk_dve(2 * j + (1 if par else 2), par)
        chunk_dve(NC - 2, (NC - 2) % 2)
        chunk_dve(NC - 1, (NC - 1) % 2, more=False)
        wd_lo(NC - 1, WD2, WD2raw)

        def finish(t0, n_):
            dve.wait_ge(S["ss3"], t0 + n_)
            inverse_root(RS3[:, t0:t0 + n_], SS3[:, t0:t0 + n_], n_, D, S["rs3"])
            dve.wait_ge(S["gfin_in"], 16)
            for t in range(t0, t0 + n_):
                if t == t0:
                    dve.wait_ge(S["rs3"], {0: 1, 2: 2, 4: 3, 6: 4, 7: 5}[t])
                dve.scalar_tensor_tensor(X[:, t, :], X[:, t, :], RS3[:, t:t + 1], GT1[:], ALU.mult, ALU.mult).then_inc(S["fin"], 1)

        for m in range(2 * NT):
            t, c_ = divmod(m, 2)
            dve.wait_ge(S["d_bank"], 16 * (NC - 1) + m + 1)
            dve.tensor_tensor(X[:, t, half(c_)], PS[:, 4 + m % 4, :], X[:, t, half(c_)], ALU.add).then_inc(S["d_free"], 1)
            if m in (5, 9, 13):
                finish((m - 5) // 2, 2)
        finish(6, 1)
        finish(7, 1)

    @block.tensor
    def _(pe):
        def product(ps, terms):
            terms = list(terms)
            for n_, (l, r) in enumerate(terms):
                ins = pe.matmul(ps, l, r, start=(n_ == 0), stop=(n_ == len(terms) - 1))
            return ins

        pe.wait_ge(S["pool_const"], 1)
        for t in range(NT):
            pe.wait_ge(S["xn1"], t + 1)
            if t >= 2:
                pe.wait_ge(S["ev1"], 2 * t - 2)
            for k in range(KT):
                ins = pe.transpose(PS[:, 2 * (t % 2) + k // 4, (k % 4) * P:(k % 4 + 1) * P], X[:, t, k * P:(k + 1) * P], IDENT[:])
            ins.then_inc(S["t1"], 1)
            if t == 3:
                pe.wait_ge(S["rows_in"], 64)
                pe.transpose(PS[:, 6, 0:N_ROWS], ROWS[0:N_ROWS, :], IDENT[0:N_ROWS, 0:N_ROWS]).then_inc(S["rowsT"], 1)

        def col_sum(o_):
            ch = DVE_CHUNKS[o_]
            pe.wait_ge(S["acc_done"], 2 * o_ + 2)
            if ch in (4, 5, 10, 11):
                gt, bank = (GT1, 6 + ch % 2) if ch < 6 else (GT2, 4 + ch % 2)
                if ch == 4:
                    pe.wait_ge(S["modcols"], 1)
                pe.matmul(PS[:, bank, :], ONES[:], gt[:, half(ch % 2)], start=True, stop=True).then_inc(S["colsum"], 1)
                return
            col = 4 * ch if ch < 4 else 16 + 4 * (ch - 6)
            for j in range(4):
                ins = pe.matmul(PS[:, 7, col + j:col + j + 1], ACC[:, ch % 2, j * P:(j + 1) * P], ONES[:, 0:1], start=True, stop=True)
            ins.then_inc(S["colsum"], 1)

        for ch in range(2):
            pe.wait_ge(sh1_in[ch], 32)
            for j in range(4):
                col = 4 * ch + j
                ins = product(PS[:, 7, col:col + 1], [(ADAS[:, 2 * ch + t // 4, t % 4, j * P:(j + 1) * P], CS[:, t:t + 1])
                                                      for t in range(KT)])
        ins.then_inc(S["sh1_sum"], 1)
        for o_ in range(2):
            col_sum(o_)

        for t in range(NT):
            pe.wait_ge(S["wtm_ready"], 4)
            pe.wait_ge(S["h_ready"], KT * (t // 4 + 1))
            if t >= 2:
                pe.wait_ge(S["tm_out"], t - 1)
            product(PS[:, 4 + t % 2, 0:TM], [(HT[:, a, k, tok(t)], WTM[:, b, k, :]) for k in range(KT) for a, b in PASSES]
                    ).then_inc(S["tm_done"], 1)
            if t in (5, 7):
                col_sum(2 + (t - 5) // 2)

        def pool_group(i):
            pe.wait_ge(S["wu_ready"], i + 1)
            for hf in range(2):
                if i >= 1:
                    pe.wait_ge(S["u_out"], 2 * i - 1 + hf)
                product(PS[:, hf, :], [(WU[:, i % 2, a, k, :], HT[:, b, k, half(hf)]) for k in range(KT) for a, b in PASSES]
                        ).then_inc(S["u_done"], 1)

        def turn_latents(t):
            pe.wait_ge(S["tm_norm"], NT)
            pe.wait_ge(S["kr_ready"], 1)
            if t >= 2:
                pe.wait_ge(S["lt_lo"], t - 1)
            for i, c0 in enumerate((0, P, QR, QR + LAT)):
                ins = pe.transpose(PS[:, 2 + t % 2, i * P:(i + 1) * P], TMO[:, t, c0:c0 + P], IDENT[:])
            ins.then_inc(S["lt_T"], 1)

        pool_group(0)
        pool_group(1)
        for t in range(4):
            turn_latents(t)
        pool_group(2)
        for t in range(4, NT):
            turn_latents(t)
        pe.wait_ge(S["wuk_in"], 16)
        for h in range(HEADS):
            ins = pe.transpose(PS[:, 4, h * P:(h + 1) * P], WUKraw[:, h, :], IDENT[:])
        ins.then_inc(S["wukT"], 1)
        pool_group(3)

        pe.wait_ge(S["wuq_ready"], 1)
        pe.wait_ge(S["lt_lo"], NT)
        for i, t in enumerate(BLOCKS):
            if i >= 2:
                pe.wait_ge(S["qr_raw"], i - 1)
            product(PS[:, 2 + i % 2, 0:HEADS * ROPE].rearrange("p (h d) -> p h d", h=HEADS),
                    [(LT[:, k, a, tok(t)], WUQ[:, b, k, :, NOPE:]) for k in range(2) for a, b in PASSES]).then_inc(S["qr_done"], 1)

        pe.wait_ge(S["wp_ready"], 1)
        pe.wait_ge(S["u_out"], 2 * GROUPS)
        pool_parts = {HI: POOLHI, LO: UR}
        for m in range(2 * GROUPS):
            g, hf = GORDER[m // 2], m % 2
            pe.wait_ge(S["pool_lo"], m // 2 + 1)
            if m >= 2:
                pe.wait_ge(S["pm_y"], m - 1)
            product(PS[:, m % 2, :], [(WP[:, a, g, :], POOLHI[:, g, half(hf)] if b == HI else UR[:, g, PADW + hf * HALF:PADW + (hf + 1) * HALF])
                                      for a, b in PASSES]).then_inc(S["pm_done"], 1)

        def q_nope(i):
            hf, h = 1 - i // 4, i % 4
            if i == 0:
                pe.wait_ge(S["wuk_ready"], 1)
            if i >= 2:
                pe.wait_ge(S["qn_lo"], i - 1)
            product(PS[:, 4 + i % 2, :], [(WUQ[:, a, k, h, 0:NOPE], LT[:, k, b, half(hf)]) for k in range(2) for a, b in PASSES]
                    ).then_inc(S["qn_done"], 1)

        def q_latent(i):
            h = i % 4
            if i == 0:
                pe.wait_ge(S["gt_ready"], 2)
            pe.wait_ge(S["qn_lo"], i + 1)
            if i >= 2:
                pe.wait_ge(S["ql_lo"], i - 1)
            product(PS[:, 6 + i % 2, :], [(WUK[:, a, h, :], QN[:, i % 2, b, :]) for a, b in PASSES]).then_inc(S["ql_done"], 1)

        def turn_rope(i):
            pe.wait_ge(S["qr_dup"], i + 1)
            pe.wait_ge(S["qr_raw"], NT)
            if i >= 2:
                pe.wait_ge(S["qr_lo"], i - 1)
            for h in range(HEADS):
                ins = pe.transpose(PS[:, 2 + i % 2, h * P:(h + 1) * P], QRD[:, i % 2, h].rearrange("p a d -> p (a d)"), IDENT[:])
            ins.then_inc(S["qr_T"], 1)

        for i in range(NT):
            q_nope(i)
            if i >= 1:
                q_latent(i - 1)
            turn_rope(i)
        q_latent(NT - 1)

        QL = (QLhi, QLlo)

        def scores(n_, h):
            b = BLOCKS[n_]
            m = 4 * n_ + h
            if m == 0:
                pe.wait_ge(S["ql_lo"], 8)
                pe.wait_ge(S["qr_lo"], NT)
                pe.wait_ge(S["pm_y"], 8)
            if m >= 2:
                pe.wait_ge(S["exp_done"], m - 1)
            for c0 in range(0, b + 1, 4):
                nk = min(4, b + 1 - c0)
                ks = slice(c0 * P, (c0 + nk) * P)
                bank = PS[:, 2 * (h % 2) + c0 // 4, 0:nk * P]
                q = tok(b)
                terms = [(QL[a_][:, h, q], LT[:, 2, b_, ks]) for a_, b_ in PASSES]
                terms += [(QS[:, h, q], KRT[:, a_, ks]) for a_ in (HI, LO)]
                diag = c0 + nk == b + 1
                for z, (l, r) in enumerate(terms):
                    ins = pe.matmul(bank, l, r, start=(z == 0), stop=(z == 4 and not diag))
                if diag:
                    ins = pe.matmul(bank[:, (nk - 1) * P:nk * P], MASKQ[:], MASKK[:], start=False, stop=True)
            ins.then_inc(S["s_done"], 1)

        def turn_p(n_, h):
            b = BLOCKS[n_]
            m = 4 * n_ + h
            pe.wait_ge(S["p_norm"], m + 1)
            if m >= 1:
                pe.wait_ge(S["pt_lo"], m)
            for j in range(b + 1):
                ins = pe.transpose(PS[:, 4 + j // 4, (j % 4) * P:(j % 4 + 1) * P], PR[:, h, j * P:(j + 1) * P], IDENT[:])
            ins.then_inc(S["p_T"], 1)

        def values(n_):
            b = BLOCKS[n_]
            pe.wait_ge(S["ckv_ready"], 1)
            pe.wait_ge(S["pt_lo"], 4 * n_ + 4)
            if n_ >= 1:
                pe.wait_ge(S["ol_lo"], n_)
            product(PS[:, 6, :], [(CKV[:, a_, j, :], PT[:, b_, j].rearrange("p h n -> p (h n)"))
                                  for j in range(b + 1) for a_, b_ in PASSES]).then_inc(S["pv_done"], 1)

        def up_values(n_):
            pe.wait_ge(S["wuv_ready"], 1)
            pe.wait_ge(S["ol_lo"], n_ + 1)
            if n_ >= 1:
                pe.wait_ge(S["y_lo"], n_)
            for h in range(HEADS):
                ins = product(PS[:, 7, h * P:(h + 1) * P], [(WUV[:, a_, h, :], OL[:, b_, h * P:(h + 1) * P]) for a_, b_ in PASSES])
            ins.then_inc(S["op_done"], 1)

        for n_ in range(NT):
            scores(n_, 0)
            if n_ >= 2:
                up_values(n_ - 2)
            if n_ >= 1:
                turn_p(n_ - 1, 0)
            scores(n_, 1)
            if n_ >= 1:
                turn_p(n_ - 1, 1)
            scores(n_, 2)
            if n_ >= 1:
                turn_p(n_ - 1, 2)
                turn_p(n_ - 1, 3)
            scores(n_, 3)
            if n_ >= 1:
                values(n_ - 1)
        up_values(NT - 2)
        for h in range(HEADS):
            turn_p(NT - 1, h)
        values(NT - 1)
        up_values(NT - 1)

        def mix(m):
            c_, t = divmod(m, NT)
            if m == 0:
                pe.wait_ge(S["y_lo"], NT)
                pe.wait_ge(S["pm_lo"], 8)
            pe.wait_ge(S["wo_ready"], KT * (c_ + 1))
            if m >= 4:
                pe.wait_ge(S["mix_gated"], m - 3)
            W = {HI: WOhi[c_], LO: WOlo[c_]}
            product(PS[:, m % 4, :], [(HT[:, a_, k, tok(t)], W[b_][:, k, :]) for k in range(KT) for a_, b_ in PASSES]
                    ).then_inc(S["mix_done"], 1)

        def turn_x(t):
            pe.wait_ge(S["xn2"], t + 1)
            if t >= 2:
                pe.wait_ge(S["ev2"], t - 1)
            for k in range(KT):
                ins = pe.transpose(PS[:, 4 + 2 * (t % 2) + k // 4, (k % 4) * P:(k % 4 + 1) * P], XN[:, t % 2, k * P:(k + 1) * P], IDENT[:])
            ins.then_inc(S["t2"], 1)

        for m in range(2 * NT):
            mix(m)
            if m in (3, 5, 7, 8):
                col_sum({3: 4, 5: 5, 7: 6, 8: 7}[m])
            if m >= NT + 2:
                turn_x(m - NT - 2)

        def gate_up(i, s, hf, first=False):
            if hf == 0:
                pe.wait_ge(S["wgu_ready"], 2 * i + s + 1)
            m = 4 * i + 2 * s + hf
            if not first:
                pe.wait_ge(S["hid"], m - 1)
            for a in range(2):
                ins = product(PS[:, 2 * hf + a, :], [(WGU[:, s, w_, a, k, :], HT[:, h_, k, half(hf)])
                                                     for k in range(KT) for w_, h_ in PASSES])
            ins.then_inc(S["gu_half"], 1)

        def down(i, par, rows=WD):
            pe.wait_ge(S["wd_ready"], i + 1)
            pe.wait_ge(S["act_ready"], 4 * i + 4)
            for m in range(2 * NT):
                t, c_ = divmod(m, 2)
                pe.wait_ge(S["d_free"], 16 * i + m + 1)
                product(PS[:, 4 + m % 4, :], [(ACTS[:, 2 * par + s, a_, tok(t)], rows[:, b_, s, half(c_)])
                                              for s in range(2) for a_, b_ in PASSES]).then_inc(S["d_bank"], 1)

        pe.wait_ge(S["mix_gated"], 2 * NT)
        pe.wait_ge(S["h2_ready"], 4)
        gate_up(0, 0, 0, first=True)
        turn_x(NT - 2)
        turn_x(NT - 1)
        pe.wait_ge(S["h2_ready"], NT)
        gate_up(0, 0, 1, first=True)
        for hf in range(2):
            gate_up(0, 1, hf)
        col_sum(8)
        col_sum(9)

        def chunk_pe(i, par):
            for s in range(2):
                for hf in range(2):
                    gate_up(i, s, hf)
            down(i - 1, 1 - par)

        with pe.Fori(0, (NC - 3) // 2) as j:
            for par in (1, 0):
                chunk_pe(2 * j + (1 if par else 2), par)
        chunk_pe(NC - 2, (NC - 2) % 2)
        chunk_pe(NC - 1, (NC - 1) % 2)
        down(NC - 1, (NC - 1) % 2, WD2)

    ctx.close()


_INS = ["x", "c", "positions", "w_ada", "b_ada", "g_mix", "w_in", "g_q", "g_kv", "w_uq", "w_uk", "w_uv",
        "w_pool", "pool_scale", "w_o", "g_ffn", "w_gate", "w_up", "w_down", "g_final"]


def kernel(**inputs):
    import concourse.bacc as bacc
    from concourse.bass_utils import run_bass_kernel_spmd as run

    nc = bacc.Bacc("TRN2", target_bir_lowering=False, num_devices=1)
    arrays, args = {}, []
    for name in _INS:
        a = np.ascontiguousarray(inputs[name])
        arrays[f"in_{name}"] = a
        args.append(nc.dram_tensor(f"in_{name}", a.shape, mybir.dt.from_np(a.dtype), kind="ExternalInput").ap())
    f = np.power(10000.0, -np.arange(RH) / RH).astype(np.float32)
    arrays["freqs"] = f
    args.append(nc.dram_tensor("freqs", f.shape, F32, kind="ExternalInput").ap())
    args.append(nc.dram_tensor("out", (1, SEQ, D), F32, kind="ExternalOutput").ap())
    hybrid_block(nc, *args)
    r = run(nc, [arrays], core_ids=[0])
    return r.results[0]["out"]
```

```python
from contextlib import ExitStack

import numpy as np

import concourse.bass as bass
from concourse import mybir

ALU = mybir.AluOpType
ACT = mybir.ActivationFunctionType
AX = mybir.AxisListType
F32 = mybir.dt.float32
F32R = mybir.dt.float32r
BF16 = mybir.dt.bfloat16
I32 = mybir.dt.int32

P = 128
SEQ = 1024
D = 1024
KT = D // P
NT = SEQ // P
HALF = 512
HEADS = 4
NOPE = 128
ROPE = 64
RH = ROPE // 2
QR = 256
LAT = 128
VD = 128
TM = QR + LAT + ROPE
TMW = TM + ROPE
CHUNK = 64
GROUPS = 4
PADW = 16
DFF = 2816
FT = DFF // P
NC = FT // 2
EPS = 1e-6
SCALE = float((NOPE + ROPE) ** -0.5)
MASKED = -float(2.0 ** 100)
HI, LO = 0, 1
PASSES = ((HI, LO), (HI, HI), (LO, HI))
RSQRT_MAGIC = float(0x5F3759DF)
ROUND_MAGIC = float(3 * 2 ** 22)
N_ROWS = 48 + 8 + 8 + 4
ROW_MIX, ROW_FFN, ROW_POOL = 48, 56, 64
KB = 1024


def two_pi_parts():
    rest, parts = 2 * np.pi, []
    for _ in range(4):
        e = int(np.floor(np.log2(rest))) - 6
        part = float(np.floor(rest / 2.0 ** e) * 2.0 ** e)
        parts.append(part)
        rest -= part
    return parts + [float(np.float32(rest))]


def hybrid_block(nc, x, c, positions, w_ada, b_ada, g_mix, w_in, g_q, g_kv, w_uq, w_uk, w_uv,
                 w_pool, pool_scale, w_o, g_ffn, w_gate, w_up, w_down, g_final, freqs, out):
    ctx = ExitStack()
    enter = ctx.enter_context
    base = 16512
    nc.alloc_sbuf_tensor("arena", [P, (229344 - base) // 4], F32)

    def at(name, kb, shape, dt=F32):
        return nc.alloc_sbuf_tensor_at(name, shape, dt, offset=base + int(kb * KB))

    def sem(name):
        return enter(nc.semaphore(name))

    X = at("X", 0, [P, NT, D])
    PT = at("PT", 0, [P, 2, NT, HEADS, P], F32R)
    U = at("U", 0, [P, GROUPS, PADW + SEQ])
    UR = at("UR", 0, [P, GROUPS, PADW + SEQ], F32R)
    WIN = at("WIN", 16.25, [P, 2, PADW + SEQ])
    ropeK = at("ropeK", 16.25, [P, 2, NT, 2, RH])
    ropeQ = at("ropeQ", 16.25, [P, 2, HEADS, 2, RH])
    QRD = at("QRD", 18.25, [P, 3, HEADS, 2, ROPE])
    WP = at("WP", 24.5, [P, 2, GROUPS, P], F32R)
    WPraw = at("WPraw", 26.5, [P, GROUPS, P])
    HT = at("HT", 32, [P, 2, KT, SEQ], F32R)
    HTf = at("HTf", 64, [P, KT, SEQ])
    ADA0 = at("ADA0", 32, [P, 4, 4, HALF])
    QRAW = at("QRAW", 32, [P, NT, HEADS, ROPE])
    QN = at("QN", 40, [P, 2, 2, HALF], F32R)
    POOLHI = at("POOLHI", 64, [P, GROUPS, SEQ], F32R)
    QS = at("QS", 64, [P, HEADS, SEQ], F32R)
    WTM = at("WTM", 96, [P, 2, KT, TM], F32R)
    WTMraw = at("WTMraw", 110, [P, KT, TM])
    LT = at("LT", 96, [P, 3, 2, SEQ], F32R)
    PR = at("PR", 96, [P, HEADS, SEQ])
    WUV = at("WUV", 120, [P, 2, HEADS, VD], F32R)
    WUVraw = at("WUVraw", 122, [P, HEADS, VD])
    WU = at("WU", 124, [P, 2, 2, KT, P], F32R)
    WUraw = at("WUraw", 124, [P, 2, 2, KT, P])
    ADAS = at("ADAS", 124, [P, 4, 4, HALF])
    QLhi = at("QLhi", 124, [P, HEADS, SEQ], F32R)
    QLlo = at("QLlo", 156, [P, HEADS, SEQ], F32R)
    ADA1 = at("ADA1", 140, [P, 2, 4, HALF])
    WUQ = at("WUQ", 140, [P, 2, 2, HEADS, NOPE + ROPE], F32R)
    WUQraw = at("WUQraw", 146, [P, 2, HEADS, NOPE + ROPE])
    WUK = at("WUK", 152, [P, 2, HEADS, LAT], F32R)
    WUKraw = at("WUKraw", 152, [P, HEADS, NOPE])
    TMO = at("TMO", 156, [P, NT, TMW])
    JUNK = at("JUNK", 188, [P, SEQ])
    ACC = at("ACC", 172, [P, 2, HALF])
    OL = at("OL", 172, [P, 2, HALF], F32R)
    CKV = at("CKV", 176, [P, 2, NT, LAT], F32R)
    KRT = at("KRT", 184, [P, 2, SEQ], F32R)
    COS = at("COS", 192, [P, NT, RH])
    SIN = at("SIN", 193, [P, NT, RH])
    GQ = at("GQ", 194, [P, QR])
    GKV = at("GKV", 195, [P, LAT])
    ROWS = at("ROWS", 195.5, [P, P])
    ANG = at("ANG", 176, [P, NT, RH])
    TURN = at("TURN", 177, [P, NT, RH])
    SHALF = at("SHALF", 178, [P, NT, RH])
    SQUART = at("SQUART", 179, [P, NT, RH])
    SHROW = at("SHROW", 180, [P, 2, HALF])
    QH0 = at("QH0", 124, [P, HEADS, 2, HALF], F32R)
    QL0 = at("QL0", 156, [P, HEADS, 2, HALF], F32R)
    WO0lo = at("WO0lo", 140, [P, KT, HALF], F32R)
    WO0raw = at("WO0raw", 140, [P, KT, HALF])
    WO1hi = at("WO1hi", 96, [P, KT, HALF], F32R)
    WO1_KB = [112 + 2 * k for k in range(6)] + [124, 160]
    WO1lo = [at(f"WO1lo{k}", kb, [P, HALF], F32R) for k, kb in enumerate(WO1_KB)]
    WO1raw = [at(f"WO1raw{k}", kb, [P, HALF]) for k, kb in enumerate(WO1_KB)]
    WOhi = [[(QH0, QL0)[k // 4][:, k % 4, 1, :] for k in range(KT)], [WO1hi[:, k, :] for k in range(KT)]]
    WOlo = [[WO0lo[:, k, :] for k in range(KT)], [WO1lo[k][:] for k in range(KT)]]
    WOraw = [[WO0raw[:, k, :] for k in range(KT)], [WO1raw[k][:] for k in range(KT)]]
    MIX = [at("MIX0", 164, [P, HALF]), at("MIX1", 168, [P, HALF])]
    JUNK2 = at("JUNK2", 180, [P, SEQ])
    XN = at("XN", 184, [P, 2, D])
    ADA2 = at("ADA2", 180, [P, 2, 4, HALF])
    ACTS = at("ACTS", 96, [P, 4, 2, SEQ], F32R)
    WGU = at("WGU", 128, [P, 2, 2, 2, KT, P], F32R)
    WGUraw = at("WGUraw", 128, [P, 2, 2, 2, KT, P])
    WD = at("WD", 160, [P, 2, 2, D], F32R)
    WDraw = at("WDraw", 168, [P, 2, D])
    WD2 = at("WD2", 128, [P, 2, 2, D], F32R)
    WD2raw = at("WD2raw", 136, [P, 2, D])
    XG = at("XG", 32, [P, NT, D])
    HID = at("HID", 176, [P, 2, HALF])
    IDENT = at("IDENT", 196, [P, P])
    ONES = at("ONES", 196.5, [P, P])
    MASKQ = at("MASKQ", 197, [P, P], BF16)
    MASKK = at("MASKK", 197.25, [P, P], BF16)
    o = 197.5

    def small(name, n, dt=F32):
        nonlocal o
        t = at(name, o, [P, n], dt)
        o += (4 * n + 31) // 32 * 32 / KB
        return t

    COLS = small("COLS", N_ROWS)
    MOD = small("MOD", 32)
    G1 = small("G1", KT)
    G2 = small("G2", KT)
    CT = small("CT", KT)
    CS = small("CS", KT)
    POSI = small("POSI", NT, I32)
    POSF = small("POSF", NT)
    FREQ = small("FREQ", RH)
    INV = small("INV", 16)
    SS = small("SS", 16)
    VAR = small("VAR", 16)
    RS = small("RS", 16)
    RT = small("RT", 16)
    RI = small("RI", 16, I32)
    VHALF = small("VHALF", 1)
    NEGM = small("NEGM", 32)
    SUM = small("SUM", 32)
    RSUM = small("RSUM", 32)
    SS2 = small("SS2", NT)
    RS2 = small("RS2", NT)
    SS3 = small("SS3", NT)
    RS3 = small("RS3", NT)
    assert o <= 199.8
    GT1 = at("GT1", 199.8125, [P, D])
    GT2 = at("GT2", 203.8125, [P, D])

    PS = enter(nc.psum_tensor("PS", [P, 8, HALF], F32))

    names = """c_in rows_in pos_in freq_in gq_in gkv_in gt_in wp_in wuv_in wuq_in wuk_in gfin_in out_done
        pool_const  act_silu ang_ready sin_ready trig_ready dve_step pool_step
        ss1 rs1 xn1 t1 gt_zero acc_done sh1_rows sh1_out sh1_sum colsum modcols gt_ready rowsT
        hmod h_hi h_ready wtm_hi wtm_ready tm_done tm_out tm_norm kr_ready ckv_hi ckv_ready
        wu_hi wu_ready u_done u_out windowed pooled lt_T lt_hi lt_lo pool_hi pool_lo wp_hi wp_ready pm_done pm_y pm_hi pm_lo
        wuq_hi wuq_ready wukT wuk_hi wuk_ready wuv_hi wuv_ready
        qr_done qr_raw qr_rot qr_dup qr_T qr_hi qr_lo qn_done qn_hi qn_lo ql_done ql_hi ql_lo
        s_done negmax exp_done rsum p_norm p_T pt_hi pt_lo pv_done ol_hi ol_lo op_done y_hi y_lo
        wo_hi wo_ready mix_done mix_gated x_new ss2 rs2 xn2 t2 ev2 h2_hi h2_ready
        wgu_hi wgu_ready wd_fold wd_hi wd_ready gu_half silu hid act_hi act_ready
        d_bank d_free ss3 rs3 x_gain fin fin_dve""".split()
    S = {n: sem(n) for n in names}
    x_in = [sem(f"x_in{t}") for t in range(NT)]
    sc1_in = [sem(f"sc1_in{i}") for i in range(4)]
    sh1_in = [sem(f"sh1_in{i}") for i in range(4)]
    ada_in = [sem(f"ada_in{i}") for i in range(2)]
    wtm_in = [sem(f"wtm_in{i}") for i in range(4)]
    wu_in = [sem(f"wu_in{i}") for i in range(2)]
    wo_in = [sem(f"wo_in{i}") for i in range(4)]
    wgu_in = [sem(f"wgu_in{i}") for i in range(2)]
    wd_in = sem("wd_in")

    x_d = x.rearrange("b (t p) d -> (b t) p d", p=P)
    out_d = out.rearrange("b (t p) d -> (b t) p d", p=P)
    ada_d = w_ada.rearrange("l (p t) n -> p (l t) n", t=KT)
    win_d = w_in.rearrange("l (k p) n -> p (l k) n", p=P)
    gate_d = w_gate.rearrange("l (k p) n -> p (l k) n", p=P)
    up_d = w_up.rearrange("l (k p) n -> p (l k) n", p=P)
    down_d = w_down.rearrange("l (f p) n -> p (l f) n", p=P)
    wo_d = w_o.rearrange("l (k p) n -> p (l k) n", p=P)
    wuq_d = w_uq.rearrange("l (k p) h d -> p (l k) h d", p=P)

    DVE_CHUNKS = (2, 3, 4, 5, 6, 7, 8, 9, 10, 11)
    N_PIECES = 2 * len(DVE_CHUNKS)

    def ada_piece(j):
        if j < 4:
            return ADA0[:, j], sc1_in[j], 16
        ring = ADA1 if j < 8 else ADA2
        return ring[:, j % 2], ada_in[j % 2], 16 * ((j - 4) // 2 + 1)

    def ada_source(ch, kh):
        return ada_d[:, 4 * kh:4 * kh + 4, ch * HALF:(ch + 1) * HALF]

    def flat(ap):
        return ap.rearrange("p a b -> p (a b)")

    def tok(t):
        return slice(t * P, (t + 1) * P)

    def half(i):
        return slice(i * HALF, (i + 1) * HALF)

    BLOCKS = list(range(NT - 1, -1, -1))
    UNITS = [(n_, h, j0) for n_ in range(NT) for h in range(HEADS) for j0 in range(0, BLOCKS[n_] + 1, 4)]

    def units(n_, h):
        return [(q, j0, min(4, BLOCKS[n_] + 1 - j0)) for q, (a, b, j0) in enumerate(UNITS) if (a, b) == (n_, h)]

    def units_done(n_, h):
        return units(n_, h)[-1][0] + 1

    PM_IN_BLOCK = ((), (0,), (1,), (2, 3), (4, 5), (6,), (7,), ())

    GORDER = list(range(GROUPS - 1, -1, -1))

    WO1_ORDER = (0, 4, 1, 5, 2, 6, 3, 7)


    block = enter(nc.Block())

    @block.sync
    def _(sp):
        def load_ada(j):
            buf, s, _ = ada_piece(j)
            if j == 4:
                sp.wait_ge(S["sh1_rows"], 1)
            elif j == 16:
                sp.wait_ge(S["t2"], NT)
            if j >= 4:
                sp.wait_ge(S["acc_done"], j - 1)
            sp.dma_start(buf, ada_source(DVE_CHUNKS[j // 2], j % 2)).then_inc(s, 16)

        sp.dma_start(CT[:], c.rearrange("b (p t) -> p (b t)", t=KT)).then_inc(S["c_in"], 16)
        def load_sh1(j):
            sp.dma_start(ADAS[:, j], ada_source(j // 2, j % 2)).then_inc(sh1_in[j], 16)

        def load_x(t):
            sp.dma_start(X[:, t, :], x_d[t]).then_inc(x_in[t], 16)

        load_sh1(0)
        load_ada(0)
        for src, r, n in ((b_ada, 0, 48), (g_mix, ROW_MIX, 8), (g_ffn, ROW_FFN, 8), (pool_scale, ROW_POOL, 4)):
            sp.dma_start(ROWS[r:r + n, :], src.rearrange("l (r n) -> (l r) n", n=P)).then_inc(S["rows_in"], 16)
        sp.dma_start(POSI[:], positions.rearrange("b (t p) -> p (b t)", p=P), allow_slow_non_contiguous=True).then_inc(S["pos_in"], 16)
        sp.dma_start(FREQ[:], freqs.partition_broadcast(P)).then_inc(S["freq_in"], 16)
        load_sh1(1)
        load_ada(1)
        load_sh1(2)
        load_ada(2)
        load_sh1(3)
        load_x(0)
        load_ada(3)
        for t in range(1, 4):
            load_x(t)
        for i in range(4):
            sp.dma_start(WTMraw[:, 2 * i:2 * i + 2, :], win_d[:, 2 * i:2 * i + 2, 0:TM]).then_inc(wtm_in[i], 16)
        for t in range(4, NT):
            load_x(t)
        sp.dma_start(GQ[:], g_q.rearrange("l n -> (l n)").partition_broadcast(P)).then_inc(S["gq_in"], 16)
        sp.dma_start(GKV[:], g_kv.rearrange("l n -> (l n)").partition_broadcast(P)).then_inc(S["gkv_in"], 16)
        sp.wait_ge(S["gt_zero"], 1)
        sp.dma_start(GT1[0:1, :], b_ada[:, 2 * D:3 * D]).then_inc(S["gt_in"], 16)
        sp.dma_start(GT2[0:1, :], b_ada[:, 5 * D:6 * D]).then_inc(S["gt_in"], 16)

        def load_wu(i):
            g = GORDER[i]
            sp.dma_start(WUraw[:, i % 2, LO], win_d[:, :, TM + g * P:TM + (g + 1) * P]).then_inc(wu_in[i % 2], 16)

        sp.wait_ge(S["sh1_rows"], 1)
        load_wu(0)
        load_wu(1)
        load_ada(4)
        load_ada(5)
        sp.wait_ge(S["t1"], NT)
        sp.dma_start(WPraw[:], w_pool.rearrange("l g c d -> c (l g) d")).then_inc(S["wp_in"], 16)
        load_ada(6)
        load_ada(7)
        sp.wait_ge(S["tm_done"], NT)
        sp.dma_start(WUVraw[:], w_uv.rearrange("l c h v -> c (l h) v")).then_inc(S["wuv_in"], 16)
        sp.wait_ge(S["u_done"], 2)
        load_wu(2)
        sp.wait_ge(S["acc_done"], 8)
        sp.dma_start(WUQraw[:], wuq_d).then_inc(S["wuq_in"], 16)
        sp.dma_start(WUKraw[:], w_uk.rearrange("l c h d -> c (l h) d")).then_inc(S["wuk_in"], 16)
        sp.wait_ge(S["u_done"], 4)
        load_wu(3)
        sp.wait_ge(S["ql_done"], 8)
        for i in range(4):
            sp.dma_start(WO0raw[:, 2 * i:2 * i + 2, :], wo_d[:, 2 * i:2 * i + 2, half(0)]).then_inc(wo_in[i], 16)
        for n_, tiles in ((4, (7, 6, 3, 2)), (NT, (5, 4))):
            sp.wait_ge(S["pv_done"], n_)
            for t in tiles:
                load_x(t)
        sp.wait_ge(S["op_done"], NT)
        for k in WO1_ORDER:
            sp.dma_start(WOraw[1][k], wo_d[:, k, half(1)]).then_inc(wo_in[k % 4], 16)
        load_ada(8)
        load_ada(9)
        load_x(1)
        load_x(0)
        for j in range(10, 16):
            load_ada(j)

        def load_wgu(f, s):
            sp.dma_start(WGUraw[:, s, LO, 0], gate_d[:, :, bass.ds(f * P, P)]).then_inc(wgu_in[s], 16)
            sp.dma_start(WGUraw[:, s, LO, 1], up_d[:, :, bass.ds(f * P, P)]).then_inc(wgu_in[s], 16)

        def load_wd(i, buf=WDraw):
            sp.dma_start(buf[:], down_d[:, bass.ds(2 * i, 2), :]).then_inc(wd_in, 16)

        sp.wait_ge(S["mix_done"], NT)
        load_wgu(0, 0)
        load_wgu(1, 1)
        sp.wait_ge(S["x_new"], 2 * NT)
        load_wd(0)
        sp.dma_start(GT1[:], g_final.partition_broadcast(P)).then_inc(S["gfin_in"], 16)

        def chunk_loads(i):
            for s in range(2):
                sp.wait_ge(S["gu_half"], 4 * i + s + 3)
                load_wgu(2 * i + 2 + s, s)
            if not isinstance(i, int) or i > 0:
                sp.wait_ge(S["d_bank"], 16 * i)
                load_wd(i)

        for j in range(16, N_PIECES):
            load_ada(j)
        chunk_loads(0)
        with sp.Fori(0, (NC - 3) // 2) as j:
            for par in (1, 0):
                chunk_loads(2 * j + (1 if par else 2))
        chunk_loads(NC - 2)
        sp.wait_ge(S["gu_half"], 4 * (NC - 1) + 3)
        sp.wait_ge(S["wd_fold"], NC - 1)
        load_wd(NC - 1, WD2raw)
        def store(t):
            sp.dma_start(out_d[t], XG[:, t, :]).then_inc(S["out_done"], 16)

        for t in range(4):
            sp.wait_ge(S["fin"], t + 1)
            store(t)
        for t in (4, 5):
            sp.wait_ge(S["fin_dve"], t - 3)
            store(t)
        sp.wait_ge(S["fin_dve"], 3)
        store(7)
        sp.wait_ge(S["fin"], 5)
        store(6)
        sp.wait_ge(S["out_done"], 16 * NT)

    @block.gpsimd
    def _(pool):
        n = 0

        def then(ins):
            nonlocal n
            n += 1
            ins.then_inc(S["pool_step"], 1)
            pool.wait_ge(S["pool_step"], n)

        then(pool.memset(IDENT[:], 0.0))
        then(pool.affine_select(out=IDENT[:], in_=IDENT[:], compare_op=ALU.not_equal, fill=1.0, base=0,
                                pattern=[[-1, P]], channel_multiplier=1))
        then(pool.memset(MASKQ[:], 0.0))
        then(pool.memset(MASKK[:], 0.0))
        then(pool.memset(MASKQ[0:1, 0:CHUNK], 1.0))
        then(pool.memset(MASKK[0:1, CHUNK:P], MASKED))
        for t in range(PADW):
            pool.memset(INV[:, t:t + 1], 1.0 / (t + 1))
        pool.memset(ONES[:], 1.0).then_inc(S["pool_const"], 1)
        pool.memset(GT1[:], 0.0)
        pool.memset(GT2[:], 0.0).then_inc(S["gt_zero"], 1)

        for i in range(4):
            pool.wait_ge(wtm_in[i], 16)
            pool.tensor_scalar(flat(WTM[:, HI, 2 * i:2 * i + 2, :]), flat(WTMraw[:, 2 * i:2 * i + 2, :]),
                               1.0, 0.0, ALU.mult, ALU.add).then_inc(S["wtm_hi"], 1)
        for t in range(NT):
            pool.wait_ge(S["hmod"], t + 1)
            pool.tensor_scalar(HT[:, HI, :, tok(t)], HTf[:, :, tok(t)], 1.0, 0.0, ALU.mult, ALU.add).then_inc(S["h_hi"], 1)

        def wu_hi(g):
            pool.wait_ge(wu_in[g % 2], 16 * (g // 2 + 1))
            pool.tensor_scalar(flat(WU[:, g % 2, HI]), flat(WUraw[:, g % 2, LO]), 1.0, 0.0, ALU.mult, ALU.add).then_inc(S["wu_hi"], 1)

        wu_hi(0)
        wu_hi(1)
        pool.wait_ge(S["tm_out"], NT)
        pool.wait_ge(S["trig_ready"], 1)
        pool.memset(U[:, :, 0:PADW], 0.0)
        keys = TMO[:, :, QR + LAT:TM].rearrange("p t (a d) -> p t a d", a=2)
        for table, trig in ((0, COS), (1, SIN)):
            for a in range(2):
                ins = pool.tensor_tensor(ropeK[:, table, :, a], keys[:, :, a], trig[:], ALU.mult)
        then(ins)
        both = TMO[:, :, QR + LAT:TMW].rearrange("p t (c a d) -> p t c a d", c=2, a=2)

        def twice(ap):
            return ap.rearrange("p t (o d) -> p t o d", o=1).broadcast_to([P, NT, 2, RH])

        pool.tensor_tensor(both[:, :, :, 0], twice(ropeK[:, 0, :, 0]), twice(ropeK[:, 1, :, 1]), ALU.subtract)
        then(pool.tensor_tensor(both[:, :, :, 1], twice(ropeK[:, 1, :, 0]), twice(ropeK[:, 0, :, 1]), ALU.add))
        pool.memset(WIN[:, :, 0:PADW], 0.0).then_inc(S["kr_ready"], 1)
        pool.wait_ge(S["tm_norm"], NT)
        pool.tensor_scalar(CKV[:, HI], TMO[:, :, QR:QR + LAT], 1.0, 0.0, ALU.mult, ALU.add).then_inc(S["ckv_hi"], 1)

        pool.wait_ge(S["wp_in"], 16)
        pool.tensor_scalar(flat(WP[:, HI]), flat(WPraw[:]), 1.0, 0.0, ALU.mult, ALU.add).then_inc(S["wp_hi"], 1)
        pool.wait_ge(S["wuv_in"], 16)
        pool.tensor_scalar(flat(WUV[:, HI]), flat(WUVraw[:]), 1.0, 0.0, ALU.mult, ALU.add).then_inc(S["wuv_hi"], 1)
        for i, g in enumerate(GORDER):
            pool.wait_ge(S["u_out"], 2 * (i + 1))
            if i == 0:
                wu_hi(2)
            u = U[:, g]
            src, dst = u, WIN[:, 0]
            for s in range(g + 1):
                then(pool.tensor_tensor(dst[:, PADW:], src[:, PADW:], src[:, PADW - 2 ** s:PADW + SEQ - 2 ** s], ALU.add))
                src, dst = dst, WIN[:, (s + 1) % 2]
            w = 2 ** (g + 1)
            then(pool.tensor_tensor(src[:, PADW:PADW + w], src[:, PADW:PADW + w], INV[:, 0:w], ALU.mult))
            pool.tensor_scalar(src[:, PADW:PADW + w], src[:, PADW:PADW + w], float(w), 0.0, ALU.mult, ALU.add).then_inc(S["windowed"], 1)
            if i == 0:
                wu_hi(3)
            pool.wait_ge(S["pooled"], i + 1)
        def rotate(i, t):
            pool.wait_ge(S["qr_raw"], i + 1)
            if i >= 3:
                pool.wait_ge(S["qr_T"], i - 2)
            q = QRAW[:, t].rearrange("p h (a d) -> p h a d", a=2)
            for table, trig in ((0, COS), (1, SIN)):
                wide = trig[:, t:t + 1, :].rearrange("p (o a) d -> p o a d", o=1).broadcast_to([P, HEADS, 2, RH])
                ins = pool.tensor_tensor(ropeQ[:, table], q, wide, ALU.mult)
            then(ins)

            pool.tensor_tensor(QRD[:, i % 3, :, 0, 0:RH], ropeQ[:, 0, :, 0], ropeQ[:, 1, :, 1], ALU.subtract)
            pool.tensor_tensor(QRD[:, i % 3, :, 0, RH:ROPE], ropeQ[:, 1, :, 0], ropeQ[:, 0, :, 1],
                               ALU.add).then_inc(S["qr_rot"], 1)
            pool.wait_ge(S["qr_rot"], i + 1)

        for i, t in enumerate(BLOCKS):
            rotate(i, t)

        pool.wait_ge(S["s_done"], 4 * 4)
        for k in range(KT):
            if k % 2 == 0:
                pool.wait_ge(wo_in[k // 2], 16)
            pool.tensor_scalar(WOhi[0][k], WOraw[0][k], 1.0, 0.0, ALU.mult, ALU.add).then_inc(S["wo_hi"], 1)
            pool.wait_ge(S["wo_hi"], k + 1)
            pool.tensor_tensor(WOlo[0][k], WOraw[0][k], WOhi[0][k].bitcast(F32), ALU.subtract).then_inc(S["wo_ready"], 1)

        def x_add(m, c_, t):
            pool.wait_ge(S["mix_gated"], m + 1)
            if c_ == 0:
                pool.wait_ge(x_in[t], 32)
            pool.tensor_tensor(X[:, t, half(c_)], X[:, t, half(c_)], MIX[m % 2][:], ALU.add).then_inc(S["x_new"], 1)

        for m, t in enumerate(BLOCKS):
            x_add(m, 0, t)

        def h2_hi(t):
            pool.wait_ge(S["ev2"], t + 1)
            pool.tensor_scalar(HT[:, HI, :, tok(t)], HTf[:, :, tok(t)], 1.0, 0.0, ALU.mult, ALU.add).then_inc(S["h2_hi"], 1)

        def wd_fold(i, buf=WDraw):
            pool.wait_ge(wd_in, 16 * i + 16)
            for r in range(2):
                ins = pool.tensor_tensor(buf[:, r], buf[:, r], GT2[:], ALU.mult)
            ins.then_inc(S["wd_fold"], 1)

        for t in range(NT):
            x_add(NT + t, 1, t)
            if t >= 2:
                h2_hi(t - 2)
        h2_hi(NT - 2)
        h2_hi(NT - 1)
        pool.wait_ge(S["gt_ready"], 4)
        wd_fold(0)
        wd_fold(1)
        with pool.Fori(2, NC - 1) as i:
            wd_fold(i)
        wd_fold(NC - 1, WD2raw)
        pool.wait_ge(S["gfin_in"], 16)
        pool.wait_ge(S["gu_half"], 4 * NC)
        for t in range(NT):
            pool.wait_ge(S["d_free"], 4 + 16 * (NC - 1) + 2 * t + 2)
            pool.tensor_tensor(XG[:, t, :], X[:, t, :], GT1[:], ALU.mult).then_inc(S["x_gain"], 1)

    @block.scalar
    def _(act):
        act.wait_ge(S["c_in"], 16)
        act.activation(CS[:], CT[:], ACT.Silu).then_inc(S["act_silu"], 1)
        act.wait_ge(S["ang_ready"], 1)
        act.activation(SHALF[:], ANG[:], ACT.Sin, scale=0.5)
        act.activation(SQUART[:], ANG[:], ACT.Sin, scale=0.25).then_inc(S["sin_ready"], 1)

        def squares1(t):
            act.wait_ge(x_in[t], 16)
            act.activation(JUNK[:], X[:, t, :], ACT.Square, accum_out=SS[:, t:t + 1]).then_inc(S["ss1"], 1)
            act.wait_ge(S["ss1"], t + 1)

        def modulate1(t):
            act.wait_ge(S["t1"], t + 1)
            act.wait_ge(S["modcols"], 1)
            for k in range(KT):
                last = act.activation(HTf[:, k, tok(t)], PS[:, 2 * (t % 2) + k // 4, (k % 4) * P:(k % 4 + 1) * P],
                                      ACT.Identity, scale=G1[:, k:k + 1], bias=MOD[:, k:k + 1])
            last.then_inc(S["hmod"], 1)

        def tm_out(t):
            act.wait_ge(S["tm_done"], t + 1)
            b = 4 + t % 2
            act.activation(TMO[:, t, 0:TM], PS[:, b, 0:TM], ACT.Copy)
            act.activation(JUNK2[:, 0:QR], PS[:, b, 0:QR], ACT.Square, accum_out=SS[:, t:t + 1])
            act.activation(JUNK2[:, QR:QR + LAT], PS[:, b, QR:QR + LAT], ACT.Square,
                           accum_out=SS[:, 8 + t:9 + t]).then_inc(S["tm_out"], 1)
            act.wait_ge(S["tm_out"], t + 1)

        squares1(0)
        act.wait_ge(S["sh1_rows"], 1)
        act.activation(SHROW[0:1], PS[0:1, 4:6, :], ACT.Copy).then_inc(S["sh1_out"], 1)
        for t in range(1, 4):
            squares1(t)
        for t in range(NT):
            modulate1(t)
            if t < 4:
                squares1(t + 4)
            if t >= 3:
                tm_out(t - 3)
        for t in range(NT - 3, NT):
            tm_out(t)

        def u_out(i):
            g = GORDER[i]
            for hf in range(2):
                act.wait_ge(S["u_done"], 2 * i + hf + 1)
                act.activation(U[:, g, PADW + hf * HALF:PADW + (hf + 1) * HALF], PS[:, hf, :], ACT.Copy).then_inc(S["u_out"], 1)

        def lt_hi(t):
            act.wait_ge(S["lt_T"], t + 1)
            b = 2 + t % 4
            act.activation(LT[:, :, HI, tok(t)], PS[:, b, 0:3 * P].rearrange("p (k n) -> p k n", k=3), ACT.Copy)
            act.activation(KRT[:, HI, tok(t)], PS[:, b, 3 * P:], ACT.Copy).then_inc(S["lt_hi"], 1)

        def pooled_hi(i):
            g = GORDER[i]
            act.wait_ge(S["pooled"], i + 1)
            act.wait_ge(S["u_done"], 2 * GROUPS)
            act.activation(POOLHI[:, g], U[:, g, PADW:], ACT.Copy).then_inc(S["pool_hi"], 1)

        u_out(0)
        u_out(1)
        for t in range(4):
            lt_hi(t)
        u_out(2)
        for t in range(4, NT):
            lt_hi(t)
        act.wait_ge(S["wukT"], 1)
        act.activation(WUK[:, HI].rearrange("p h c -> p (h c)"), PS[:, 6, :], ACT.Copy).then_inc(S["wuk_hi"], 1)
        act.wait_ge(S["wuq_in"], 16)
        act.activation(WUQ[:, HI].rearrange("p k h d -> p (k h d)"), WUQraw[:].rearrange("p k h d -> p (k h d)"),
                       ACT.Copy).then_inc(S["wuq_hi"], 1)
        u_out(3)
        for i, t in enumerate(BLOCKS):
            act.wait_ge(S["qr_done"], i + 1)
            act.activation(QRAW[:, t].rearrange("p h d -> p (h d)"), PS[:, 2 + i % 2, 0:HEADS * ROPE], ACT.Copy).then_inc(S["qr_raw"], 1)
            if i % 2 == 1:
                pooled_hi(i // 2)

        def pm_y(m):
            g, hf = GORDER[m // 2], m % 2
            act.wait_ge(S["pm_done"], m + 1)
            act.activation(HTf[:, 4 + g, half(hf)], PS[:, m % 2, :], ACT.Copy,
                           scale=COLS[:, ROW_POOL + g:ROW_POOL + g + 1]).then_inc(S["pm_y"], 1)

        def ql_hi(i):
            hf, h = 1 - i // 4, i % 4
            act.wait_ge(S["ql_done"], i + 1)
            act.activation(QLhi[:, h, half(hf)], PS[:, 6 + i % 2, :], ACT.Copy).then_inc(S["ql_hi"], 1)

        def qr_twice(i):
            act.wait_ge(S["qr_rot"], i + 1)
            act.activation(QRD[:, i % 3, :, 1], QRD[:, i % 3, :, 0], ACT.Copy).then_inc(S["qr_dup"], 1)

        for m in range(8):
            pm_y(m)
            if m in (3, 5, 7):
                qr_twice((m - 3) // 2)
        for i, t in enumerate(BLOCKS):
            act.wait_ge(S["qn_done"], i + 1)
            if i >= 2:
                act.wait_ge(S["ql_done"], i - 1)
            act.activation(QN[:, i % 2, HI], PS[:, 4 + i % 2, :], ACT.Copy).then_inc(S["qn_hi"], 1)
            if i >= 1:
                ql_hi(i - 1)
            act.wait_ge(S["qr_T"], i + 1)
            act.activation(QS[:, :, tok(t)], PS[:, 2 + i % 2, :].rearrange("p (h n) -> p h n", h=HEADS), ACT.Copy).then_inc(S["qr_hi"], 1)
            if i < NT - 3:
                qr_twice(i + 3)
        ql_hi(7)

        def softmax_exp(n_, b, h):
            m = 4 * n_ + h
            act.wait_ge(S["negmax"], m + 1)
            if n_ >= 1:
                act.wait_ge(S["p_T"], units_done(n_ - 1, h))
            sl = 2 * (h % 2)
            act.activation(PR[:, h, 0:(b + 1) * P], flat(PS[:, sl:sl + 2, :])[:, 0:(b + 1) * P], ACT.Exp,
                           scale=SCALE, bias=NEGM[:, m:m + 1], accum_out=SUM[:, m:m + 1]).then_inc(S["exp_done"], 1)

        def normalise(m):
            if m < 0:
                return
            h, b = m % 4, BLOCKS[m // 4]
            act.wait_ge(S["rsum"], m + 1)
            act.activation(PR[:, h, 0:(b + 1) * P], PR[:, h, 0:(b + 1) * P], ACT.Copy, scale=RSUM[:, m:m + 1]).then_inc(S["p_norm"], 1)

        def turned_hi(n_, h):
            for q, j0, nj in units(n_, h):
                act.wait_ge(S["p_T"], q + 1)
                if h == 0 and n_ >= 1:
                    act.wait_ge(S["pv_done"], n_)
                act.activation(PT[:, HI, j0:j0 + nj, h, :],
                               PS[:, 4 + q % 2, 0:nj * P].rearrange("p (j n) -> p j n", j=nj), ACT.Copy).then_inc(S["pt_hi"], 1)

        def latent_hi(n_):
            act.wait_ge(S["pv_done"], n_ + 1)
            if n_ >= 1:
                act.wait_ge(S["op_done"], n_)
            act.activation(OL[:, HI], PS[:, 6, :], ACT.Copy).then_inc(S["ol_hi"], 1)

        def out_hi(n_):
            act.wait_ge(S["op_done"], n_ + 1)
            act.activation(HT[:, HI, 0:HEADS, tok(BLOCKS[n_])], PS[:, 7, :].rearrange("p (h n) -> p h n", h=HEADS),
                           ACT.Copy).then_inc(S["y_hi"], 1)

        def pm_hi(i):
            g, hf = GORDER[i // 2], i % 2
            act.activation(HT[:, HI, 4 + g, half(hf)], HTf[:, 4 + g, half(hf)], ACT.Copy).then_inc(S["pm_hi"], 1)

        act.wait_ge(S["pm_y"], 8)
        for n_ in range(NT):
            for h in range(HEADS + 1):
                if n_ == 0 and h == HEADS:
                    turned_hi(0, 0)
                elif n_ >= 1 and h < HEADS and n_ + h > 1:
                    turned_hi(n_ - 1, h)
                if h >= 1:
                    softmax_exp(n_, BLOCKS[n_], h - 1)
                    normalise(4 * n_ + h - 2)
            if n_ >= 2:
                out_hi(n_ - 2)
            if n_ >= 1:
                for i in PM_IN_BLOCK[n_]:
                    pm_hi(i)
                latent_hi(n_ - 1)
        normalise(4 * NT - 1)
        for h in range(HEADS):
            turned_hi(NT - 1, h)
        out_hi(NT - 2)
        latent_hi(NT - 1)
        out_hi(NT - 1)
        act.wait_ge(S["op_done"], NT)
        for k in WO1_ORDER:
            act.wait_ge(wo_in[k % 4], 48)
            act.activation(WOhi[1][k], WOraw[1][k], ACT.Copy).then_inc(S["wo_hi"], 1)

        def squares2(t):
            act.wait_ge(S["x_new"], NT + t + 1)
            if t == 0:
                act.wait_ge(S["acc_done"], 15)
            act.activation(JUNK2[:], X[:, t, :], ACT.Square, accum_out=SS2[:, t:t + 1]).then_inc(S["ss2"], 1)
            act.wait_ge(S["ss2"], t + 1)

        def modulate2(t):
            act.wait_ge(S["t2"], t + 1)
            act.wait_ge(S["modcols"], 2)
            for k in range(KT):
                bank = 4 + 2 * (t % 2) + k // 4
                last = act.activation(HTf[:, k, tok(t)], PS[:, bank, (k % 4) * P:(k % 4 + 1) * P], ACT.Identity,
                                      scale=G2[:, k:k + 1], bias=MOD[:, 16 + k:17 + k])
            last.then_inc(S["ev2"], 1)

        def wgu_hi(i, s):
            act.wait_ge(wgu_in[s], 32 * i + 32)
            act.activation(WGU[:, s, HI].rearrange("p a k n -> p (a k n)"),
                           WGUraw[:, s, LO].rearrange("p a k n -> p (a k n)"), ACT.Copy).then_inc(S["wgu_hi"], 1)

        def wd_hi(i, rows=WD, raw=WDraw):
            act.wait_ge(S["wd_fold"], i + 1)
            act.activation(flat(rows[:, HI]), flat(raw[:]), ACT.Copy).then_inc(S["wd_hi"], 1)

        for t in range(NT):
            squares2(t)
            if t >= 2:
                modulate2(t - 2)
            if t in (4, 6):
                wgu_hi(0, t // 2 - 2)
        modulate2(NT - 2)
        modulate2(NT - 1)

        def chunk_act(i, par, more=True):
            first = isinstance(i, int) and i == 0
            if not first:
                wgu_hi(i, 1)
            for hf in range(2):
                for s in range(2):
                    m = 4 * i + 2 * hf + s
                    act.wait_ge(S["gu_half"], m + 1)
                    if not isinstance(m, int) or m >= 2:
                        act.wait_ge(S["act_ready"], m - 1)
                    act.activation(HID[:, s], PS[:, 2 * s, :], ACT.Silu).then_inc(S["silu"], 1)
                    act.wait_ge(S["hid"], m + 1)
                    act.activation(ACTS[:, 2 * par + s, HI, half(hf)], HID[:, s], ACT.Copy).then_inc(S["act_hi"], 1)
                    if hf == 1 and s == 0:
                        if first:
                            wgu_hi(i + 1, 0)
                        else:
                            wd_hi(i - 1)
            if more and not first:
                wgu_hi(i + 1, 0)

        chunk_act(0, 0)
        with act.Fori(0, (NC - 3) // 2) as j:
            for par in (1, 0):
                chunk_act(2 * j + (1 if par else 2), par)
        chunk_act(NC - 2, (NC - 2) % 2)
        chunk_act(NC - 1, (NC - 1) % 2, more=False)
        wd_hi(NC - 1, WD2, WD2raw)

        def scale_out(t):
            act.wait_ge(S["rs3"], 1 if t < 4 else 3)
            act.wait_ge(S["x_gain"], t + 1)
            act.activation(XG[:, t, :], XG[:, t, :], ACT.Copy, scale=RS3[:, t:t + 1]).then_inc(S["fin"], 1)

        def squares3(t):
            act.wait_ge(S["d_free"], 4 + 16 * (NC - 1) + 2 * t + 2)
            act.activation(JUNK2[:], X[:, t, :], ACT.Square, accum_out=SS3[:, t:t + 1]).then_inc(S["ss3"], 1)
            act.wait_ge(S["ss3"], t + 1)

        for t in range(6):
            squares3(t)
        for t in range(3):
            scale_out(t)
        squares3(6)
        scale_out(3)
        squares3(7)
        scale_out(6)

    @block.vector
    def _(dve):
        n = 0

        def then(ins):
            nonlocal n
            n += 1
            ins.then_inc(S["dve_step"], 1)
            dve.wait_ge(S["dve_step"], n)

        def inverse_root(res, ss, cols, width, done):
            v, r, rt, ri = VAR[:, 0:cols], RS[:, 0:cols], RT[:, 0:cols], RI[:, 0:cols]
            if res is not None:
                r = res
            then(dve.tensor_scalar(v, ss, 1.0 / width, EPS, ALU.mult, ALU.add))
            if cols == 1:
                dve.tensor_scalar(VHALF[:], v, -0.5, None, ALU.mult)
            then(dve.tensor_scalar(ri, v.bitcast(I32), 1, None, ALU.logical_shift_right))
            then(dve.tensor_scalar(r.bitcast(I32), ri, -1.0, RSQRT_MAGIC, ALU.mult, ALU.add))
            for step in range(3):
                if cols == 1:
                    then(dve.tensor_scalar(rt, r, r, VHALF[:], ALU.mult, ALU.mult))
                else:
                    then(dve.tensor_tensor(rt, r, r, ALU.mult))
                    then(dve.scalar_tensor_tensor(rt, rt, -0.5, v, ALU.mult, ALU.mult))
                ins = dve.scalar_tensor_tensor(r, rt, 1.5, r, ALU.add, ALU.mult)
                if step < 2:
                    then(ins)
            ins.then_inc(done, 1)

        def accumulate(j):
            buf, s, v = ada_piece(j)
            o_, kh = divmod(j, 2)
            ch = DVE_CHUNKS[o_]
            dve.wait_ge(s, v)
            gate_sum = ch in (4, 5, 10, 11)
            if gate_sum:
                dve.wait_ge(S["gt_in"], 32)
                acc = (GT1 if ch < 6 else GT2)[:, half(ch % 2)]
            else:
                acc = ACC[:, ch % 2]
                if kh == 0 and o_ >= 2:
                    dve.wait_ge(S["colsum"], o_ - 1)
            for t in range(4):
                cs = CS[:, 4 * kh + t:4 * kh + t + 1]
                if not gate_sum and kh == 0 and t == 0:
                    ins = dve.tensor_scalar(acc, buf[:, t, :], cs, None, ALU.mult)
                else:
                    ins = dve.scalar_tensor_tensor(acc, buf[:, t, :], cs, acc, ALU.mult, ALU.add)
                if t < 3:
                    then(ins)
            ins.then_inc(S["acc_done"], 1)
            dve.wait_ge(S["acc_done"], j + 1)

        def xn1(t):
            dve.tensor_scalar(X[:, t, :], X[:, t, :], RS[:, t:t + 1], None, ALU.mult).then_inc(S["xn1"], 1)

        def lo(out_, full, hi, ready):
            dve.tensor_tensor(out_, full, hi.bitcast(F32), ALU.subtract).then_inc(ready, 1)

        dve.wait_ge(S["act_silu"], 1)
        accumulate(0)
        dve.wait_ge(S["pos_in"], 16)
        dve.wait_ge(S["freq_in"], 16)
        then(dve.tensor_copy(POSF[:], POSI[:]))
        for t in range(NT):
            ins = dve.tensor_scalar(ANG[:, t, :], FREQ[:], POSF[:, t:t + 1], None, ALU.mult)
        then(ins)
        for turns in (4096.0, 1.0):
            then(dve.tensor_scalar(TURN[:], ANG[:], float(1 / (2 * np.pi * turns)), ROUND_MAGIC, ALU.mult, ALU.add))
            then(dve.tensor_scalar(TURN[:], TURN[:], -ROUND_MAGIC, None, ALU.add))
            for part in two_pi_parts():
                ins = dve.scalar_tensor_tensor(ANG[:], TURN[:], -part * turns, ANG[:], ALU.mult, ALU.add)
                then(ins)
        dve.sem_inc(S["ang_ready"], 1)

        for j in range(1, 4):
            accumulate(j)
        dve.wait_ge(S["rowsT"], 1)
        dve.tensor_copy(COLS[:], PS[:, 6, 0:N_ROWS])

        def roots1(t0):
            dve.wait_ge(S["ss1"], t0 + 2)
            inverse_root(RS[:, t0:t0 + 2], SS[:, t0:t0 + 2], 2, D, S["rs1"])
            dve.wait_ge(S["rs1"], t0 // 2 + 1)
            xn1(t0)
            xn1(t0 + 1)

        def h_lo(t):
            dve.wait_ge(S["h_hi"], t + 1)
            lo(HT[:, LO, :, tok(t)], HTf[:, :, tok(t)], HT[:, HI, :, tok(t)], S["h_ready"])

        roots1(0)
        dve.wait_ge(S["colsum"], 2)
        dve.wait_ge(S["sh1_sum"], 1)
        then(dve.tensor_tensor(MOD[:, 0:16], PS[:, 7, 0:16], COLS[:, 0:16], ALU.add))
        dve.scalar_tensor_tensor(G1[:], MOD[:, 8:16], 1.0, COLS[:, ROW_MIX:ROW_MIX + 8], ALU.add, ALU.mult).then_inc(S["modcols"], 1)
        for i in range(4):
            if i == 1:
                roots1(2)
            if i == 2:
                h_lo(0)
            dve.wait_ge(S["wtm_hi"], i + 1)
            lo(flat(WTM[:, LO, 2 * i:2 * i + 2, :]), flat(WTMraw[:, 2 * i:2 * i + 2, :]),
               flat(WTM[:, HI, 2 * i:2 * i + 2, :]), S["wtm_ready"])
        for t in range(1, NT):
            h_lo(t)
            if t in (1, 3):
                roots1(t + 3)

        def wu_lo(g):
            dve.wait_ge(S["wu_hi"], g + 1)
            lo(flat(WU[:, g % 2, LO]), flat(WUraw[:, g % 2, LO]), flat(WU[:, g % 2, HI]), S["wu_ready"])

        def gate(n_):
            dve.wait_ge(S["colsum"], (3, 4, 9, 10)[n_])
            gt = GT1 if n_ < 2 else GT2
            dve.tensor_copy(gt[:, half(n_ % 2)], PS[:, 6 + n_ % 2 if n_ < 2 else 4 + n_ % 2, :]).then_inc(S["gt_ready"], 1)

        wu_lo(0)
        wu_lo(1)
        accumulate(4)
        accumulate(5)
        dve.wait_ge(S["sin_ready"], 1)
        then(dve.tensor_tensor(COS[:], SHALF[:], SHALF[:], ALU.mult))
        then(dve.tensor_scalar(COS[:], COS[:], -2.0, 1.0, ALU.mult, ALU.add))
        then(dve.tensor_tensor(SIN[:], SQUART[:], SQUART[:], ALU.mult))
        then(dve.tensor_scalar(SIN[:], SIN[:], -4.0, 2.0, ALU.mult, ALU.add))
        dve.tensor_tensor(SIN[:], SIN[:], SHALF[:], ALU.mult).then_inc(S["trig_ready"], 1)
        dve.wait_ge(S["tm_out"], NT)
        inverse_root(None, SS[:, 0:8], 8, QR, S["rs1"])
        dve.wait_ge(S["rs1"], 5)
        dve.wait_ge(S["gq_in"], 16)
        dve.wait_ge(S["gkv_in"], 16)
        for t in range(NT):
            ins = dve.scalar_tensor_tensor(TMO[:, t, 0:QR], TMO[:, t, 0:QR], RS[:, t:t + 1], GQ[:], ALU.mult, ALU.mult)
        then(ins)
        inverse_root(None, SS[:, 8:16], 8, LAT, S["rs1"])
        dve.wait_ge(S["rs1"], 6)
        for t in range(NT):
            dve.scalar_tensor_tensor(TMO[:, t, QR:QR + LAT], TMO[:, t, QR:QR + LAT], RS[:, t:t + 1], GKV[:],
                                     ALU.mult, ALU.mult).then_inc(S["tm_norm"], 1)
        dve.wait_ge(S["ckv_hi"], 1)
        lo(CKV[:, LO], TMO[:, :, QR:QR + LAT], CKV[:, HI], S["ckv_ready"])
        accumulate(6)
        accumulate(7)

        def lt_lo(t):
            dve.wait_ge(S["lt_hi"], t + 1)
            b = 2 + t % 4
            dve.tensor_tensor(LT[:, :, LO, tok(t)], PS[:, b, 0:3 * P].rearrange("p (k n) -> p k n", k=3),
                              LT[:, :, HI, tok(t)].bitcast(F32), ALU.subtract)
            lo(KRT[:, LO, tok(t)], PS[:, b, 3 * P:], KRT[:, HI, tok(t)], S["lt_lo"])

        def pooled(i):
            g = GORDER[i]
            dve.wait_ge(S["windowed"], i + 1)
            sums = WIN[:, (0, 1, 0, 1)[g], PADW:]
            dve.scalar_tensor_tensor(U[:, g, PADW:], sums, 1.0 / 2 ** (g + 1), U[:, g, PADW:],
                                     ALU.mult, ALU.subtract).then_inc(S["pooled"], 1)

        lt_lo(0)
        lt_lo(1)
        wu_lo(2)
        lt_lo(2)
        lt_lo(3)
        dve.wait_ge(S["wp_hi"], 1)
        lo(flat(WP[:, LO]), flat(WPraw[:]), flat(WP[:, HI]), S["wp_ready"])
        dve.wait_ge(S["wuv_hi"], 1)
        lo(flat(WUV[:, LO]), flat(WUVraw[:]), flat(WUV[:, HI]), S["wuv_ready"])
        gate(0)
        gate(1)
        wu_lo(3)
        pooled(0)
        for t in range(4, NT):
            lt_lo(t)
            if t == 5:
                pooled(1)
        dve.wait_ge(S["wuq_hi"], 1)
        lo(WUQ[:, LO].rearrange("p k h d -> p (k h d)"), WUQraw[:].rearrange("p k h d -> p (k h d)"),
           WUQ[:, HI].rearrange("p k h d -> p (k h d)"), S["wuq_ready"])
        pooled(2)

        def pool_lo(i):
            g = GORDER[i]
            dve.wait_ge(S["pool_hi"], i + 1)
            lo(UR[:, g, PADW:], U[:, g, PADW:], POOLHI[:, g], S["pool_lo"])

        pool_lo(0)
        pool_lo(1)
        pooled(3)
        dve.wait_ge(S["wuk_hi"], 1)
        lo(WUK[:, LO].rearrange("p h c -> p (h c)"), PS[:, 6, :], WUK[:, HI].rearrange("p h c -> p (h c)"), S["wuk_ready"])
        pool_lo(2)
        pool_lo(3)

        def pm_lo(m):
            g, hf = GORDER[m // 2], m % 2
            dve.wait_ge(S["pm_hi"], m + 1)
            lo(HT[:, LO, 4 + g, half(hf)], HTf[:, 4 + g, half(hf)], HT[:, HI, 4 + g, half(hf)], S["pm_lo"])

        def ql_lo(i):
            hf, h = 1 - i // 4, i % 4
            dve.wait_ge(S["ql_hi"], i + 1)
            lo(QLlo[:, h, half(hf)], PS[:, 6 + i % 2, :], QLhi[:, h, half(hf)], S["ql_lo"])

        for i, t in enumerate(BLOCKS):
            dve.wait_ge(S["qn_hi"], i + 1)
            lo(QN[:, i % 2, LO], PS[:, 4 + i % 2, :], QN[:, i % 2, HI], S["qn_lo"])
            if i >= 1:
                ql_lo(i - 1)
            dve.wait_ge(S["qr_hi"], i + 1)
            lo(QS[ROPE:P, :, tok(t)], PS[ROPE:P, 2 + i % 2, :].rearrange("p (h n) -> p h n", h=HEADS),
               QS[ROPE:P, :, tok(t)], S["qr_lo"])

        def row_max(n_, h):
            m = 4 * n_ + h
            dve.wait_ge(S["s_done"], m + 1)
            sl = 2 * (h % 2)
            then(dve.tensor_reduce(NEGM[:, m:m + 1], flat(PS[:, sl:sl + 2, :])[:, 0:(BLOCKS[n_] + 1) * P], AX.X, ALU.max))
            dve.tensor_scalar(NEGM[:, m:m + 1], NEGM[:, m:m + 1], -SCALE, None, ALU.mult).then_inc(S["negmax"], 1)

        def inv_sum(m):
            if m < 0:
                return
            dve.wait_ge(S["exp_done"], m + 1)
            dve.reciprocal(RSUM[:, m:m + 1], SUM[:, m:m + 1]).then_inc(S["rsum"], 1)

        def turned_lo(n_, h):
            for q, j0, nj in units(n_, h):
                dve.wait_ge(S["pt_hi"], q + 1)
                dve.tensor_tensor(PT[:, LO, j0:j0 + nj, h, :],
                                  PS[:, 4 + q % 2, 0:nj * P].rearrange("p (j n) -> p j n", j=nj),
                                  PT[:, HI, j0:j0 + nj, h, :].bitcast(F32), ALU.subtract).then_inc(S["pt_lo"], 1)

        def latent_lo(n_):
            dve.wait_ge(S["ol_hi"], n_ + 1)
            lo(OL[:, LO], PS[:, 6, :], OL[:, HI], S["ol_lo"])

        def out_lo(n_):
            dve.wait_ge(S["y_hi"], n_ + 1)
            t = tok(BLOCKS[n_])
            lo(HT[:, LO, 0:HEADS, t], PS[:, 7, :].rearrange("p (h n) -> p h n", h=HEADS), HT[:, HI, 0:HEADS, t], S["y_lo"])

        for n_ in range(NT):
            for h in range(HEADS + 1):
                if h >= 1:
                    row_max(n_, h - 1)
                    if n_ == 0 and h == 1:
                        ql_lo(NT - 1)
                    inv_sum(4 * n_ + h - 2)
                if n_ >= 1 and h < HEADS:
                    turned_lo(n_ - 1, h)
            if n_ >= 2:
                out_lo(n_ - 2)
            if n_ >= 1:
                for i in PM_IN_BLOCK[n_]:
                    pm_lo(i)
                latent_lo(n_ - 1)
        inv_sum(4 * NT - 1)
        for h in range(HEADS):
            turned_lo(NT - 1, h)
        out_lo(NT - 2)
        latent_lo(NT - 1)

        def wo_lo(j):
            k = WO1_ORDER[j]
            dve.wait_ge(S["wo_hi"], KT + j + 1)
            lo(WOlo[1][k], WOraw[1][k], WOhi[1][k], S["wo_ready"])

        def gated(m, c_):
            dve.wait_ge(S["mix_done"], m + 1)
            if m >= 2:
                dve.wait_ge(S["x_new"], m - 1)
            dve.tensor_tensor(MIX[m % 2][:], PS[:, m % 4, :], GT1[:, half(c_)], ALU.mult).then_inc(S["mix_gated"], 1)

        for m in range(NT):
            gated(m, 0)
            if m == 0:
                out_lo(NT - 1)
            if 2 <= m < 6:
                wo_lo(2 * m - 4)
                wo_lo(2 * m - 3)
            if m >= 2:
                accumulate(6 + m)

        def wgu_lo(i, s):
            dve.wait_ge(S["wgu_hi"], 2 * i + s + 1)
            dve.tensor_tensor(WGU[:, s, LO].rearrange("p a k n -> p (a k n)"),
                              WGUraw[:, s, LO].rearrange("p a k n -> p (a k n)"),
                              WGU[:, s, HI].bitcast(F32).rearrange("p a k n -> p (a k n)"), ALU.subtract).then_inc(S["wgu_ready"], 1)

        def h2_lo(t):
            dve.wait_ge(S["h2_hi"], t + 1)
            lo(HT[:, LO, :, tok(t)], HTf[:, :, tok(t)], HT[:, HI, :, tok(t)], S["h2_ready"])

        def xn2(t):
            dve.wait_ge(S["ss2"], t + 1)
            inverse_root(RS2[:, t:t + 1], SS2[:, t:t + 1], 1, D, S["rs2"])
            dve.wait_ge(S["rs2"], t + 1)
            if t >= 2:
                dve.wait_ge(S["t2"], t - 1)
            dve.tensor_scalar(XN[:, t % 2], X[:, t, :], RS2[:, t:t + 1], None, ALU.mult).then_inc(S["xn2"], 1)

        for t in range(NT):
            gated(NT + t, 1)
            if t == 3:
                dve.wait_ge(S["colsum"], 8)
                then(dve.tensor_tensor(MOD[:, 16:32], PS[:, 7, 16:32], COLS[:, 24:40], ALU.add))
                dve.scalar_tensor_tensor(G2[:], MOD[:, 24:32], 1.0, COLS[:, ROW_FFN:ROW_FFN + 8],
                                         ALU.add, ALU.mult).then_inc(S["modcols"], 1)
            if t >= 1:
                xn2(t - 1)
            if t < 2:
                accumulate(14 + t)
            if t >= 3:
                h2_lo(t - 3)
            if t == 6:
                wgu_lo(0, 0)
        xn2(NT - 1)
        h2_lo(NT - 3)
        wgu_lo(0, 1)
        h2_lo(NT - 2)
        h2_lo(NT - 1)

        def hid(m, r):
            dve.wait_ge(S["silu"], m + 1)
            dve.tensor_tensor(HID[:, r], HID[:, r], PS[:, 2 * r + 1, :], ALU.mult).then_inc(S["hid"], 1)

        def act_lo(m, r, slot, hf):
            dve.wait_ge(S["act_hi"], m + 1)
            lo(ACTS[:, slot, LO, half(hf)], HID[:, r], ACTS[:, slot, HI, half(hf)], S["act_ready"])

        def wd_lo(i, rows=WD, raw=WDraw):
            dve.wait_ge(S["wd_hi"], i + 1)
            lo(flat(rows[:, LO]), flat(raw[:]), flat(rows[:, HI]), S["wd_ready"])

        def add_down(i, wgu_next=False):
            for m in range(2 * NT):
                if m == 3 and wgu_next:
                    wgu_lo(i + 2, 0)
                if m == 10 and not wgu_next:
                    wd_lo(NC - 1, WD2, WD2raw)
                t, c_ = divmod(m, 2)
                dve.wait_ge(S["d_bank"], 16 * i + m + 1)
                dve.tensor_tensor(X[:, t, half(c_)], PS[:, 4 + m % 4, :], X[:, t, half(c_)], ALU.add).then_inc(S["d_free"], 1)

        def chunk_dve(i, par, more=True):
            first = isinstance(i, int) and i == 0
            if not first:
                wgu_lo(i, 1)
            for hf in range(2):
                for s in range(2):
                    m = 4 * i + 2 * hf + s
                    hid(m, s)
                    act_lo(m, s, 2 * par + s, hf)
                    if hf == 1 and s == 0:
                        if first:
                            wgu_lo(i + 1, 0)
                        else:
                            wd_lo(i - 1)
                    if first and m < 2:
                        accumulate(16 + 2 * m)
                        accumulate(17 + 2 * m)
            if not first:
                add_down(i - 1, wgu_next=more)

        chunk_dve(0, 0)
        gate(2)
        gate(3)
        dve.sem_inc(S["d_free"], 4)
        with dve.Fori(0, (NC - 3) // 2) as j:
            for par in (1, 0):
                chunk_dve(2 * j + (1 if par else 2), par)
        chunk_dve(NC - 2, (NC - 2) % 2)
        chunk_dve(NC - 1, (NC - 1) % 2, more=False)

        def roots3(t0, n_):
            dve.wait_ge(S["ss3"], t0 + n_)
            inverse_root(RS3[:, t0:t0 + n_], SS3[:, t0:t0 + n_], n_, D, S["rs3"])

        for m in range(2 * NT):
            t, c_ = divmod(m, 2)
            dve.wait_ge(S["d_bank"], 16 * (NC - 1) + m + 1)
            dve.tensor_tensor(X[:, t, half(c_)], PS[:, 4 + m % 4, :], X[:, t, half(c_)], ALU.add).then_inc(S["d_free"], 1)
            if m == 9:
                roots3(0, 4)
            elif m == 12:
                roots3(4, 2)

        def scale_out(t):
            dve.wait_ge(S["rs3"], 3 if t == 7 else 2)
            dve.wait_ge(S["x_gain"], t + 1)
            dve.tensor_scalar(XG[:, t, :], XG[:, t, :], RS3[:, t:t + 1], None, ALU.mult).then_inc(S["fin_dve"], 1)

        scale_out(4)
        scale_out(5)
        roots3(6, 2)
        scale_out(7)

    @block.tensor
    def _(pe):
        def product(ps, terms):
            terms = list(terms)
            for n_, (l, r) in enumerate(terms):
                ins = pe.matmul(ps, l, r, start=(n_ == 0), stop=(n_ == len(terms) - 1))
            return ins

        pe.wait_ge(S["pool_const"], 1)
        def col_sum(o_):
            ch = DVE_CHUNKS[o_]
            pe.wait_ge(S["acc_done"], 2 * o_ + 2)
            if ch in (4, 5, 10, 11):
                gt, bank = (GT1, 6 + ch % 2) if ch < 6 else (GT2, 4 + ch % 2)
                if ch == 4:
                    pe.wait_ge(S["modcols"], 1)
                pe.matmul(PS[:, bank, :], ONES[:], gt[:, half(ch % 2)], start=True, stop=True).then_inc(S["colsum"], 1)
                return
            col = 4 * ch if ch < 4 else 16 + 4 * (ch - 6)
            for j in range(4):
                ins = pe.matmul(PS[:, 7, col + j:col + j + 1], ACC[:, ch % 2, j * P:(j + 1) * P], ONES[:, 0:1], start=True, stop=True)
            ins.then_inc(S["colsum"], 1)

        pe.wait_ge(S["rows_in"], 64)
        pe.transpose(PS[:, 6, 0:N_ROWS], ROWS[0:N_ROWS, :], IDENT[0:N_ROWS, 0:N_ROWS]).then_inc(S["rowsT"], 1)
        pe.wait_ge(S["act_silu"], 1)
        for ch in range(2):
            for t in range(KT):
                if t % 4 == 0:
                    pe.wait_ge(sh1_in[2 * ch + t // 4], 16)
                ins = pe.matmul(PS[0:1, 4 + ch, :], CS[:, t:t + 1], ADAS[:, 2 * ch + t // 4, t % 4, :], start=(t == 0), stop=(t == KT - 1))
        ins.then_inc(S["sh1_rows"], 1)
        col_sum(0)
        pe.wait_ge(S["sh1_out"], 1)
        for k in range(KT):
            ins = pe.matmul(PS[:, 7, k:k + 1], SHROW[0:1, k // 4, (k % 4) * P:(k % 4 + 1) * P], ONES[0:1, 0:1], start=True, stop=True)
        ins.then_inc(S["sh1_sum"], 1)
        col_sum(1)

        def turn_x1(t):
            pe.wait_ge(S["xn1"], t + 1)
            if t >= 2:
                pe.wait_ge(S["hmod"], t - 1)
            for k in range(KT):
                ins = pe.transpose(PS[:, 2 * (t % 2) + k // 4, (k % 4) * P:(k % 4 + 1) * P], X[:, t, k * P:(k + 1) * P], IDENT[:])
            ins.then_inc(S["t1"], 1)

        turn_x1(0)
        turn_x1(1)
        for t in range(NT):
            if t < NT - 2:
                turn_x1(t + 2)
            pe.wait_ge(S["h_ready"], t + 1)
            if t >= 2:
                pe.wait_ge(S["tm_out"], t - 1)
            for k in range(KT):
                if t == 0 and k % 2 == 0:
                    pe.wait_ge(S["wtm_ready"], k // 2 + 1)
                for p, (a, b) in enumerate(PASSES):
                    ins = pe.matmul(PS[:, 4 + t % 2, 0:TM], HT[:, a, k, tok(t)], WTM[:, b, k, :],
                                    start=(k == 0 and p == 0), stop=(k == KT - 1 and p == 2))
            ins.then_inc(S["tm_done"], 1)

        def pool_group(i):
            pe.wait_ge(S["wu_ready"], i + 1)
            for hf in range(2):
                if i >= 1:
                    pe.wait_ge(S["u_out"], 2 * i - 1 + hf)
                product(PS[:, hf, :], [(WU[:, i % 2, a, k, :], HT[:, b, k, half(hf)]) for k in range(KT) for a, b in PASSES]
                        ).then_inc(S["u_done"], 1)

        def turn_latents(t):
            pe.wait_ge(S["tm_norm"], NT)
            pe.wait_ge(S["kr_ready"], 1)
            if t >= 4:
                pe.wait_ge(S["lt_lo"], t - 3)
            for i, c0 in enumerate((0, P, QR, QR + LAT)):
                ins = pe.transpose(PS[:, 2 + t % 4, i * P:(i + 1) * P], TMO[:, t, c0:c0 + P], IDENT[:])
            ins.then_inc(S["lt_T"], 1)

        pool_group(0)
        pool_group(1)
        for t in range(4):
            turn_latents(t)
        col_sum(2)
        col_sum(3)
        pool_group(2)
        for t in range(4, NT):
            turn_latents(t)
        pe.wait_ge(S["wuk_in"], 16)
        pe.wait_ge(S["gt_ready"], 2)
        for h in range(HEADS):
            ins = pe.transpose(PS[:, 6, h * P:(h + 1) * P], WUKraw[:, h, :], IDENT[:])
        ins.then_inc(S["wukT"], 1)
        pool_group(3)

        pe.wait_ge(S["wuq_ready"], 1)
        pe.wait_ge(S["lt_lo"], NT)
        for i, t in enumerate(BLOCKS):
            if i >= 2:
                pe.wait_ge(S["qr_raw"], i - 1)
            product(PS[:, 2 + i % 2, 0:HEADS * ROPE].rearrange("p (h d) -> p h d", h=HEADS),
                    [(LT[:, k, a, tok(t)], WUQ[:, b, k, :, NOPE:]) for k in range(2) for a, b in PASSES]).then_inc(S["qr_done"], 1)

        pe.wait_ge(S["wp_ready"], 1)
        pe.wait_ge(S["u_out"], 2 * GROUPS)
        pool_parts = {HI: POOLHI, LO: UR}
        for m in range(2 * GROUPS):
            g, hf = GORDER[m // 2], m % 2
            pe.wait_ge(S["pool_lo"], m // 2 + 1)
            if m >= 2:
                pe.wait_ge(S["pm_y"], m - 1)
            product(PS[:, m % 2, :], [(WP[:, a, g, :], POOLHI[:, g, half(hf)] if b == HI else UR[:, g, PADW + hf * HALF:PADW + (hf + 1) * HALF])
                                      for a, b in PASSES]).then_inc(S["pm_done"], 1)

        def q_nope(i):
            hf, h = 1 - i // 4, i % 4
            if i == 0:
                pe.wait_ge(S["wuk_ready"], 1)
            if i >= 2:
                pe.wait_ge(S["qn_lo"], i - 1)
            product(PS[:, 4 + i % 2, :], [(WUQ[:, a, k, h, 0:NOPE], LT[:, k, b, half(hf)]) for k in range(2) for a, b in PASSES]
                    ).then_inc(S["qn_done"], 1)

        def q_latent(i):
            h = i % 4
            pe.wait_ge(S["qn_lo"], i + 1)
            if i >= 2:
                pe.wait_ge(S["ql_lo"], i - 1)
            product(PS[:, 6 + i % 2, :], [(WUK[:, a, h, :], QN[:, i % 2, b, :]) for a, b in PASSES]).then_inc(S["ql_done"], 1)

        def turn_rope(i):
            pe.wait_ge(S["qr_dup"], i + 1)
            pe.wait_ge(S["qr_raw"], NT)
            if i >= 2:
                pe.wait_ge(S["qr_lo"], i - 1)
            for h in range(HEADS):
                ins = pe.transpose(PS[:, 2 + i % 2, h * P:(h + 1) * P], QRD[:, i % 3, h].rearrange("p a d -> p (a d)"), IDENT[:])
            ins.then_inc(S["qr_T"], 1)

        for i in range(NT):
            q_nope(i)
            if i >= 1:
                q_latent(i - 1)
            turn_rope(i)
        QL = (QLhi, QLlo)

        def scores(n_, h):
            b = BLOCKS[n_]
            m = 4 * n_ + h
            if m == 0:
                pe.wait_ge(S["ql_lo"], 4)
                pe.wait_ge(S["qr_lo"], 4)
                pe.wait_ge(S["pm_y"], 8)
            elif m == 1:
                pe.wait_ge(S["qr_lo"], NT)
            elif m == 16:
                pe.wait_ge(S["ql_lo"], 8)
            if m >= 2:
                pe.wait_ge(S["exp_done"], m - 1)
            for c0 in range(0, b + 1, 4):
                nk = min(4, b + 1 - c0)
                ks = slice(c0 * P, (c0 + nk) * P)
                bank = PS[:, 2 * (h % 2) + c0 // 4, 0:nk * P]
                q = tok(b)
                terms = [(QL[a_][:, h, q], LT[:, 2, b_, ks]) for a_, b_ in PASSES]
                terms += [(QS[:, h, q], KRT[:, a_, ks]) for a_ in (HI, LO)]
                diag = c0 + nk == b + 1
                for z, (l, r) in enumerate(terms):
                    ins = pe.matmul(bank, l, r, start=(z == 0), stop=(z == 4 and not diag))
                if diag:
                    ins = pe.matmul(bank[:, (nk - 1) * P:nk * P], MASKQ[:], MASKK[:], start=False, stop=True)
            ins.then_inc(S["s_done"], 1)

        def turn_p(n_, h):
            pe.wait_ge(S["p_norm"], 4 * n_ + h + 1)
            for q, j0, nj in units(n_, h):
                if q >= 2:
                    pe.wait_ge(S["pt_lo"], q - 1)
                for j in range(nj):
                    ins = pe.transpose(PS[:, 4 + q % 2, j * P:(j + 1) * P], PR[:, h, (j0 + j) * P:(j0 + j + 1) * P], IDENT[:])
                ins.then_inc(S["p_T"], 1)

        def values(n_):
            b = BLOCKS[n_]
            pe.wait_ge(S["ckv_ready"], 1)
            pe.wait_ge(S["pt_lo"], units_done(n_, HEADS - 1))
            if n_ >= 1:
                pe.wait_ge(S["ol_lo"], n_)
            product(PS[:, 6, :], [(CKV[:, a_, j, :], PT[:, b_, j].rearrange("p h n -> p (h n)"))
                                  for j in range(b + 1) for a_, b_ in PASSES]).then_inc(S["pv_done"], 1)

        def up_values(n_):
            pe.wait_ge(S["wuv_ready"], 1)
            pe.wait_ge(S["ol_lo"], n_ + 1)
            if n_ >= 1:
                pe.wait_ge(S["y_lo"], n_)
            for h in range(HEADS):
                ins = product(PS[:, 7, h * P:(h + 1) * P], [(WUV[:, a_, h, :], OL[:, b_, h * P:(h + 1) * P]) for a_, b_ in PASSES])
            ins.then_inc(S["op_done"], 1)

        for n_ in range(NT):
            for h in range(HEADS):
                if n_ >= 1:
                    turn_p(n_ - 1, h)
                scores(n_, h)
                if n_ == 0 and h == 0:
                    q_latent(NT - 1)
            if n_ >= 2:
                up_values(n_ - 2)
            if n_ >= 1:
                values(n_ - 1)
        def mix(m):
            c_, t = (0, BLOCKS[m]) if m < NT else (1, m - NT)
            if c_ == 0:
                pe.wait_ge(S["y_lo"], m + 1)
            if m == 0:
                pe.wait_ge(S["pm_lo"], 8)
                pe.wait_ge(S["exp_done"], 4 * NT)
            pe.wait_ge(S["wo_ready"], KT * (c_ + 1))
            if m >= 4:
                pe.wait_ge(S["mix_gated"], m - 3)
            W = {HI: WOhi[c_], LO: WOlo[c_]}
            product(PS[:, m % 4, :], [(HT[:, a_, k, tok(t)], W[b_][k]) for k in range(KT) for a_, b_ in PASSES]
                    ).then_inc(S["mix_done"], 1)

        def turn_x(t):
            pe.wait_ge(S["xn2"], t + 1)
            if t == 1:
                pe.wait_ge(S["modcols"], 2)
            if t >= 2:
                pe.wait_ge(S["ev2"], t - 1)
            for k in range(KT):
                ins = pe.transpose(PS[:, 4 + 2 * (t % 2) + k // 4, (k % 4) * P:(k % 4 + 1) * P], XN[:, t % 2, k * P:(k + 1) * P], IDENT[:])
            ins.then_inc(S["t2"], 1)

        mix(0)
        for h in range(HEADS):
            turn_p(NT - 1, h)
        up_values(NT - 2)
        mix(1)
        values(NT - 1)
        mix(2)
        up_values(NT - 1)
        for m in range(3, 2 * NT):
            mix(m)
            if m in (6, 8, 9):
                col_sum({6: 4, 8: 5, 9: 6}[m])
            if m >= NT + 2:
                if m == NT + 3:
                    col_sum(7)
                turn_x(m - NT - 2)

        def gate_up(i, s, hf, first=False):
            if hf == 0:
                pe.wait_ge(S["wgu_ready"], 2 * i + s + 1)
            m = 4 * i + 2 * hf + s
            if not first:
                pe.wait_ge(S["hid"], m - 1)
            for a in range(2):
                ins = product(PS[:, 2 * s + a, :], [(WGU[:, s, w_, a, k, :], HT[:, h_, k, half(hf)])
                                                    for k in range(KT) for w_, h_ in PASSES])
            ins.then_inc(S["gu_half"], 1)

        def down(i, par, rows=WD):
            pe.wait_ge(S["wd_ready"], i + 1)
            pe.wait_ge(S["act_ready"], 4 * i + 4)
            for m in range(2 * NT):
                t, c_ = divmod(m, 2)
                pe.wait_ge(S["d_free"], 16 * i + m + 1)
                product(PS[:, 4 + m % 4, :], [(ACTS[:, 2 * par + s, a_, tok(t)], rows[:, b_, s, half(c_)])
                                              for s in range(2) for a_, b_ in PASSES]).then_inc(S["d_bank"], 1)

        pe.wait_ge(S["h2_ready"], 4)
        for s in range(2):
            pe.wait_ge(S["mix_gated"], 2 * NT - 2 + 2 * s)
            gate_up(0, s, 0, first=True)
            if s == 0:
                turn_x(NT - 2)
                turn_x(NT - 1)
        pe.wait_ge(S["h2_ready"], NT)
        for s in range(2):
            gate_up(0, s, 1)
        col_sum(8)
        col_sum(9)

        def chunk_pe(i, par):
            for hf in range(2):
                for s in range(2):
                    gate_up(i, s, hf)
            down(i - 1, 1 - par)

        with pe.Fori(0, (NC - 3) // 2) as j:
            for par in (1, 0):
                chunk_pe(2 * j + (1 if par else 2), par)
        chunk_pe(NC - 2, (NC - 2) % 2)
        chunk_pe(NC - 1, (NC - 1) % 2)
        down(NC - 1, (NC - 1) % 2, WD2)

    ctx.close()


_INS = ["x", "c", "positions", "w_ada", "b_ada", "g_mix", "w_in", "g_q", "g_kv", "w_uq", "w_uk", "w_uv",
        "w_pool", "pool_scale", "w_o", "g_ffn", "w_gate", "w_up", "w_down", "g_final"]


def kernel(**inputs):
    import concourse.bacc as bacc
    from concourse.bass_utils import run_bass_kernel_spmd as run

    nc = bacc.Bacc("TRN2", target_bir_lowering=False, num_devices=1)
    arrays, args = {}, []
    for name in _INS:
        a = np.ascontiguousarray(inputs[name])
        arrays[f"in_{name}"] = a
        args.append(nc.dram_tensor(f"in_{name}", a.shape, mybir.dt.from_np(a.dtype), kind="ExternalInput").ap())
    f = np.power(10000.0, -np.arange(RH) / RH).astype(np.float32)
    arrays["freqs"] = f
    args.append(nc.dram_tensor("freqs", f.shape, F32, kind="ExternalInput").ap())
    args.append(nc.dram_tensor("out", (1, SEQ, D), F32, kind="ExternalOutput").ap())
    hybrid_block(nc, *args)
    r = run(nc, [arrays], core_ids=[0])
    return r.results[0]["out"]
```
